# Optimizing a Trainium2 kernel written in Bass

```python
import math
import jax, jax.numpy as jnp
from jax import lax
import numpy as np

D_MODEL = 1024
BATCH = 1
SEQ = 1024
DEPTH = 1

CHUNK = 64
N_LEFT_CHUNKS = 8
LEFT = N_LEFT_CHUNKS * CHUNK
BAND = (N_LEFT_CHUNKS + 1) * CHUNK
ATTN_HEADS = 8
HEAD_DIM = 64
D_ATTN = ATTN_HEADS * HEAD_DIM
MAX_REL = 256
N_REL = 2 * MAX_REL + 1
D_CONV = D_MODEL - D_ATTN
CONV_WIDTH = 31
N_BRANCHES = 2
D_IN = 2 * D_CONV + 3 * D_ATTN + N_BRANCHES * D_MODEL
N_EXPERTS = 16
N_GROUPS = 4
EXPERTS_PER_GROUP = N_EXPERTS // N_GROUPS
TOP_K = 2
D_FF_EXPERT = 512
ALPHA = (2.0 * DEPTH) ** 0.25
BETA = (8.0 * DEPTH) ** -0.25
LN_EPS = 1e-5

kernel_name = "hybrid_conv_chunkattn_grouped_moe_deepnorm"

def layer_norm(x, g, b):
    xf = x.astype(jnp.float32)
    mu = jnp.mean(xf, axis=-1, keepdims=True)
    var = jnp.mean(jnp.square(xf - mu), axis=-1, keepdims=True)
    return ((xf - mu) * lax.rsqrt(var + LN_EPS)).astype(x.dtype) * g + b

def conv_branch(glu_in, w_dw, b_dw, ln_g, ln_b, w_out):
    a, gate = jnp.split(glu_in, 2, axis=-1)
    u = a * jax.nn.sigmoid(gate)
    u = lax.conv_general_dilated(
        u, w_dw[:, None, :].astype(u.dtype),
        window_strides=(1,),
        padding=((CONV_WIDTH - 1, 0),),
        dimension_numbers=("NWC", "WIO", "NWC"),
        feature_group_count=D_CONV) + b_dw
    u = jax.nn.silu(layer_norm(u, ln_g, ln_b))
    return u @ w_out

def rel_index():
    i = jnp.arange(CHUNK)[:, None]
    j = jnp.arange(BAND)[None, :]
    rel = i - j + LEFT
    return jnp.clip(rel, -MAX_REL, MAX_REL) + MAX_REL

def chunked_attention(q, k, v, rel_bias):
    b, s = q.shape[0], q.shape[1]
    n_chunks = s // CHUNK
    qc = q.reshape(b, n_chunks, CHUNK, ATTN_HEADS, HEAD_DIM).transpose(1, 0, 3, 2, 4)
    kp = jnp.pad(k, ((0, 0), (LEFT, 0), (0, 0), (0, 0)))
    vp = jnp.pad(v, ((0, 0), (LEFT, 0), (0, 0), (0, 0)))
    bias = rel_bias[:, rel_index()].astype(jnp.float32)
    key_slot = jnp.arange(BAND)
    scale = HEAD_DIM ** -0.5

    def one_chunk(args):
        q_blk, c = args
        start = c * CHUNK
        k_blk = lax.dynamic_slice_in_dim(kp, start, BAND, axis=1)
        v_blk = lax.dynamic_slice_in_dim(vp, start, BAND, axis=1)
        scores = jnp.einsum("bhqd,bkhd->bhqk", q_blk, k_blk,
                            preferred_element_type=jnp.float32) * scale + bias
        valid = (start + key_slot) >= LEFT
        scores = jnp.where(valid, scores, -jnp.inf)
        p = jax.nn.softmax(scores, axis=-1).astype(v_blk.dtype)
        return jnp.einsum("bhqk,bkhd->bqhd", p, v_blk)

    out = lax.map(one_chunk, (qc, jnp.arange(n_chunks)))
    return out.transpose(1, 0, 2, 3, 4).reshape(b, s, D_ATTN)

def grouped_moe(h, w_router, b_router, w_gate_up, w_down):
    b, s, d = h.shape
    t = h.reshape(-1, d)
    logits = (t @ w_router + b_router).astype(jnp.float32)
    probs = jax.nn.softmax(logits, axis=-1)
    grouped = probs.reshape(-1, N_GROUPS, EXPERTS_PER_GROUP)
    top_vals, top_idx = lax.top_k(grouped, TOP_K)
    group_sel = jnp.argmax(jnp.sum(top_vals, axis=-1), axis=-1)
    sel_vals = jnp.take_along_axis(top_vals, group_sel[:, None, None], axis=1)[:, 0]
    sel_idx = (jnp.take_along_axis(top_idx, group_sel[:, None, None], axis=1)[:, 0]
               + group_sel[:, None] * EXPERTS_PER_GROUP)
    weights = sel_vals / jnp.sum(sel_vals, axis=-1, keepdims=True)
    combine = jnp.einsum("tk,tke->te", weights,
                         jax.nn.one_hot(sel_idx, N_EXPERTS, dtype=jnp.float32)).astype(t.dtype)
    out = jnp.zeros_like(t)
    for e in range(N_EXPERTS):
        g, u = jnp.split(t @ w_gate_up[e], 2, axis=-1)
        out = out + combine[:, e:e + 1] * ((jax.nn.silu(g) * u) @ w_down[e])
    return out.reshape(b, s, d)

def setup_inputs(seed: int = 0) -> dict:
    key = jax.random.key(seed)
    ks = jax.random.split(key, 24)
    L, D = DEPTH, D_MODEL
    nrm = lambda k, shape, s: jax.random.normal(k, shape, jnp.float32) * s
    return {
        "x": nrm(ks[0], (BATCH, SEQ, D), 1.0),
        "w_in": nrm(ks[1], (L, D, D_IN), D ** -0.5),
        "b_in": nrm(ks[2], (L, D_IN), 0.02),
        "w_dw": nrm(ks[3], (L, CONV_WIDTH, D_CONV), CONV_WIDTH ** -0.5),
        "b_dw": nrm(ks[4], (L, D_CONV), 0.02),
        "ln_conv_g": 1.0 + nrm(ks[5], (L, D_CONV), 0.02),
        "ln_conv_b": nrm(ks[6], (L, D_CONV), 0.02),
        "w_conv_out": nrm(ks[7], (L, D_CONV, D), D_CONV ** -0.5),
        "rel_bias": nrm(ks[8], (L, ATTN_HEADS, N_REL), 0.1),
        "w_attn_out": nrm(ks[9], (L, D_ATTN, D), D_ATTN ** -0.5),
        "w_o": nrm(ks[10], (L, D, D), BETA * D ** -0.5),
        "b_o": nrm(ks[11], (L, D), 0.02),
        "ln1_g": 1.0 + nrm(ks[12], (L, D), 0.02),
        "ln1_b": nrm(ks[13], (L, D), 0.02),
        "w_router": nrm(ks[14], (D, N_EXPERTS), D ** -0.5),
        "b_router": nrm(ks[15], (N_EXPERTS,), 0.01),
        "w_gate_up": nrm(ks[16], (L, N_EXPERTS, D, 2 * D_FF_EXPERT), D ** -0.5),
        "w_down": nrm(ks[17], (L, N_EXPERTS, D_FF_EXPERT, D), BETA * D_FF_EXPERT ** -0.5),
        "ln2_g": 1.0 + nrm(ks[18], (L, D), 0.02),
        "ln2_b": nrm(ks[19], (L, D), 0.02),
    }

def reference(x, w_in, b_in, w_dw, b_dw, ln_conv_g, ln_conv_b, w_conv_out, rel_bias,
              w_attn_out, w_o, b_o, ln1_g, ln1_b, w_router, b_router, w_gate_up,
              w_down, ln2_g, ln2_b):
    b, s, _ = x.shape
    splits = [2 * D_CONV, 2 * D_CONV + D_ATTN, 2 * D_CONV + 2 * D_ATTN, 2 * D_CONV + 3 * D_ATTN]
    for l in range(DEPTH):
        proj = x @ w_in[l] + b_in[l]
        glu_in, q, k, v, gate_logits = jnp.split(proj, splits, axis=-1)
        y_conv = conv_branch(glu_in, w_dw[l], b_dw[l], ln_conv_g[l], ln_conv_b[l], w_conv_out[l])
        heads = lambda t: t.reshape(b, s, ATTN_HEADS, HEAD_DIM)
        y_attn = chunked_attention(heads(q), heads(k), heads(v), rel_bias[l]) @ w_attn_out[l]
        g_conv, g_attn = jnp.split(jax.nn.sigmoid(gate_logits), N_BRANCHES, axis=-1)
        mixed = (g_conv * y_conv + g_attn * y_attn) @ w_o[l] + b_o[l]
        x = layer_norm(ALPHA * x + mixed, ln1_g[l], ln1_b[l])
        x = layer_norm(ALPHA * x + grouped_moe(x, w_router, b_router, w_gate_up[l], w_down[l]),
                       ln2_g[l], ln2_b[l])
    return x


_drawn_inputs = setup_inputs


def setup_inputs(seed=0):
    import zlib

    import numpy as np

    out = dict(_drawn_inputs(seed))
    spreads = {}
    factors = {'b_in': 3.246,
     'b_dw': 3.32,
     'ln_conv_g': 4.58,
     'ln_conv_b': 8.0,
     'rel_bias': 5.346,
     'ln2_g': 8.47,
     'ln2_b': 8.262,
     'b_router': 3.111}
    for name, (base, spread) in spreads.items():
        noise = np.random.default_rng([zlib.crc32(name.encode()), seed]).standard_normal(out[name].shape)
        drawn = base * np.exp(spread * noise) if base else spread * noise
        out[name] = __import__('jax').numpy.asarray(drawn.astype(out[name].dtype))
    for name, factor in factors.items():
        out[name] = (out[name] * factor).astype(out[name].dtype)
    return out
```

```python
import numpy as np
import concourse.bass as bass
from concourse import mybir
from contextlib import ExitStack

F32 = mybir.dt.float32
F32R = mybir.dt.float32r
I32 = mybir.dt.int32
U32 = mybir.dt.uint32
ALU = mybir.AluOpType
ACT = mybir.ActivationFunctionType
AX = mybir.AxisListType

P = 128
D = 1024
SEQ = 1024
KC = D // P
TT = SEQ // P
HALF = 512
DC = 512
CB = DC // P
CW = 31
PAD = CW - 1
HEADS, HD = 8, 64
PAIRS = HEADS // 2
BANDT = 5
BANDW = BANDT * P
SCALE = HD ** -0.5
NE, NGRP, EPG = 16, 4, 4
FF = 512
FC = FF // P
MAX_TILES = NE + (2 * SEQ - 1) // P
TAB = 32
WROWS = KC + FC
ALPHA = 2.0 ** 0.25
EPS = 1e-5
MASKED = -1e30
RING, RAWS = 4, 2

N_GLU = 2 * CB
N_SEG = 2 + 2 * 2
N_ATT = 2 * N_SEG
FIRST_OUT = N_GLU + N_ATT
FIRST_WO = FIRST_OUT + 3 * KC
N_BLOCKS = FIRST_WO + KC


def block_columns():
    a, g, q, k, v, gc, ga = (np.cumsum([0, 4, 4, 4, 4, 4, 8])).tolist()
    o, wo = 36, 44
    cols = []
    for j in range(CB):
        cols += [a + j, g + j]
    for s in range(2):
        cols += [v + 2 * s, v + 2 * s + 1, q + 2 * s, k + 2 * s, q + 2 * s + 1, k + 2 * s + 1]
    for j in range(KC):
        cols += [gc + j, ga + j, o + j]
    cols += [wo + j for j in range(KC)]
    return cols


C_ID, C_TRI, C_IOTA, C_TOK, C_THR = 0, 128, 256, 384, 392
C_WIDTH = 400
C_REST = C_WIDTH - C_TRI


def constants():
    c = np.zeros((P, C_WIDTH), np.float32)
    c[:, C_ID:C_ID + P] = np.eye(P)
    c[:, C_TRI:C_TRI + P] = np.triu(np.ones((P, P)), 1)
    c[:, C_IOTA:C_IOTA + P] = np.arange(P)[None, :]
    c[:, C_TOK:C_TOK + TT] = np.arange(P)[:, None] + P * np.arange(TT)[None, :]
    c[:, C_THR:C_THR + 7] = P * np.arange(1, 8)[None, :]
    return c


def encoder_layer(nc, xT, x, wblk, b_in, dw, dwb, lncg, lncb, relb, b_o, ln1_g, ln1_b,
                  w_r, b_r, wexp, ln2_g, ln2_b, consts, out):
    x1_dram = nc.dram_tensor("x1_rows", (SEQ, D), F32, kind="Internal").ap()
    y_dram = nc.dram_tensor("y_slots", (MAX_TILES * P, D), F32, kind="Internal").ap()
    ctx = ExitStack()
    with ctx:
        ARENA = 207 * 1024 + 512
        arena = ctx.enter_context(nc.sbuf_tensor("arena", [P, ARENA], mybir.dt.uint8))
        base = nc.sbuf_base - ARENA
        KB = 1024

        def at(name, shape, dt, kb):
            size = int(np.prod(shape[1:])) * 4
            assert kb * KB + size <= ARENA, name
            return nc.alloc_sbuf_tensor_at(name, shape, dt, offset=base + int(kb * KB))

        xh = at("xh", [P, KC, SEQ], F32R, 0)
        xl = at("xl", [P, KC, SEQ], F32R, 32)
        wh = at("wh", [P, RING, KC, P], F32R, 64)
        wl = at("wl", [P, RING, KC, P], F32R, 80)
        raw = at("raw", [P, RAWS, KC, P], F32, 96)
        attn = at("attn", [P, PAIRS, SEQ], F32, 104)
        u = at("u", [P, CB, PAD + SEQ], F32, 120)
        cv = at("cv", [P, CB, SEQ], F32, 136.5)
        qh = at("qh", [P, SEQ], F32R, 152.5)
        ql = at("ql", [P, SEQ], F32R, 156.5)
        kh = at("kh", [P, SEQ], F32R, 160.5)
        kl = at("kl", [P, SEQ], F32R, 164.5)
        vh = at("vh", [P, TT, 2 * P], F32R, 168.5)
        vl = at("vl", [P, TT, 2 * P], F32R, 176.5)
        bias = at("bias", [P, 2, BANDW], F32, 184.5)
        pr = at("pr", [P, 2, BANDW], F32, 189.5)
        pth = at("pth", [P, BANDT, 2, P], F32R, 194.5)
        ptl = at("ptl", [P, BANDT, 2, P], F32R, 199.5)
        tapped = at("tapped", [P, SEQ], F32, 116)
        xraw = at("xraw", [P, KC, SEQ], F32, 152.5)
        sig = at("sig", [P, 2, SEQ], F32, 189.5)
        ah = at("ah", [P, PAIRS, SEQ], F32R, 152.5)
        al = at("al", [P, PAIRS, SEQ], F32R, 168.5)
        uoh = at("uoh", [P, CB, SEQ], F32R, 120)
        uol = at("uol", [P, CB, SEQ], F32R, 136.5)
        mixa = at("mixa", [P, 4, SEQ], F32, 104)
        mixb = at("mixb", [P, 4, SEQ], F32, 184.5)
        sqr = at("sqr", [P, 2, SEQ], F32, 184.5)
        rstdc = at("rstdc", [P, SEQ], F32, 192.5)
        act_u = at("act_u", [P, 1, SEQ], F32, 196.5)
        sgc = at("sgc", [P, HALF], F32, 200.5)
        sga = at("sga", [P, HALF], F32, 202.5)
        mh = at("mh", [P, KC, SEQ], F32R, 0)
        ml = at("ml", [P, KC, SEQ], F32R, 32)
        x1 = at("x1", [P, TT, D], F32, 170)
        bo_b = at("bo_b", [P, D], F32, 152.5)
        g1_b = at("g1_b", [P, D], F32, 156.5)
        b1_b = at("b1_b", [P, D], F32, 160.5)
        w_e = at("w_e", [P, 3, WROWS, 1024], F32, 0)
        xg = at("xg", [P, D], F32, 144)
        xgt = at("xgt", [P, KC, P], F32, 148)
        sg = at("sg", [P, FF], F32, 152)
        hb = at("hb", [P, FF], F32, 154)
        hbt = at("hbt", [P, FC, P], F32, 156)
        ys = at("ys", [P, D], F32, 158)
        rt = at("rt", [P, 14 * 128], F32, 158)
        y1 = at("y1", [P, 2, D], F32, 0)
        y2 = at("y2", [P, 2, D], F32, 8)
        g2_b = at("g2_b", [P, D], F32, 16)
        b2_b = at("b2_b", [P, D], F32, 20)
        small = 204.5
        cst = at("cst", [P, C_REST], F32, 166)

        def tiny(name, shape, dt=F32):
            nonlocal small
            t = at(name, shape, dt, small)
            small += -(-int(np.prod(shape[1:])) * 4 // 32) * 32 / KB
            return t
        b_in_t = tiny("b_in_t", [P, 36])
        cpar = tiny("cpar", [P, 3, CB])
        dw_t = tiny("dw_t", [P, CB, CW])
        eps = tiny("eps", [P, 1])
        mx = tiny("mx", [P, 2])
        nmx = tiny("nmx", [P, 2])
        rs = tiny("rs", [P, 2])
        rinv = tiny("rinv", [P, 2])
        st6 = tiny("st6", [P, 2, 6])
        mv = tiny("mv", [P, TT, 2])
        rstd = tiny("rstd", [P, TT])
        nmr = tiny("nmr", [P, TT])
        wgt = tiny("wgt", [P, 2, TT])
        slot_i = tiny("slot_i", [P, 2, TT], I32)
        ids_i = tiny("ids_i", [P, TAB], I32)
        id_now = tiny("id_now", [P, 1], I32)
        e_tab = tiny("e_tab", [P, TAB], I32)
        s_tab = tiny("s_tab", [P, TAB], I32)
        cum_i = tiny("cum_i", [P, NE], I32)
        ends_i = tiny("ends_i", [P, 2], I32)
        br_b = tiny("br_b", [P, NE])
        ident_t = tiny("ident_t", [P, P])
        ident = ident_t[:]

        ps = ctx.enter_context(nc.psum_tensor("ps", [P, 8, HALF], F32))
        psf = ps[:, :, :].rearrange("p b n -> p (b n)")

        def sem(name):
            return ctx.enter_context(nc.semaphore(name))

        x_in = [sem(f"x_in{k}") for k in range(KC)]
        par_in = sem("par_in")
        raw_in = [sem(f"raw_in{r}") for r in range(RAWS)]
        bias_in = sem("bias_in")
        x_hi = sem("x_hi"); x_lo = sem("x_lo")
        w_hi = sem("w_hi"); w_lo = sem("w_lo")
        blk_used = sem("blk_used")
        sig_ready = sem("sig_ready"); u_ready = sem("u_ready")
        conv_d = sem("conv_d"); conv_p = sem("conv_p"); init_d = sem("init_d"); init_p = sem("init_p")
        v_done = sem("v_done"); v_hi = sem("v_hi"); v_lo = sem("v_lo")
        qk_hi = sem("qk_hi"); qk_lo = sem("qk_lo")
        bias_ok = sem("bias_ok")
        s_done = sem("s_done"); s_max = sem("s_max"); s_nmx = sem("s_nmx"); exp_done = sem("exp_done")
        p_inv = sem("p_inv"); p_ready = sem("p_ready")
        t_done = sem("t_done"); pt_hi = sem("pt_hi"); pt_lo = sem("pt_lo")
        pv_done = sem("pv_done"); o_done = sem("o_done")
        a_hi = sem("a_hi"); a_lo = sem("a_lo")
        mean_done = sem("mean_done"); cent = sem("cent"); sq_done = sem("sq_done"); sq_used = sem("sq_used")
        var_done = sem("var_done"); std_done = sem("std_done"); rstd_ok = sem("rstd_ok")
        nrm = sem("nrm"); silu_done = sem("silu_done"); uo_hi = sem("uo_hi"); uo_lo = sem("uo_lo")
        sig_gc = sem("sig_gc"); sig_ga = sem("sig_ga")
        mix1 = sem("mix1"); mix2 = sem("mix2"); mixed = sem("mixed")
        m_hi = sem("m_hi"); m_lo = sem("m_lo")
        xres_in = [sem(f"xres_in{i}") for i in range(TT)]
        lnp_in = sem("lnp_in"); xres_ok = sem("xres_ok"); xres_s = sem("xres_s"); tap_p = sem("tap_p"); zero_ok = sem("zero_ok"); zero_out = sem("zero_out")
        wo_done = sem("wo_done"); wo_add = sem("wo_add")
        st_ok = sem("st_ok"); var_ok = sem("var_ok"); sd_ok = sem("sd_ok"); rst_ok = sem("rst_ok")
        nmr_ok = sem("nmr_ok"); ln_a = sem("ln_a"); ln_g = sem("ln_g"); x1_ok = sem("x1_ok")
        x1_out = sem("x1_out")

        def blk(n):
            return n + 1 - sum(2 for s in range(2) if n > N_GLU + N_SEG * s)

        def wait_used(eng, n):
            s, r = divmod(n - N_GLU, N_SEG)
            if 0 <= s < 2 and r < 2:
                eng.wait_ge(v_done, TT * (s + 1))
            elif n >= FIRST_WO:
                eng.wait_ge(wo_done, TT * ((n - FIRST_WO) // 2 + 1))
            else:
                eng.wait_ge(blk_used, blk(n))

        def tiles_of(c):
            return max(0, c - BANDT + 1), min(c, BANDT - 1) + 1

        with nc.Block() as block:
            @block.sync
            def _(sp):
                sp.dma_start(b_in_t[:], b_in).then_inc(par_in, 16)
                sp.dma_start(ident, consts[:, C_ID:C_ID + P]).then_inc(par_in, 16)
                for i, src in enumerate((dwb, lncg, lncb)):
                    sp.dma_start(cpar[:, i, :], src).then_inc(par_in, 16)
                sp.dma_start(dw_t[:], dw).then_inc(par_in, 16)

                def load_block(n):
                    if n >= RAWS:
                        sp.wait_ge(w_lo, n - RAWS + 1)
                    sp.dma_start(raw[:, n % RAWS], wblk[n]).then_inc(raw_in[n % RAWS], 16)

                def load_bias(b):
                    if b:
                        sp.wait_ge(s_max, 2 * TT * b)
                    sp.dma_start(bias[:], relb[b]).then_inc(bias_in, 16)

                for k in range(KC):
                    sp.dma_start(xraw[:, k, :], xT[k]).then_inc(x_in[k], 16)
                    if k < RAWS:
                        load_block(k)
                load_bias(0)
                after = {N_GLU + 6: 1, N_GLU + N_SEG + 4: 2, FIRST_OUT: 3}
                for n in range(RAWS, FIRST_WO + 4):
                    load_block(n)
                    if n in after:
                        load_bias(after[n])
                    for i in range(NE + 2 * (n - RAWS), min(NE + 2 * (n - RAWS) + 2, MAX_TILES)):
                        if i == NE:
                            sp.wait_ge(zero_ok, 1)
                        sp.dma_start(y_dram[P * i:P * i + P, :], tapped[:]).then_inc(zero_out, 16)
                sp.wait_ge(blk_used, blk(FIRST_WO - 1))
                for dst, src in ((bo_b, b_o), (g1_b, ln1_g), (b1_b, ln1_b)):
                    sp.dma_start(dst[:], src.partition_broadcast(P)).then_inc(lnp_in, 16)
                for t in range(TT):
                    if t == 3:
                        sp.wait_ge(m_lo, KC)
                    sp.dma_start(x1[:, t, :], x[P * t:P * t + P, :]).then_inc(xres_in[t], 16)
                for n in range(FIRST_WO + 4, N_BLOCKS):
                    load_block(n)
                for t in range(TT):
                    sp.wait_ge(x1_ok, t + 1)
                    sp.dma_start(x1_dram[P * t:P * t + P, :], x1[:, t, :]).then_inc(x1_out, 16)
                sp.wait_ge(x1_out, 16 * TT)

            @block.gpsimd
            def _(pool):
                pool.memset(tapped[:], 0.0).then_inc(zero_ok, 1)
                pool.memset(eps[:], EPS).then_inc(init_p, 1)
                pool.memset(u[:, :, 0:PAD], 0.0).then_inc(init_p, 1)

                def split_block(n):
                    pool.wait_ge(raw_in[n % RAWS], 16 * (n // RAWS + 1))
                    if n >= RING:
                        wait_used(pool, n - RING)
                    pool.tensor_scalar(wh[:, n % RING], raw[:, n % RAWS], 1.0, None, ALU.mult).then_inc(w_hi, 1)
                    pool.wait_ge(w_hi, n + 1)
                    pool.tensor_tensor(wl[:, n % RING], raw[:, n % RAWS], wh[:, n % RING], ALU.subtract).then_inc(w_lo, 1)

                def conv_taps(j, k0, k1):
                    pool.wait_ge(u_ready, j + 1)
                    for k in range(k0, k1):
                        tap, w = u[:, j, k:k + SEQ], dw_t[:, j, k:k + 1]
                        if k == 0:
                            pool.tensor_scalar(cv[:, j, :], tap, w, cpar[:, 0, j:j + 1], ALU.mult, ALU.add).then_inc(conv_p, 1)
                        else:
                            if k > 1:
                                pool.wait_ge(conv_p, k)
                            pool.tensor_scalar(tapped[:], tap, w, None, ALU.mult).then_inc(tap_p, 1)
                            pool.wait_ge(tap_p, k)
                            pool.wait_ge(conv_p, k)
                            pool.tensor_tensor(cv[:, j, :], cv[:, j, :], tapped[:], ALU.add).then_inc(conv_p, 1)

                for n in range(N_GLU + 4):
                    split_block(n)
                pool.wait_ge(par_in, 96)
                pool.wait_ge(zero_out, 16 * (MAX_TILES - NE))
                for i in range(3):
                    conv_taps(CB - 1, 10 * i, min(10 * i + 10 + i // 2, CW))
                    split_block(N_GLU + 4 + 2 * i)
                    split_block(N_GLU + 5 + 2 * i)
                for n in range(N_GLU + 10, FIRST_WO + 4):
                    split_block(n)
                pool.wait_ge(lnp_in, 48)
                for t in range(TT):
                    pool.wait_ge(xres_s, t + 1)
                    pool.tensor_tensor(x1[:, t, :], x1[:, t, :], bo_b[:], ALU.add).then_inc(xres_ok, 1)
                for n in range(FIRST_WO + 4, N_BLOCKS):
                    split_block(n)

            @block.tensor
            def _(pe):
                def mm3(o, a_h, a_l, b_h, b_l, first, last):
                    pe.matmul(o, a_h, b_h, start=first, stop=False)
                    pe.matmul(o, a_h, b_l, start=False, stop=False)
                    return pe.matmul(o, a_l, b_h, start=False, stop=last)

                def weights_left(n, bank):
                    pe.wait_ge(w_lo, n + 1)
                    s = n % RING
                    for k in range(KC):
                        if n == 0:
                            pe.wait_ge(x_lo, k + 1)
                        for h in range(2):
                            c = slice(HALF * h, HALF * h + HALF)
                            last = mm3(ps[:, bank + h, :], wh[:, s, k], wl[:, s, k], xh[:, k, c], xl[:, k, c],
                                       k == 0, k == KC - 1)
                    return last

                for j in range(CB):
                    if j >= 2:
                        pe.wait_ge(u_ready, j - 1)
                    bank = 4 * (j % 2)
                    weights_left(2 * j, bank).then_inc(blk_used, 1)
                    weights_left(2 * j + 1, bank + 2).then_inc(blk_used, 1)

                def project_v(s):
                    n = N_GLU + N_SEG * s
                    pe.wait_ge(w_lo, n + 2)
                    r = n % RING
                    for t in range(TT):
                        i = TT * s + t
                        if i >= 4:
                            pe.wait_ge(v_lo, i - 3)
                        else:
                            pe.wait_ge(u_ready, CB)
                        if s and t == 0:
                            pe.wait_ge(o_done, 4 * TT)
                        c = slice(P * t, P * t + P)
                        for k in range(KC):
                            last = mm3(ps[:, 4 + t % 4, 0:2 * P], xh[:, k, c], xl[:, k, c],
                                       wh[:, r:r + 2, k, :], wl[:, r:r + 2, k, :], k == 0, k == KC - 1)
                        last.then_inc(v_done, 1)

                def project_qk(b):
                    n = N_GLU + N_SEG * (b // 2) + 2 + 2 * (b % 2)
                    if b:
                        pe.wait_ge(s_max, 2 * TT * b)
                    for i in range(2):
                        weights_left(n + i, 2 * i).then_inc(blk_used, 1)

                def scores(n, h):
                    b, c = divmod(n, TT)
                    kt, nt = tiles_of(c)
                    if n:
                        pe.wait_ge(s_max, 2 * n - 1 + h)
                    r = slice(HD * h, HD * h + HD)
                    q = slice(P * c, P * c + P)
                    for k0 in range(0, nt * P, HALF):
                        w = min(HALF, nt * P - k0)
                        kk = slice(P * kt + k0, P * kt + k0 + w)
                        last = mm3(ps[:, 2 * h + k0 // HALF, 0:w], qh[r, q], ql[r, q], kh[r, kk], kl[r, kk], True, True)
                    last.then_inc(s_done, 1)

                def transpose_probs(n, h):
                    nt = tiles_of(n % TT)[1]
                    m = 2 * n + h
                    pe.wait_ge(p_ready, m + 1)
                    if m:
                        pe.wait_ge(pt_lo, m)
                    for t in range(nt):
                        last = pe.transpose(psf[:, 4 * HALF + P * t:4 * HALF + P * t + P], pr[:, h, P * t:P * t + P], ident)
                    last.then_inc(t_done, 1)

                def weigh_values(n):
                    b, c = divmod(n, TT)
                    kt, nt = tiles_of(c)
                    pe.wait_ge(pt_lo, 2 * n + 2)
                    if n >= 2:
                        pe.wait_ge(o_done, 2 * n - 2)
                    v = slice(P * (b % 2), P * (b % 2) + P)
                    for t in range(nt):
                        last = mm3(ps[:, 6 + n % 2, 0:2 * P], vh[:, kt + t, v], vl[:, kt + t, v],
                                   pth[:, t], ptl[:, t], t == 0, t == nt - 1)
                    last.then_inc(pv_done, 1)

                for s in range(2):
                    project_v(s)
                    for n in range(2 * TT * s, 2 * TT * (s + 1) + 1):
                        lead = n < 2 * TT * (s + 1)
                        if lead and n % TT == 0:
                            project_qk(n // TT)
                            pe.wait_ge(qk_lo, 2 * (n // TT + 1))
                        if n == 2 * TT * s:
                            pe.wait_ge(v_lo, TT * (s + 1))
                        for h in range(2):
                            if lead:
                                scores(n, h)
                            if n > 2 * TT * s:
                                transpose_probs(n - 1, h)
                        if n > 2 * TT * s:
                            weigh_values(n - 1)

                def channel_mean(bank, src, ready):
                    for j in range(CB):
                        ready(j)
                        for h in range(2):
                            last = pe.matmul(ps[:, bank + h, :], ones_c, src(j)[:, HALF * h:HALF * h + HALF],
                                             start=j == 0, stop=j == CB - 1)
                    return last

                ones_c = rstdc[:, 0:P]
                pe.wait_ge(init_d, 1)
                pe.wait_ge(conv_d, 3 * CW)
                pe.wait_ge(conv_p, CW)
                pe.wait_ge(pt_lo, 4 * TT * PAIRS // 2)
                channel_mean(4, lambda j: cv[:, j, :], lambda j: None).then_inc(mean_done, 1)
                n = FIRST_OUT
                weights_left(n, 0).then_inc(blk_used, 1)
                pe.wait_ge(o_done, 2 * TT * PAIRS)
                for j in range(CB):
                    pe.wait_ge(sq_done, j + 1)
                    for h in range(2):
                        last = pe.matmul(ps[:, 6 + h, :], ones_c, sqr[:, j % 2, HALF * h:HALF * h + HALF],
                                         start=j == 0, stop=j == CB - 1)
                    last.then_inc(sq_used, 1)

                for j in range(KC):
                    n = FIRST_OUT + 3 * j
                    if j:
                        pe.wait_ge(sig_gc, 2 * j)
                        weights_left(n, 0).then_inc(blk_used, 1)
                        pe.wait_ge(sig_ga, 2 * j)
                    weights_left(n + 1, 2).then_inc(blk_used, 1)
                    s = (n + 2) % RING
                    pe.wait_ge(w_lo, n + 3)
                    if j == 0:
                        pe.wait_ge(rstd_ok, 1)
                        pe.wait_ge(cent, CB)
                        pe.wait_ge(uo_lo, CB)
                        pe.wait_ge(a_lo, PAIRS)
                    else:
                        pe.wait_ge(mix2, 2 * j)
                    for bank, hi, lo, k0 in ((4, uoh, uol, 0), (6, ah, al, CB)):
                        for k in range(CB):
                            for h in range(2):
                                c = slice(HALF * h, HALF * h + HALF)
                                last = mm3(ps[:, bank + h, :], wh[:, s, k0 + k], wl[:, s, k0 + k],
                                           hi[:, k, c], lo[:, k, c], k == 0, k == CB - 1)
                    last.then_inc(blk_used, 1)

                pe.wait_ge(mixed, 2 * KC)
                for g in range(4):
                    n = FIRST_WO + 2 * g
                    r = n % RING
                    pe.wait_ge(w_lo, n + 2)
                    for t in range(TT):
                        if g:
                            pe.wait_ge(wo_add, TT * (g - 1) + t + 1)
                        c = slice(P * t, P * t + P)
                        for k in range(KC):
                            if g == 0 and t == 0:
                                pe.wait_ge(m_lo, k + 1)
                            last = mm3(ps[:, t, 0:2 * P], mh[:, k, c], ml[:, k, c],
                                       wh[:, r:r + 2, k, :], wl[:, r:r + 2, k, :], k == 0, k == KC - 1)
                        last.then_inc(wo_done, 1)

            @block.scalar
            def _(act):
                for k in range(KC):
                    act.wait_ge(x_in[k], 16)
                    act.activation(xh[:, k, :], xraw[:, k, :], ACT.Copy).then_inc(x_hi, 1)
                act.wait_ge(par_in, 96)
                for j in range(CB):
                    act.wait_ge(blk_used, blk(2 * j + 1))
                    if j >= 2:
                        act.wait_ge(u_ready, j - 1)
                    g = 4 * (j % 2) + 2
                    act.activation(sig[:, j % 2, :], psf[:, HALF * g:HALF * g + SEQ], ACT.Sigmoid,
                                   bias=b_in_t[:, CB + j:CB + j + 1]).then_inc(sig_ready, 1)
                for s in range(2):
                    for t in range(TT):
                        i = TT * s + t
                        act.wait_ge(v_done, i + 1)
                        if s:
                            act.wait_ge(pv_done, 2 * TT)
                        act.activation(vh[:, t, :], ps[:, 4 + t % 4, 0:2 * P], ACT.Copy).then_inc(v_hi, 1)

                    for n in range(2 * TT * s, 2 * TT * (s + 1) + 1):
                        lead = n < 2 * TT * (s + 1)
                        if lead and n % TT == 0:
                            b = n // TT
                            act.wait_ge(blk_used, blk(N_GLU + N_SEG * (b // 2) + 3 + 2 * (b % 2)))
                            for i, dst in enumerate((qh, kh)):
                                col = 8 + 4 * i + b
                                act.activation(dst[:], psf[:, 2 * HALF * i:2 * HALF * (i + 1)], ACT.Identity,
                                               bias=b_in_t[:, col:col + 1]).then_inc(qk_hi, 1)
                        for h in range(2):
                            if n > 2 * TT * s:
                                m = 2 * (n - 1) + h
                                nt = tiles_of((n - 1) % TT)[1]
                                act.wait_ge(t_done, m + 1)
                                if n > 1:
                                    act.wait_ge(pv_done, n - 1)
                                act.activation(pth[:, 0:nt, h, :],
                                               psf[:, 4 * HALF:4 * HALF + P * nt].rearrange("p (t q) -> p t q", q=P),
                                               ACT.Copy).then_inc(pt_hi, 1)
                            if lead:
                                nt = tiles_of(n % TT)[1]
                                act.wait_ge(s_nmx, 2 * n + h + 1)
                                act.activation(pr[:, h, 0:nt * P], pr[:, h, 0:nt * P], ACT.Exp, scale=SCALE,
                                               bias=nmx[:, h:h + 1], accum_out=rs[:, h:h + 1]).then_inc(exp_done, 1)
                        if n > 2 * TT * s:
                            b, c = divmod(n - 1, TT)
                            act.wait_ge(pv_done, n)
                            if n - 1 == TT * (PAIRS - 1):
                                act.wait_ge(conv_p, CW)
                            for h in range(2):
                                r = slice(HD * h, HD * h + HD)
                                act.activation(attn[r, b, P * c:P * c + P], ps[r, 6 + (n - 1) % 2, P * h:P * h + P],
                                               ACT.Identity, bias=b_in_t[r, 16 + b:17 + b]).then_inc(o_done, 1)
                act.wait_ge(o_done, 2 * TT * PAIRS)
                act.wait_ge(s_max, 2 * TT * PAIRS)
                for b in range(PAIRS):
                    act.activation(ah[:, b, :], attn[:, b, :], ACT.Copy).then_inc(a_hi, 1)
                for j in range(CB):
                    act.wait_ge(cent, j + 1)
                    if j >= 2:
                        act.wait_ge(sq_used, j - 1)
                    act.activation(sqr[:, j % 2, :], cv[:, j, :], ACT.Square).then_inc(sq_done, 1)
                act.wait_ge(sq_used, CB)
                act.activation(act_u[:, 0, :], psf[:, 6 * HALF:8 * HALF], ACT.Sqrt, bias=eps[:]).then_inc(std_done, 1)
                for j in range(CB):
                    act.wait_ge(nrm, j + 1)
                    if j >= 1:
                        act.wait_ge(uo_lo, j)
                    act.activation(act_u[:, 0, :], cv[:, j, :], ACT.Silu, scale=cpar[:, 1, j:j + 1],
                                   bias=cpar[:, 2, j:j + 1]).then_inc(silu_done, 1)
                    act.wait_ge(silu_done, j + 1)
                    act.activation(uoh[:, j, :], act_u[:, 0, :], ACT.Copy).then_inc(uo_hi, 1)
                for j in range(KC):
                    for h in range(2):
                        i = 2 * j + h
                        act.wait_ge(blk_used, blk(FIRST_OUT + 3 * j))
                        if i:
                            act.wait_ge(mix1, i)
                        act.activation(sgc[:], ps[:, h, :], ACT.Sigmoid, bias=b_in_t[:, 20 + j:21 + j]).then_inc(sig_gc, 1)
                        act.wait_ge(blk_used, blk(FIRST_OUT + 3 * j + 1))
                        if i:
                            act.wait_ge(mixed, i)
                        act.activation(sga[:], ps[:, 2 + h, :], ACT.Sigmoid, bias=b_in_t[:, 28 + j:29 + j]).then_inc(sig_ga, 1)
                act.wait_ge(mixed, 2 * KC)
                act.wait_ge(blk_used, blk(FIRST_WO - 1))
                for j in range(KC):
                    src = mixa if j < 4 else mixb
                    act.activation(mh[:, j, :], src[:, j % 4, :], ACT.Copy).then_inc(m_hi, 1)
                for t in range(TT):
                    act.wait_ge(xres_in[t], 16)
                    act.activation(x1[:, t, :], x1[:, t, :], ACT.Copy, scale=ALPHA).then_inc(xres_s, 1)
                for t in range(TT):
                    act.wait_ge(st_ok, t + 1)
                    act.activation(rstd[:, t:t + 1], mv[:, t, 1:2], ACT.Sqrt, bias=eps[:]).then_inc(sd_ok, 1)
                    act.wait_ge(nmr_ok, t + 1)
                    act.activation(x1[:, t, :], x1[:, t, :], ACT.Identity, scale=rstd[:, t:t + 1],
                                   bias=nmr[:, t:t + 1]).then_inc(ln_a, 1)

            @block.vector
            def _(dve):
                for k in range(KC):
                    dve.wait_ge(x_hi, k + 1)
                    dve.tensor_tensor(xl[:, k, :], xraw[:, k, :], xh[:, k, :], ALU.subtract).then_inc(x_lo, 1)
                dve.wait_ge(init_p, 2)
                dve.wait_ge(par_in, 96)

                def glu(j):
                    dve.wait_ge(sig_ready, j + 1)
                    a = 4 * (j % 2)
                    dve.scalar_tensor_tensor(out=u[:, j, PAD:], in0=psf[:, HALF * a:HALF * a + SEQ],
                                             scalar=b_in_t[:, j:j + 1], in1=sig[:, j % 2, :],
                                             op0=ALU.add, op1=ALU.mult).then_inc(u_ready, 1)

                def conv_taps(j, k0, k1):
                    dve.wait_ge(u_ready, j + 1)
                    for k in range(k0, k1):
                        tap, w = u[:, j, k:k + SEQ], dw_t[:, j, k:k + 1]
                        if k == 0:
                            dve.tensor_scalar(cv[:, j, :], tap, w, cpar[:, 0, j:j + 1], ALU.mult, ALU.add).then_inc(conv_d, 1)
                        else:
                            dve.wait_ge(conv_d, CW * j + k)
                            dve.scalar_tensor_tensor(out=cv[:, j, :], in0=tap, scalar=w, in1=cv[:, j, :],
                                                     op0=ALU.mult, op1=ALU.add).then_inc(conv_d, 1)

                glu(0)
                conv_taps(0, 0, 14)
                glu(1)
                conv_taps(0, 14, CW)
                glu(2)
                conv_taps(1, 0, 14)
                glu(3)
                conv_taps(1, 14, CW)

                def transposed_lo(n, h):
                    m = 2 * n + h
                    nt = tiles_of(n % TT)[1]
                    dve.wait_ge(pt_hi, m + 1)
                    dve.tensor_tensor(ptl[:, 0:nt, h, :], psf[:, 4 * HALF:4 * HALF + P * nt].rearrange("p (t q) -> p t q", q=P),
                                      pth[:, 0:nt, h, :], ALU.subtract).then_inc(pt_lo, 1)

                for s in range(2):
                    for t in range(TT):
                        i = TT * s + t
                        dve.wait_ge(v_hi, i + 1)
                        dve.tensor_tensor(vl[:, t, :], ps[:, 4 + t % 4, 0:2 * P], vh[:, t, :], ALU.subtract).then_inc(v_lo, 1)
                    for n in range(2 * TT * s, 2 * TT * (s + 1) + 1):
                        lead = n < 2 * TT * (s + 1)
                        if lead and n % TT == 0:
                            b = n // TT
                            conv_taps(2, 8 * b, min(8 * b + 8, CW))
                            for i, (hi, lo) in enumerate(((qh, ql), (kh, kl))):
                                col = 8 + 4 * i + b
                                dve.wait_ge(qk_hi, 2 * b + i + 1)
                                dve.scalar_tensor_tensor(out=lo[:], in0=psf[:, 2 * HALF * i:2 * HALF * (i + 1)],
                                                         scalar=b_in_t[:, col:col + 1], in1=hi[:],
                                                         op0=ALU.add, op1=ALU.subtract).then_inc(qk_lo, 1)
                            dve.wait_ge(bias_in, 16 * (b + 1))
                            dve.tensor_scalar(bias[:], bias[:], 1.0 / SCALE, None, ALU.mult).then_inc(bias_ok, 1)
                            dve.wait_ge(bias_ok, 3 * b + 1)
                            dve.memset(bias[0:HD, :, BANDW - HD:BANDW], MASKED).then_inc(bias_ok, 1)
                            dve.memset(bias[HD:P, :, 0:HD], MASKED).then_inc(bias_ok, 1)
                            dve.wait_ge(bias_ok, 3 * b + 3)
                        for h in range(2):
                            m = 2 * n + h
                            nt = tiles_of(n % TT)[1]
                            if lead:
                                dve.wait_ge(s_done, m + 1)
                                if n > 0:
                                    dve.wait_ge(t_done, m - 1)
                                dve.tensor_tensor_reduce(out=pr[:, h, 0:nt * P], in0=psf[:, 2 * HALF * h:2 * HALF * h + nt * P],
                                                         in1=bias[:, h, BANDW - nt * P:BANDW], scale=1.0, scalar=-3e38,
                                                         op0=ALU.add, op1=ALU.max, accum_out=mx[:, h:h + 1]).then_inc(s_max, 1)
                                dve.wait_ge(s_max, m + 1)
                                dve.tensor_scalar(nmx[:, h:h + 1], mx[:, h:h + 1], -SCALE, None, ALU.mult).then_inc(s_nmx, 1)
                            if n > 2 * TT * s:
                                transposed_lo(n - 1, h)
                        if lead:
                            for h in range(2):
                                m = 2 * n + h
                                dve.wait_ge(exp_done, m + 1)
                                dve.reciprocal(rinv[:, h:h + 1], rs[:, h:h + 1]).then_inc(p_inv, 1)
                                dve.wait_ge(p_inv, m + 1)
                                dve.tensor_scalar(pr[:, h, 0:nt * P], pr[:, h, 0:nt * P], rinv[:, h:h + 1], None,
                                                  ALU.mult).then_inc(p_ready, 1)
                dve.wait_ge(t_done, 2 * TT * PAIRS)
                dve.memset(rstdc[:, 0:P], 1.0 / DC).then_inc(init_d, 1)
                for b in range(PAIRS):
                    dve.wait_ge(a_hi, b + 1)
                    if b == 0:
                        dve.wait_ge(pv_done, TT * PAIRS)
                    dve.tensor_tensor(al[:, b, :], attn[:, b, :], ah[:, b, :], ALU.subtract).then_inc(a_lo, 1)
                dve.wait_ge(mean_done, 1)
                for j in range(CB):
                    dve.tensor_tensor(cv[:, j, :], cv[:, j, :], psf[:, 4 * HALF:6 * HALF], ALU.subtract).then_inc(cent, 1)
                dve.wait_ge(std_done, 1)
                dve.reciprocal(rstdc[:], act_u[:, 0, :]).then_inc(rstd_ok, 1)
                dve.wait_ge(rstd_ok, 1)
                dve.wait_ge(cent, CB)
                for j in range(CB):
                    dve.tensor_tensor(cv[:, j, :], cv[:, j, :], rstdc[:], ALU.mult).then_inc(nrm, 1)
                for j in range(CB):
                    dve.wait_ge(uo_hi, j + 1)
                    dve.tensor_tensor(uol[:, j, :], act_u[:, 0, :], uoh[:, j, :], ALU.subtract).then_inc(uo_lo, 1)
                dve.wait_ge(a_lo, PAIRS)
                for j in range(KC):
                    dst = mixa if j < 4 else mixb
                    for h in range(2):
                        i = 2 * j + h
                        c = slice(HALF * h, HALF * h + HALF)
                        dve.wait_ge(sig_ga, i + 1)
                        dve.wait_ge(blk_used, blk(FIRST_OUT + 3 * j + 2))
                        dve.tensor_tensor(dst[:, j % 4, c], sgc[:], ps[:, 4 + h, :], ALU.mult).then_inc(mix1, 1)
                        dve.tensor_tensor(sga[:], sga[:], ps[:, 6 + h, :], ALU.mult).then_inc(mix2, 1)
                        dve.wait_ge(mix1, i + 1)
                        dve.wait_ge(mix2, i + 1)
                        dve.tensor_tensor(dst[:, j % 4, c], dst[:, j % 4, c], sga[:], ALU.add).then_inc(mixed, 1)
                for j in range(KC):
                    src = mixa if j < 4 else mixb
                    dve.wait_ge(m_hi, j + 1)
                    dve.tensor_tensor(ml[:, j, :], src[:, j % 4, :], mh[:, j, :], ALU.subtract).then_inc(m_lo, 1)

                def finish_row(t):
                    for h in range(2):
                        dve.bn_stats(st6[:, h, :], x1[:, t, HALF * h:HALF * h + HALF]).then_inc(var_ok, 1)
                    dve.wait_ge(var_ok, 2 * t + 2)
                    dve.bn_aggr(mv[:, t, :], st6[:]).then_inc(st_ok, 1)
                    dve.wait_ge(sd_ok, t + 1)
                    dve.reciprocal(rstd[:, t:t + 1], rstd[:, t:t + 1]).then_inc(rst_ok, 1)
                    dve.wait_ge(rst_ok, t + 1)
                    dve.scalar_tensor_tensor(out=nmr[:, t:t + 1], in0=mv[:, t, 0:1], scalar=-1.0, in1=rstd[:, t:t + 1],
                                             op0=ALU.mult, op1=ALU.mult).then_inc(nmr_ok, 1)

                def affine_row(t):
                    dve.wait_ge(ln_a, t + 1)
                    dve.tensor_tensor(x1[:, t, :], x1[:, t, :], g1_b[:], ALU.mult).then_inc(ln_g, 1)
                    dve.wait_ge(ln_g, t + 1)
                    dve.tensor_tensor(x1[:, t, :], x1[:, t, :], b1_b[:], ALU.add).then_inc(x1_ok, 1)

                for g in range(4):
                    for t in range(TT):
                        c = slice(2 * P * g, 2 * P * g + 2 * P)
                        dve.wait_ge(wo_done, TT * g + t + 1)
                        if g == 0:
                            dve.wait_ge(xres_ok, t + 1)
                        dve.tensor_tensor(x1[:, t, c], x1[:, t, c], ps[:, t, 0:2 * P], ALU.add).then_inc(wo_add, 1)
                        if g == 3:
                            dve.wait_ge(wo_add, TT * g + t + 1)
                            if t:
                                affine_row(t - 1)
                            finish_row(t)
                affine_row(TT - 1)

        moe(nc, sem, locals())
    return nc


def moe(nc, sem, m):
    (x1, w_e, xg, xgt, sg, hb, hbt, ys, rt, y1, y2, g2_b, b2_b, cst, eps, st6, mv, rstd, nmr, wgt, slot_i, ids_i,
     id_now, e_tab, s_tab, cum_i, ends_i, br_b, ps, psf, ident) = (m[k] for k in (
         "x1 w_e xg xgt sg hb hbt ys rt y1 y2 g2_b b2_b cst eps st6 mv rstd nmr wgt slot_i ids_i "
         "id_now e_tab s_tab cum_i ends_i br_b ps psf ident").split())
    w_r, b_r, wexp, ln2_g, ln2_b, consts, out, x1_dram, y_dram = (
        m[k] for k in "w_r b_r wexp ln2_g ln2_b consts out x1_dram y_dram".split())
    wr_in = sem("wr_in"); w_in = [sem(f"we_in{i}") for i in range(3)]; expert_in = sem("expert_in")
    xt_r = sem("xt_r"); xt_rc = sem("xt_rc"); lg_done = sem("lg_done")
    rchain = sem("rchain"); r_exp = sem("r_exp"); r_exp_in = sem("r_exp_in")
    m_ready = sem("m_ready"); pos_done = sem("pos_done"); hot = sem("hot"); hot_used = sem("hot_used"); ids_done = sem("ids_done")
    tables = sem("tables"); ids_ok = sem("ids_ok")
    idc = sem("idc"); id_set = sem("id_set"); gath = sem("gath")
    tx_done = sem("tx_done"); tx_ok = sem("tx_ok"); gu_done = sem("gu_done"); silu_ok = sem("silu_ok"); h_ok = sem("h_ok")
    th_done = sem("th_done"); th_ok = sem("th_ok"); dn_done = sem("dn_done"); y_ok = sem("y_ok"); y_out = sem("y_out")
    ln2_in = sem("ln2_in"); y_in = [sem(f"y_in{i}") for i in range(2)]
    f_res = sem("f_res"); f_a = sem("f_a"); f_b = sem("f_b"); f_st = sem("f_st"); f_mv = sem("f_mv"); f_sd = sem("f_sd")
    f_rs = sem("f_rs"); f_nm = sem("f_nm"); f_ln = sem("f_ln"); f_g = sem("f_g"); f_ok = sem("f_ok"); f_out = sem("f_out")

    def tmp(i, n=128):
        return rt[:, 128 * i:128 * i + n]
    by_te = lambda a: a.rearrange("p (t e) -> p t e", e=NE)
    by_g = lambda a: a.rearrange("p (g e) -> p g e", e=EPG)
    wr_t = w_e[:, 2, 0, 0:P].rearrange("p (k e) -> p k e", e=NE)
    tri = cst[:, 0:P]
    iota = cst[:, C_IOTA - C_TRI:C_IOTA - C_TRI + P]
    tok = cst[:, C_TOK - C_TRI:C_TOK - C_TRI + TT]
    ones = w_e[:, 2, 1, 0:P]
    hot_a = w_e[:, 2, 2, :].rearrange("p (i n) -> p i n", n=P)
    hot_b = w_e[:, 2, 3, 0:8 * TAB].rearrange("p (i n) -> p i n", n=TAB)

    with nc.Block() as block:
        @block.sync
        def _(sp):
            sp.dma_start(wr_t, w_r).then_inc(wr_in, 16)
            sp.dma_start(br_b[:], b_r.partition_broadcast(P)).then_inc(wr_in, 16)
            sp.dma_start(cst[:], consts[:, C_TRI:C_WIDTH]).then_inc(wr_in, 16)

            def load_expert(e):
                for r in range(0, WROWS, 4):
                    sp.dma_start(w_e[:, e % 3, r:r + 4, :], wexp[e][:, r:r + 4, :]).then_inc(w_in[e % 3], 16)

            def announce(e):
                sp.wait_ge(w_in[e % 3], 48 * (e // 3 + 1))
                sp.sem_inc(expert_in, 1)
            load_expert(0)
            load_expert(1)
            announce(0)
            announce(1)
            sp.wait_ge(tables, 1)
            sp.wait_ge(ids_done, 2)
            load_expert(2)
            announce(2)
            for e in range(3, NE):
                last = sp.value_load(cum_i[0:1, e - 3:e - 2], min_val=1, max_val=MAX_TILES)
                sp.wait_ge(dn_done, last)
                load_expert(e)
                announce(e)
            total = sp.value_load(cum_i[0:1, NE - 1:NE], min_val=NE, max_val=MAX_TILES)
            sp.wait_ge(dn_done, total)
            sp.dma_start(g2_b[:], ln2_g.partition_broadcast(P)).then_inc(ln2_in, 16)
            sp.dma_start(b2_b[:], ln2_b.partition_broadcast(P)).then_inc(ln2_in, 16)
            for t in range(TT):
                sp.wait_ge(f_ok, t + 1)
                sp.dma_start(out[P * t:P * t + P, :], x1[:, t, :]).then_inc(f_out, 16)
            sp.wait_ge(f_out, 16 * TT)

        @block.gpsimd
        def _(pool):
            pool.wait_ge(ids_ok, 1)
            total = pool.value_load(cum_i[0:1, NE - 1:NE], min_val=NE, max_val=MAX_TILES)
            end2 = pool.value_load(ends_i[0:1, 0:1], min_val=NE - 2, max_val=MAX_TILES - 2)
            end1 = pool.value_load(ends_i[0:1, 1:2], min_val=NE - 1, max_val=MAX_TILES - 1)

            def gather(i):
                pool.tensor_copy(id_now[:], ids_i[:, bass.ds(i, 1)]).then_inc(idc, 1)
                pool.wait_ge(idc, i + 1)
                pool.sem_inc(id_set, 1)
                pool.indirect_dma_start(out=xg[:], out_offset=None, in_=x1_dram,
                                        in_offset=bass.IndirectOffsetOnAxis(ap=id_now[:, 0:1], axis=0)).then_inc(gath, 16)

            def store(i):
                pool.wait_ge(y_ok, i + 1)
                pool.dma_start(y_dram[bass.ds(i * P, P), :], ys[:]).then_inc(y_out, 16)

            def step(i):
                pool.wait_ge(tx_done, i)
                gather(i)

            gather(0)
            for i in range(1, 3):
                step(i)
            store(0)
            with pool.Fori(3, MAX_TILES) as i:
                with pool.If(i < total):
                    step(i)
                    store(i - 2)
                pool.nop()
            store(end2)
            store(end1)
            pool.wait_ge(y_out, end1 * 16 + 16)
            pool.sem_inc(id_set, 1)
            for t in range(TT):
                if t >= 2:
                    pool.wait_ge(f_b, 2 * (t - 1))
                for c, y in enumerate((y1, y2)):
                    pool.indirect_dma_start(out=y[:, t % 2, :], out_offset=None, in_=y_dram,
                                            in_offset=bass.IndirectOffsetOnAxis(ap=slot_i[:, c, t:t + 1], axis=0)
                                            ).then_inc(y_in[t % 2], 16)

        @block.tensor
        def _(pe):
            for t in range(TT):
                if t:
                    pe.wait_ge(xt_rc, t)
                for k in range(KC):
                    last = pe.transpose(psf[:, P * k:P * k + P], x1[:, t, P * k:P * k + P], ident)
                last.then_inc(xt_r, 1)
                pe.wait_ge(xt_rc, t + 1)
                if t == 0:
                    pe.wait_ge(wr_in, 48)
                for k in range(KC):
                    last = pe.matmul(ps[:, 2, NE * t:NE * t + NE], xgt[:, k, :], wr_t[:, k, :], start=k == 0, stop=k == KC - 1)
                last.then_inc(lg_done, 1)
            pe.wait_ge(m_ready, 2)
            pe.matmul(ps[:, 3, 0:P], tri, tmp(2), start=True, stop=True)
            pe.matmul(ps[:, 4, 0:P], ones, tmp(2), start=True, stop=True).then_inc(pos_done, 1)
            for c in range(2):
                pe.wait_ge(hot, c + 1)
                for t in range(TT):
                    last = pe.matmul(ps[:, 5, 0:TAB], hot_a[:, t, :], hot_b[:, t, :], start=c == 0 and t == 0,
                                     stop=c == 1 and t == TT - 1)
                last.then_inc(ids_done, 1)

            pe.wait_ge(tables, 1)
            total = pe.value_load(cum_i[0:1, NE - 1:NE], min_val=NE, max_val=MAX_TILES)
            end2 = pe.value_load(ends_i[0:1, 0:1], min_val=NE - 2, max_val=MAX_TILES - 2)
            end1 = pe.value_load(ends_i[0:1, 1:2], min_val=NE - 1, max_val=MAX_TILES - 1)

            def transpose_x(i, first=False):
                pe.wait_ge(gath, i * 16 + 16)
                if not first:
                    pe.wait_ge(tx_ok, i)
                for k in range(KC):
                    last = pe.transpose(psf[:, P * k:P * k + P], xg[:, P * k:P * k + P], ident)
                last.then_inc(tx_done, 1)

            def up(i):
                e = pe.value_load(e_tab[0:1, bass.ds(i, 1)], min_val=0, max_val=NE - 1)
                s = pe.value_load(s_tab[0:1, bass.ds(i, 1)], min_val=0, max_val=2)
                pe.wait_ge(tx_ok, i + 1)
                pe.wait_ge(expert_in, e + 1)
                for k in range(KC):
                    for h in range(2):
                        last = pe.matmul(ps[:, 2 + h, :], xgt[:, k, :], w_e[:, bass.ds(s, 1), k, HALF * h:HALF * h + HALF],
                                         start=k == 0, stop=k == KC - 1)
                last.then_inc(gu_done, 1)

            def transpose_h(i):
                pe.wait_ge(h_ok, i + 1)
                for k in range(FC):
                    last = pe.transpose(ps[:, 4, P * k:P * k + P], hb[:, P * k:P * k + P], ident)
                last.then_inc(th_done, 1)

            def down(i, first=False):
                s = pe.value_load(s_tab[0:1, bass.ds(i, 1)], min_val=0, max_val=2)
                pe.wait_ge(th_ok, i + 1)
                if not first:
                    pe.wait_ge(y_ok, i)
                for k in range(FC):
                    for h in range(2):
                        last = pe.matmul(ps[:, 6 + h, :], hbt[:, k, :], w_e[:, bass.ds(s, 1), KC + k, HALF * h:HALF * h + HALF],
                                         start=k == 0, stop=k == FC - 1)
                last.then_inc(dn_done, 1)

            transpose_x(0, True)
            up(0)
            transpose_x(1)
            transpose_h(0)
            up(1)
            transpose_x(2)
            down(0, True)
            transpose_h(1)
            up(2)
            with pe.Fori(3, MAX_TILES) as i:
                with pe.If(i < total):
                    transpose_x(i)
                    down(i - 2)
                    transpose_h(i - 1)
                    up(i)
                pe.nop()
            down(end2)
            transpose_h(end1)
            down(end1)

        @block.scalar
        def _(act):
            for t in range(TT):
                act.wait_ge(xt_r, t + 1)
                if t:
                    act.wait_ge(lg_done, t)
                act.activation(xgt[:, :, :].rearrange("p k c -> p (k c)"), psf[:, 0:SEQ], ACT.Copy).then_inc(xt_rc, 1)
            act.wait_ge(r_exp_in, 1)
            act.activation(tmp(0), tmp(0), ACT.Exp).then_inc(r_exp, 1)
            act.wait_ge(tables, 1)
            total = act.value_load(cum_i[0:1, NE - 1:NE], min_val=NE, max_val=MAX_TILES)
            end2 = act.value_load(ends_i[0:1, 0:1], min_val=NE - 2, max_val=MAX_TILES - 2)
            end1 = act.value_load(ends_i[0:1, 1:2], min_val=NE - 1, max_val=MAX_TILES - 1)

            def x_t(i, first=False):
                act.wait_ge(tx_done, i + 1)
                if not first:
                    act.wait_ge(gu_done, i)
                act.activation(xgt[:, :, :].rearrange("p k c -> p (k c)"), psf[:, 0:SEQ], ACT.Copy).then_inc(tx_ok, 1)

            def silu(i, first=False):
                act.wait_ge(gu_done, i + 1)
                if not first:
                    act.wait_ge(h_ok, i)
                act.activation(sg[:], ps[:, 2, :], ACT.Silu).then_inc(silu_ok, 1)

            def h_t(i, first=False):
                act.wait_ge(th_done, i + 1)
                if not first:
                    act.wait_ge(dn_done, i)
                act.activation(hbt[:, :, :].rearrange("p k c -> p (k c)"), ps[:, 4, :], ACT.Copy).then_inc(th_ok, 1)

            x_t(0, True)
            silu(0, True)
            x_t(1)
            h_t(0, True)
            silu(1)
            x_t(2)
            h_t(1)
            silu(2)
            with act.Fori(3, MAX_TILES) as i:
                with act.If(i < total):
                    x_t(i)
                    h_t(i - 1)
                    silu(i)
                act.nop()
            h_t(end1)
            for t in range(TT):
                act.wait_ge(f_mv, t + 1)
                act.activation(rstd[:, t:t + 1], mv[:, t, 1:2], ACT.Sqrt, bias=eps[:]).then_inc(f_sd, 1)
                act.wait_ge(f_nm, t + 1)
                act.activation(x1[:, t, :], x1[:, t, :], ACT.Identity, scale=rstd[:, t:t + 1],
                               bias=nmr[:, t:t + 1]).then_inc(f_ln, 1)

        @block.vector
        def _(dve):
            count = [0]

            def link(ins):
                count[0] += 1
                ins.then_inc(rchain, 1)
                dve.wait_ge(rchain, count[0])

            V = nc.vector
            link(V.memset(ones, 1.0))
            V_te = lambda a: a.unsqueeze(2).broadcast_to([P, TT, NE])
            dve.wait_ge(lg_done, TT)
            dve.wait_ge(wr_in, 48)
            p, t1 = tmp(0), tmp(1)
            link(V.tensor_tensor(by_te(p), by_te(ps[:, 2, 0:P]), br_b[:, :].unsqueeze(1).broadcast_to([P, TT, NE]), ALU.add))
            link(V.reduce_max(tmp(13, TT), by_te(p), AX.X))
            V.tensor_tensor(by_te(p), by_te(p), V_te(tmp(13, TT)), ALU.subtract).then_inc(r_exp_in, 1)
            dve.wait_ge(r_exp, 1)
            link(V.reduce_sum(tmp(13, TT), by_te(p), AX.X))
            link(V.reciprocal(tmp(13, TT), tmp(13, TT)))
            link(V.tensor_tensor(by_te(p), by_te(p), V_te(tmp(13, TT)), ALU.mult))

            def rank(dst, src, n, pair):
                d = dst.rearrange("p (g e) -> p g e", e=EPG)
                s = src.rearrange("p (g e) -> p g e", e=EPG)
                for a in range(EPG):
                    last = V.memset(d[:, :, a], float(EPG - 1 - a))
                link(last)
                for b in range(EPG):
                    for a in range(b + 1, EPG):
                        link(V.tensor_tensor(pair, s[:, :, b], s[:, :, a], ALU.is_ge))
                        link(V.tensor_tensor(d[:, :, a], d[:, :, a], pair, ALU.add))
                        link(V.tensor_tensor(d[:, :, b], d[:, :, b], pair, ALU.subtract))

            rk = tmp(3)
            rank(rk, p, 32, tmp(12, 32))
            link(V.tensor_scalar(t1, rk, 1.5, None, ALU.is_lt))
            link(V.tensor_tensor(t1, t1, p, ALU.mult))
            gs = tmp(13, 32)
            link(V.reduce_sum(gs, by_g(t1), AX.X))
            gr = tmp(11, 32)
            rank(gr, gs, 8, tmp(12, 8))
            link(V.tensor_scalar(gr, gr, 0.5, None, ALU.is_lt))
            picks = (tmp(4), tmp(5))
            for c, pick in enumerate(picks):
                link(V.tensor_scalar(pick, rk, float(c), None, ALU.is_equal))
                link(V.tensor_tensor(by_g(pick), by_g(pick), gr.unsqueeze(2).broadcast_to([P, 32, EPG]), ALU.mult))
            V.tensor_tensor(tmp(2), picks[0], picks[1], ALU.add).then_inc(m_ready, 1)
            dve.wait_ge(m_ready, 1)
            for c, pick in enumerate(picks):
                link(V.tensor_tensor(t1, p, pick, ALU.mult))
                link(V.reduce_sum(wgt[:, c, :], by_te(t1), AX.X))
            V.memset(tmp(13, 8), 0.0).then_inc(m_ready, 1)
            dve.wait_ge(m_ready, 2)
            link(V.tensor_tensor(tmp(13, TT), wgt[:, 0, :], wgt[:, 1, :], ALU.add))
            link(V.reciprocal(tmp(13, TT), tmp(13, TT)))
            for c in range(2):
                link(V.tensor_tensor(wgt[:, c, :], wgt[:, c, :], tmp(13, TT), ALU.mult))
            dve.wait_ge(pos_done, 1)
            pos, tot = by_te(tmp(6)), by_te(tmp(7))
            link(V.tensor_copy(tmp(6), ps[:, 3, 0:P]))
            link(V.tensor_copy(tmp(7), ps[:, 4, 0:P]))
            acc = tmp(13, NE)
            link(V.tensor_copy(acc, tot[:, 0, :]))
            for t in range(1, TT):
                link(V.tensor_tensor(pos[:, t, :], pos[:, t, :], acc, ALU.add))
                link(V.tensor_tensor(acc, acc, tot[:, t, :], ALU.add))
            thr = cst[:, C_THR - C_TRI:C_THR - C_TRI + 7]
            cmp7 = tmp(8, NE * 7).rearrange("p (e k) -> p e k", k=7)
            link(V.tensor_tensor(cmp7, acc.unsqueeze(2).broadcast_to([P, NE, 7]), thr.unsqueeze(1).broadcast_to([P, NE, 7]), ALU.is_gt))
            nt = tmp(9, NE)
            link(V.reduce_sum(nt, cmp7, AX.X))
            link(V.tensor_scalar(nt, nt, 1.0, None, ALU.add))
            cum = rt[:, 128 * 9 + 16:128 * 9 + 32]
            link(V.tensor_copy(cum, nt))
            for e in range(1, NE):
                link(V.tensor_tensor(cum[:, e:e + 1], cum[:, e:e + 1], cum[:, e - 1:e], ALU.add))
            base = rt[:, 128 * 9 + 32:128 * 9 + 48]
            link(V.tensor_tensor(base, cum, nt, ALU.subtract))
            i32 = iota[:, 0:TAB]
            et = rt[:, 128 * 9 + 64:128 * 9 + 96]
            st = rt[:, 128 * 9 + 96:128 * 9 + 128]
            big = rt[:, 128 * 7:128 * 11].rearrange("p (i e) -> p i e", e=NE)
            link(V.memset(et, 0.0))
            for e in range(NE):
                link(V.tensor_scalar(st, i32, cum[:, e:e + 1], None, ALU.is_ge))
                link(V.tensor_tensor(et, et, st, ALU.add))
            link(V.tensor_scalar(et, et, float(NE - 1), None, ALU.min))
            link(V.tensor_copy(e_tab[:], et))
            link(V.tensor_copy(st, et))
            for k in range(1, 6):
                link(V.tensor_scalar(tmp(8, TAB), et, 3.0 * k, -3.0, ALU.is_ge, ALU.mult))
                link(V.tensor_tensor(st, st, tmp(8, TAB), ALU.add))
            link(V.tensor_copy(s_tab[:], st))
            link(V.tensor_scalar(ends_i[:, 0:1], cum[:, NE - 1:NE], -2.0, None, ALU.add))
            link(V.tensor_scalar(ends_i[:, 1:2], cum[:, NE - 1:NE], -1.0, None, ALU.add))
            V.tensor_copy(cum_i[:], cum).then_inc(tables, 1)
            dve.wait_ge(tables, 1)
            for c, pick in enumerate(picks):
                hi, lo, a8 = tmp(12, 8), rt[:, 128 * 12 + 8:128 * 12 + 16], rt[:, 128 * 12 + 16:128 * 12 + 24]
                link(V.tensor_tensor(t1, pick, tmp(6), ALU.mult))
                link(V.reduce_sum(lo, by_te(t1), AX.X))
                link(V.tensor_tensor(by_te(t1), by_te(pick), base.unsqueeze(1).broadcast_to([P, TT, NE]), ALU.mult))
                link(V.reduce_sum(hi, by_te(t1), AX.X))
                c8 = tmp(8, TT * 7).rearrange("p (t k) -> p t k", k=7)
                link(V.tensor_tensor(c8, lo.unsqueeze(2).broadcast_to([P, TT, 7]), thr.unsqueeze(1).broadcast_to([P, TT, 7]), ALU.is_ge))
                link(V.reduce_sum(a8, c8, AX.X))
                link(V.tensor_tensor(hi, hi, a8, ALU.add))
                link(V.scalar_tensor_tensor(out=lo, in0=a8, scalar=-float(P), in1=lo, op0=ALU.mult, op1=ALU.add))
                link(V.scalar_tensor_tensor(out=a8, in0=hi, scalar=float(P), in1=lo, op0=ALU.mult, op1=ALU.add))
                link(V.tensor_copy(slot_i[:, c, :], a8))
                if c:
                    dve.wait_ge(ids_done, 1)
                for t in range(TT):
                    V.tensor_scalar(hot_a[:, t, :], iota, lo[:, t:t + 1], None, ALU.is_equal)
                    last = V.tensor_scalar(hot_b[:, t, :], i32, hi[:, t:t + 1], tok[:, t:t + 1],
                                           ALU.is_equal, ALU.mult)
                    link(last) if t < TT - 1 else last.then_inc(hot, 1)
                dve.wait_ge(hot, c + 1)
            dve.wait_ge(ids_done, 2)
            V.tensor_copy(ids_i[:], ps[:, 5, 0:TAB]).then_inc(ids_ok, 1)

            total = dve.value_load(cum_i[0:1, NE - 1:NE], min_val=NE, max_val=MAX_TILES)
            end2 = dve.value_load(ends_i[0:1, 0:1], min_val=NE - 2, max_val=MAX_TILES - 2)
            end1 = dve.value_load(ends_i[0:1, 1:2], min_val=NE - 1, max_val=MAX_TILES - 1)

            def gate(i, first=False):
                dve.wait_ge(silu_ok, i + 1)
                if not first:
                    dve.wait_ge(th_done, i)
                dve.tensor_tensor(hb[:], sg[:], ps[:, 3, :], ALU.mult).then_inc(h_ok, 1)

            def y(i, first=False):
                dve.wait_ge(dn_done, i + 1)
                if not first:
                    dve.wait_ge(y_out, i * 16)
                dve.tensor_copy(ys[:], psf[:, 6 * HALF:8 * HALF]).then_inc(y_ok, 1)

            gate(0, True)
            gate(1)
            y(0, True)
            gate(2)
            with dve.Fori(3, MAX_TILES) as i:
                with dve.If(i < total):
                    y(i - 2)
                    gate(i)
                dve.nop()
            y(end2)
            y(end1)

            def combine(t):
                dve.tensor_scalar(x1[:, t, :], x1[:, t, :], ALPHA, None, ALU.mult).then_inc(f_a, 1)
                dve.wait_ge(f_a, t + 1)
                dve.wait_ge(y_in[t % 2], 32 * (t // 2 + 1))
                for c, yy in enumerate((y1, y2)):
                    dve.scalar_tensor_tensor(out=x1[:, t, :], in0=yy[:, t % 2, :], scalar=wgt[:, c, t:t + 1],
                                             in1=x1[:, t, :], op0=ALU.mult, op1=ALU.add).then_inc(f_b, 1)
                    dve.wait_ge(f_b, 2 * t + c + 1)
                for h in range(2):
                    dve.bn_stats(st6[:, h, :], x1[:, t, HALF * h:HALF * h + HALF]).then_inc(f_st, 1)
                dve.wait_ge(f_st, 2 * t + 2)
                dve.bn_aggr(mv[:, t, :], st6[:]).then_inc(f_mv, 1)
                dve.wait_ge(f_sd, t + 1)
                dve.reciprocal(rstd[:, t:t + 1], rstd[:, t:t + 1]).then_inc(f_rs, 1)
                dve.wait_ge(f_rs, t + 1)
                dve.scalar_tensor_tensor(out=nmr[:, t:t + 1], in0=mv[:, t, 0:1], scalar=-1.0, in1=rstd[:, t:t + 1],
                                         op0=ALU.mult, op1=ALU.mult).then_inc(f_nm, 1)

            def affine(t):
                dve.wait_ge(f_ln, t + 1)
                dve.tensor_tensor(x1[:, t, :], x1[:, t, :], g2_b[:], ALU.mult).then_inc(f_g, 1)
                dve.wait_ge(f_g, t + 1)
                dve.tensor_tensor(x1[:, t, :], x1[:, t, :], b2_b[:], ALU.add).then_inc(f_ok, 1)

            dve.wait_ge(ln2_in, 32)
            for t in range(TT):
                combine(t)
                if t:
                    affine(t - 1)
            affine(TT - 1)


def laid_out(x, w_in, b_in, w_dw, b_dw, ln_conv_g, ln_conv_b, w_conv_out, rel_bias, w_attn_out, w_o, b_o,
             ln1_g, ln1_b, w_router, b_router, w_gate_up, w_down, ln2_g, ln2_b):
    con = np.ascontiguousarray
    x = np.asarray(x)[0]
    w_all = np.concatenate([np.asarray(w_in)[0], np.concatenate([np.asarray(w_conv_out)[0], np.asarray(w_attn_out)[0]], 0),
                            np.asarray(w_o)[0]], 1)
    blocks = w_all.reshape(KC, P, -1, P).transpose(2, 1, 0, 3)[block_columns()]
    rel = np.clip(np.arange(P)[:, None] - np.arange(BANDW)[None, :] + 512, -256, 256) + 256
    band = np.asarray(rel_bias)[0][:, rel]
    wexp = np.concatenate([np.asarray(w_gate_up)[0].reshape(NE, KC, P, 2 * FF), np.asarray(w_down)[0].reshape(NE, FC, P, D)], 1)
    col = lambda a, n: con(np.asarray(a)[0].reshape(n, P).T)
    return {
        "xT": con(x.T.reshape(KC, P, SEQ)), "x": con(x), "wblk": con(blocks), "b_in": col(b_in, 36),
        "dw": con(np.asarray(w_dw)[0].T.reshape(CB, P, CW).transpose(1, 0, 2)),
        "dwb": col(b_dw, CB), "lncg": col(ln_conv_g, CB), "lncb": col(ln_conv_b, CB),
        "relb": con(band.reshape(PAIRS, 2, P, BANDW).transpose(0, 2, 1, 3)),
        "b_o": con(np.asarray(b_o)[0]), "ln1_g": con(np.asarray(ln1_g)[0]), "ln1_b": con(np.asarray(ln1_b)[0]),
        "w_r": con(np.asarray(w_router).reshape(KC, P, NE).transpose(1, 0, 2)), "b_r": con(np.asarray(b_router)),
        "wexp": con(wexp.transpose(0, 2, 1, 3)),
        "ln2_g": con(np.asarray(ln2_g)[0]), "ln2_b": con(np.asarray(ln2_b)[0]), "consts": constants(),
    }


def kernel(**inputs):
    import concourse.bacc as bacc
    from concourse.bass_utils import run_bass_kernel_spmd

    nc = bacc.Bacc("TRN2", target_bir_lowering=False, num_devices=1)
    arrays = {f"in_{k}": v for k, v in laid_out(**inputs).items()}
    args = [nc.dram_tensor(n, a.shape, F32, kind="ExternalInput").ap() for n, a in arrays.items()]
    out = nc.dram_tensor("out_rows", (SEQ, D), F32, kind="ExternalOutput").ap()
    encoder_layer(nc, *args, out)
    r = run_bass_kernel_spmd(nc, [arrays], core_ids=[0])
    return r.results[0]["out_rows"].reshape(1, SEQ, D)
```

```python
import numpy as np
import concourse.bass as bass
from concourse import mybir
from contextlib import ExitStack

F32 = mybir.dt.float32
F32R = mybir.dt.float32r
I32 = mybir.dt.int32
U32 = mybir.dt.uint32
ALU = mybir.AluOpType
ACT = mybir.ActivationFunctionType
AX = mybir.AxisListType

P = 128
D = 1024
SEQ = 1024
KC = D // P
TT = SEQ // P
HALF = 512
DC = 512
CB = DC // P
CW = 31
PAD = CW - 1
HEADS, HD = 8, 64
PAIRS = HEADS // 2
BANDT = 5
BANDW = BANDT * P
SCALE = HD ** -0.5
NE, NGRP, EPG = 16, 4, 4
FF = 512
FC = FF // P
MAX_TILES = NE + (2 * SEQ - 1) // P
TAB = 32
WROWS = KC + FC
ALPHA = 2.0 ** 0.25
EPS = 1e-5
MASKED = -1e30
RING, RAWS = 4, 2

N_GLU = 2 * CB
N_SEG = 2 + 2 * 2
N_ATT = 2 * N_SEG
FIRST_OUT = N_GLU + N_ATT
FIRST_WO = FIRST_OUT + 3 * KC
N_BLOCKS = FIRST_WO + KC


def block_columns():
    a, g, q, k, v, gc, ga = (np.cumsum([0, 4, 4, 4, 4, 4, 8])).tolist()
    o, wo = 36, 44
    cols = []
    for j in range(CB):
        cols += [a + j, g + j]
    for s in range(2):
        cols += [v + 2 * s, v + 2 * s + 1, q + 2 * s, k + 2 * s, q + 2 * s + 1, k + 2 * s + 1]
    for j in range(KC):
        cols += [gc + j, ga + j, o + j]
    cols += [wo + j for j in range(KC)]
    return cols


C_ID, C_TRI, C_IOTA, C_TOK, C_THR, C_UPTO, C_BEFORE, C_EARLIER = 0, 128, 256, 384, 392, 400, 656, 720
C_WIDTH = 736
C_REST = C_WIDTH - C_TRI


def constants():
    c = np.zeros((P, C_WIDTH), np.float32)
    c[:, C_ID:C_ID + P] = np.eye(P)
    c[:, C_TRI:C_TRI + P] = np.triu(np.ones((P, P)), 1)
    c[:, C_IOTA:C_IOTA + P] = np.arange(P)[None, :]
    c[:, C_TOK:C_TOK + TT] = np.arange(P)[:, None] + P * np.arange(TT)[None, :]
    c[:, C_THR:C_THR + 7] = P * np.arange(1, 8)[None, :]
    c[:, C_UPTO:C_UPTO + NE * NE] = np.tril(np.ones((NE, NE))).ravel()
    c[:, C_BEFORE:C_BEFORE + TT * TT] = np.tril(np.ones((TT, TT)), -1).ravel()
    c[:, C_EARLIER:C_EARLIER + 16] = np.tril(np.ones((4, 4)), -1).ravel()
    return c


def encoder_layer(nc, xT, x, wblk, b_in, dw, dwb, lncg, lncb, relb, b_o, ln1_g, ln1_b,
                  w_r, b_r, wexp, ln2_g, ln2_b, consts, out):
    x1_dram = nc.dram_tensor("x1_rows", (SEQ, D), F32, kind="Internal").ap()
    y_dram = nc.dram_tensor("y_slots", (MAX_TILES * P, D), F32, kind="Internal").ap()
    ctx = ExitStack()
    with ctx:
        ARENA = 207 * 1024 + 512
        arena = ctx.enter_context(nc.sbuf_tensor("arena", [P, ARENA], mybir.dt.uint8))
        base = nc.sbuf_base - ARENA
        KB = 1024

        def at(name, shape, dt, kb):
            size = int(np.prod(shape[1:])) * 4
            assert kb * KB + size <= ARENA, name
            return nc.alloc_sbuf_tensor_at(name, shape, dt, offset=base + int(kb * KB))

        xh = at("xh", [P, KC, SEQ], F32R, 0)
        xl = at("xl", [P, KC, SEQ], F32R, 32)
        wh = at("wh", [P, RING, KC, P], F32R, 64)
        wl = at("wl", [P, RING, KC, P], F32R, 80)
        raw = at("raw", [P, RAWS, KC, P], F32, 96)
        attn = at("attn", [P, PAIRS, SEQ], F32, 104)
        u = at("u", [P, CB, PAD + SEQ], F32, 120)
        cv = at("cv", [P, CB, SEQ], F32, 136.5)
        qh = at("qh", [P, SEQ], F32R, 152.5)
        ql = at("ql", [P, SEQ], F32R, 156.5)
        kh = at("kh", [P, SEQ], F32R, 160.5)
        kl = at("kl", [P, SEQ], F32R, 164.5)
        vh = at("vh", [P, TT, 2 * P], F32R, 168.5)
        vl = at("vl", [P, TT, 2 * P], F32R, 176.5)
        bias = at("bias", [P, 2, BANDW], F32, 184.5)
        pr = (at("pr0", [P, 2, BANDW], F32, 189.5), at("pr1", [P, 2, BANDW], F32, 120))
        pth = at("pth", [P, BANDT, 2, P], F32R, 194.5)
        ptl = at("ptl", [P, BANDT, 2, P], F32R, 199.5)
        tapped = at("tapped", [P, SEQ], F32, 116)
        xraw = at("xraw", [P, KC, SEQ], F32, 152.5)
        sig = at("sig", [P, 2, SEQ], F32, 189.5)
        ah = at("ah", [P, PAIRS, SEQ], F32R, 152.5)
        al = at("al", [P, PAIRS, SEQ], F32R, 168.5)
        uoh = at("uoh", [P, CB, SEQ], F32R, 120)
        uol = at("uol", [P, CB, SEQ], F32R, 136.5)
        mixa = at("mixa", [P, 4, SEQ], F32, 104)
        mixb = at("mixb", [P, 4, SEQ], F32, 184.5)
        sqr = at("sqr", [P, 2, SEQ], F32, 184.5)
        rstdc = at("rstdc", [P, SEQ], F32, 192.5)
        act_u = at("act_u", [P, 1, SEQ], F32, 196.5)
        sgc = at("sgc", [P, HALF], F32, 200.5)
        sga = at("sga", [P, HALF], F32, 202.5)
        mh = at("mh", [P, KC, SEQ], F32R, 0)
        ml = at("ml", [P, KC, SEQ], F32R, 32)
        x1 = at("x1", [P, TT, D], F32, 170)
        bo_b = at("bo_b", [P, D], F32, 152.5)
        g1_b = at("g1_b", [P, D], F32, 156.5)
        b1_b = at("b1_b", [P, D], F32, 160.5)
        wh2 = at("wh2", [P, 4, KC, P], F32R, 120)
        wl2 = at("wl2", [P, 4, KC, P], F32R, 136)
        x1t = at("x1t", [P, KC, P], F32, 164.5)
        hot_a = at("hot_a", [P, 2, TT, P], F32, 96)
        cst = at("cst", [P, C_REST], F32, 104)
        wr_t = at("wr_t", [P, KC, NE], F32, 106.5)
        ones = at("ones", [P, P], F32, 107)
        hot_b = at("hot_b", [P, 2, TT, TAB], F32, 107.5)
        rt = at("rt", [P, 10, P], F32, 109.5)
        big = at("big", [P, TT * NE * TT], F32, 114.5)
        gu_h = at("gu_h", [P, 2, KC, 1024], F32R, 0)
        gu_l = at("gu_l", [P, 2, KC, 1024], F32R, 64)
        gu_raw = at("gu_raw", [P, 2, KC, 1024], F32, 64)
        dn_h = at("dn_h", [P, FC, 1024], F32R, 128)
        dn_l = at("dn_l", [P, FC, 1024], F32R, 144)
        dn_raw = at("dn_raw", [P, FC, 1024], F32, 160)
        xg = at("xg", [P, D], F32, 176)
        xgh = at("xgh", [P, D], F32R, 180)
        xgl = at("xgl", [P, D], F32R, 184)
        hb = at("hb", [P, FF], F32, 188)
        hbh = at("hbh", [P, FF], F32R, 190)
        hbl = at("hbl", [P, FF], F32R, 192)
        ys = at("ys", [P, D], F32, 194)
        xf = at("xf", [P, TT, D], F32, 0)
        y1 = at("y1", [P, 4, D], F32, 32)
        y2 = at("y2", [P, 4, D], F32, 48)
        g2_b = at("g2_b", [P, D], F32, 64)
        b2_b = at("b2_b", [P, D], F32, 68)
        small = 204.5

        def tiny(name, shape, dt=F32):
            nonlocal small
            t = at(name, shape, dt, small)
            small += -(-int(np.prod(shape[1:])) * 4 // 32) * 32 / KB
            return t
        b_in_t = tiny("b_in_t", [P, 36])
        cpar = tiny("cpar", [P, 3, CB])
        dw_t = tiny("dw_t", [P, CB, CW])
        eps = tiny("eps", [P, 1])
        mx = tiny("mx", [P, 2])
        nmx = tiny("nmx", [P, 2])
        rs = tiny("rs", [P, 2])
        rinv = tiny("rinv", [P, 2])
        st6 = tiny("st6", [P, 2, 6])
        mv = tiny("mv", [P, TT, 2])
        rstd = tiny("rstd", [P, TT])
        nmr = tiny("nmr", [P, TT])
        wgt = tiny("wgt", [P, 2, TT])
        slot_i = tiny("slot_i", [P, 2, TT], I32)
        ids_i = tiny("ids_i", [P, TAB], I32)
        id_now = tiny("id_now", [P, 1], I32)
        tab = tiny("tab", [P, 5, TAB], I32)
        cum_i = tiny("cum_i", [P, NE], I32)
        ends_i = tiny("ends_i", [P, 2], I32)
        rows_i = tiny("rows_i", [P, NE], I32)
        br_b = tiny("br_b", [P, NE])
        ident_t = tiny("ident_t", [P, P])
        ident = ident_t[:]

        ps = ctx.enter_context(nc.psum_tensor("ps", [P, 8, HALF], F32))
        psf = ps[:, :, :].rearrange("p b n -> p (b n)")

        def sem(name):
            return ctx.enter_context(nc.semaphore(name))

        x_in = [sem(f"x_in{k}") for k in range(KC)]
        par_in = sem("par_in")
        raw_in = [sem(f"raw_in{r}") for r in range(RAWS)]
        bias_in = sem("bias_in")
        x_hi = sem("x_hi"); x_lo = sem("x_lo")
        w_hi = sem("w_hi"); w_lo = sem("w_lo")
        blk_used = sem("blk_used")
        sig_ready = sem("sig_ready"); u_ready = sem("u_ready")
        conv_d = sem("conv_d"); conv_p = sem("conv_p"); init_d = sem("init_d"); init_p = sem("init_p")
        v_done = sem("v_done"); v_hi = sem("v_hi"); v_lo = sem("v_lo")
        qk_half = sem("qk_half"); qk_hi = sem("qk_hi"); qk_lo = sem("qk_lo")
        bias_ok = sem("bias_ok")
        s_done = sem("s_done"); s_max = sem("s_max"); s_nmx = sem("s_nmx"); exp_done = sem("exp_done")
        p_inv = sem("p_inv"); p_ready = sem("p_ready")
        t_done = sem("t_done"); pt_hi = sem("pt_hi"); pt_lo = sem("pt_lo")
        pv_done = sem("pv_done"); o_done = sem("o_done")
        a_hi = sem("a_hi"); a_lo = sem("a_lo")
        mean_done = sem("mean_done"); cent = sem("cent"); sq_done = sem("sq_done"); sq_used = sem("sq_used")
        var_done = sem("var_done"); std_done = sem("std_done"); rstd_ok = sem("rstd_ok")
        nrm = sem("nrm"); silu_done = sem("silu_done"); uo_hi = sem("uo_hi"); uo_lo = sem("uo_lo")
        sig_gc = sem("sig_gc"); sig_ga = sem("sig_ga")
        mix1 = sem("mix1"); mix2 = sem("mix2"); mixed = sem("mixed")
        m_hi = sem("m_hi"); m_lo = sem("m_lo")
        xres_in = [sem(f"xres_in{i}") for i in range(TT)]
        lnp_in = sem("lnp_in"); xres_ok = sem("xres_ok"); xres_s = sem("xres_s"); tap_p = sem("tap_p"); zero_ok = sem("zero_ok"); zero_out = sem("zero_out")
        wo_done = sem("wo_done"); wo_add = sem("wo_add")
        st_ok = sem("st_ok"); var_ok = sem("var_ok"); sd_ok = sem("sd_ok"); rst_ok = sem("rst_ok")
        nmr_ok = sem("nmr_ok"); ln_a = sem("ln_a"); ln_g = sem("ln_g"); x1_ok = sem("x1_ok")
        x1_out = sem("x1_out"); wr_in = sem("wr_in")

        def blk(n):
            return n + 1 - sum(2 for s in range(2) if n > N_GLU + N_SEG * s)

        def wait_used(eng, n):
            s, r = divmod(n - N_GLU, N_SEG)
            if 0 <= s < 2 and r < 2:
                eng.wait_ge(v_done, TT * (s + 1))
            elif n >= FIRST_WO:
                eng.wait_ge(wo_done, TT)
            else:
                eng.wait_ge(blk_used, blk(n))

        def tiles_of(c):
            return max(0, c - BANDT + 1), min(c, BANDT - 1) + 1

        def chunks(c):
            return (tiles_of(c)[1] + 1) // 2

        def chunks_before(n):
            return sum(chunks(i % TT) for i in range(n))

        def chunk(n, j):
            w = min(2, tiles_of(n % TT)[1] - 2 * j)
            return 4 + j, 2 * P * w, w

        moe_parts = moe(nc, sem, locals())

        with nc.Block() as block:
            @block.sync
            def _(sp):
                sp.dma_start(b_in_t[:], b_in).then_inc(par_in, 16)
                sp.dma_start(ident, consts[:, C_ID:C_ID + P]).then_inc(par_in, 16)
                for i, src in enumerate((dwb, lncg, lncb)):
                    sp.dma_start(cpar[:, i, :], src).then_inc(par_in, 16)
                sp.dma_start(dw_t[:], dw).then_inc(par_in, 16)

                def load_block(n):
                    if n >= RAWS:
                        sp.wait_ge(w_lo, n - RAWS + 1)
                    sp.dma_start(raw[:, n % RAWS], wblk[n]).then_inc(raw_in[n % RAWS], 16)

                def load_bias(b):
                    if b:
                        sp.wait_ge(s_max, 2 * TT * b)
                    sp.dma_start(bias[:], relb[b]).then_inc(bias_in, 16)

                for k in range(KC):
                    sp.dma_start(xraw[:, k, :], xT[k]).then_inc(x_in[k], 16)
                    if k < RAWS:
                        load_block(k)
                load_bias(0)
                after = {N_GLU + 6: 1, N_GLU + N_SEG + 4: 2, FIRST_OUT: 3}
                for n in range(RAWS, FIRST_WO + 4 + RAWS):
                    load_block(n)
                    if n in after:
                        load_bias(after[n])
                    for i in range(NE + 2 * (n - RAWS), min(NE + 2 * (n - RAWS) + 2, MAX_TILES)):
                        if i == NE:
                            sp.wait_ge(zero_ok, 1)
                        sp.dma_start(y_dram[P * i:P * i + P, :], tapped[:]).then_inc(zero_out, 16)
                sp.wait_ge(blk_used, blk(FIRST_WO - 1))
                for dst, src in ((bo_b, b_o), (g1_b, ln1_g), (b1_b, ln1_b)):
                    sp.dma_start(dst[:], src.partition_broadcast(P)).then_inc(lnp_in, 16)
                for t in range(TT):
                    if t == 3:
                        sp.wait_ge(m_lo, KC)
                    sp.dma_start(x1[:, t, :], x[P * t:P * t + P, :]).then_inc(xres_in[t], 16)
                for n in range(FIRST_WO + 4 + RAWS, N_BLOCKS):
                    load_block(n)
                sp.dma_start(cst[:], consts[:, C_TRI:C_WIDTH]).then_inc(wr_in, 16)
                sp.dma_start(wr_t[:], w_r).then_inc(wr_in, 16)
                sp.dma_start(br_b[:], b_r.partition_broadcast(P)).then_inc(wr_in, 16)
                sp.wait_ge(wo_done, TT)
                moe_parts["load_expert_0"](sp)
                for t in range(TT):
                    sp.wait_ge(x1_ok, t + 1)
                    sp.dma_start(x1_dram[P * t:P * t + P, :], x1[:, t, :]).then_inc(x1_out, 16)
                moe_parts["sync"](sp)

            @block.gpsimd
            def _(pool):
                pool.memset(tapped[:], 0.0).then_inc(zero_ok, 1)
                pool.memset(eps[:], EPS).then_inc(init_p, 1)
                pool.memset(u[:, :, 0:PAD], 0.0).then_inc(init_p, 1)

                def split_block(n):
                    own = n - FIRST_WO - RING
                    hi, lo = (wh2[:, own], wl2[:, own]) if own >= 0 else (wh[:, n % RING], wl[:, n % RING])
                    pool.wait_ge(raw_in[n % RAWS], 16 * (n // RAWS + 1))
                    if own >= 0:
                        wait_used(pool, FIRST_WO - 1)
                    elif n >= RING:
                        wait_used(pool, n - RING)
                    pool.tensor_scalar(hi, raw[:, n % RAWS], 1.0, 1.0, ALU.mult, ALU.mult).then_inc(w_hi, 1)
                    pool.wait_ge(w_hi, n + 1)
                    pool.tensor_tensor(lo, raw[:, n % RAWS], hi, ALU.subtract).then_inc(w_lo, 1)

                def conv_taps(j, k0, k1):
                    pool.wait_ge(u_ready, j + 1)
                    for k in range(k0, k1):
                        tap, w = u[:, j, k:k + SEQ], dw_t[:, j, k:k + 1]
                        if k == 0:
                            pool.tensor_scalar(cv[:, j, :], tap, w, cpar[:, 0, j:j + 1], ALU.mult, ALU.add).then_inc(conv_p, 1)
                        else:
                            if k > 1:
                                pool.wait_ge(conv_p, k)
                            pool.tensor_scalar(tapped[:], tap, w, 1.0, ALU.mult, ALU.mult).then_inc(tap_p, 1)
                            pool.wait_ge(tap_p, k)
                            pool.wait_ge(conv_p, k)
                            pool.tensor_tensor(cv[:, j, :], cv[:, j, :], tapped[:], ALU.add).then_inc(conv_p, 1)

                for n in range(N_GLU + 4):
                    split_block(n)
                pool.wait_ge(par_in, 96)
                pool.wait_ge(zero_out, 16 * (MAX_TILES - NE))
                for i in range(3):
                    conv_taps(CB - 1, 10 * i, min(10 * i + 10 + i // 2, CW))
                    split_block(N_GLU + 4 + 2 * i)
                    split_block(N_GLU + 5 + 2 * i)
                for n in range(N_GLU + 10, FIRST_WO + 4):
                    split_block(n)
                pool.wait_ge(lnp_in, 48)
                for t in range(TT):
                    pool.wait_ge(xres_s, t + 1)
                    pool.tensor_tensor(x1[:, t, :], x1[:, t, :], bo_b[:], ALU.add).then_inc(xres_ok, 1)
                for n in range(FIRST_WO + 4, N_BLOCKS):
                    split_block(n)
                moe_parts["gpsimd"](pool)

            @block.tensor
            def _(pe):
                def mm3(o, a_h, a_l, b_h, b_l, first, last):
                    pe.matmul(o, a_h, b_h, start=first, stop=False)
                    pe.matmul(o, a_h, b_l, start=False, stop=False)
                    return pe.matmul(o, a_l, b_h, start=False, stop=last)

                def weights_left(n, bank):
                    pe.wait_ge(w_lo, n + 1)
                    s = n % RING
                    for k in range(KC):
                        if n == 0:
                            pe.wait_ge(x_lo, k + 1)
                        for h in range(2):
                            c = slice(HALF * h, HALF * h + HALF)
                            last = mm3(ps[:, bank + h, :], wh[:, s, k], wl[:, s, k], xh[:, k, c], xl[:, k, c],
                                       k == 0, k == KC - 1)
                    return last

                for j in range(CB):
                    if j >= 2:
                        pe.wait_ge(u_ready, j - 1)
                    bank = 4 * (j % 2)
                    weights_left(2 * j, bank).then_inc(blk_used, 1)
                    weights_left(2 * j + 1, bank + 2).then_inc(blk_used, 1)

                def project_v(s):
                    n = N_GLU + N_SEG * s
                    pe.wait_ge(w_lo, n + 2)
                    r = n % RING
                    for t in range(TT):
                        i = TT * s + t
                        if i >= 4:
                            pe.wait_ge(v_lo, i - 3)
                        else:
                            pe.wait_ge(u_ready, CB)
                        if s and t == 0:
                            pe.wait_ge(o_done, 4 * TT)
                        c = slice(P * t, P * t + P)
                        for k in range(KC):
                            last = mm3(ps[:, 4 + t % 4, 0:2 * P], xh[:, k, c], xl[:, k, c],
                                       wh[:, r:r + 2, k, :], wl[:, r:r + 2, k, :], k == 0, k == KC - 1)
                        last.then_inc(v_done, 1)

                def project_qk(b):
                    n = N_GLU + N_SEG * (b // 2) + 2 + 2 * (b % 2)
                    if b:
                        pe.wait_ge(s_max, 2 * TT * b)
                    for i in range(2):
                        pe.wait_ge(w_lo, n + i + 1)
                        r = (n + i) % RING
                        for h in range(2):
                            c = slice(HALF * h, HALF * h + HALF)
                            for k in range(KC):
                                last = mm3(ps[:, 2 * i + h, :], wh[:, r, k], wl[:, r, k], xh[:, k, c], xl[:, k, c],
                                           k == 0, k == KC - 1)
                            last.then_inc(blk_used if h else qk_half, 1)

                def scores(n, h):
                    b, c = divmod(n, TT)
                    kt, nt = tiles_of(c)
                    if n:
                        pe.wait_ge(s_max, 2 * n - 1 + h)
                    r = slice(HD * h, HD * h + HD)
                    q = slice(P * c, P * c + P)
                    for k0 in range(0, nt * P, HALF):
                        w = min(HALF, nt * P - k0)
                        kk = slice(P * kt + k0, P * kt + k0 + w)
                        last = mm3(ps[:, 2 * h + k0 // HALF, 0:w], qh[r, q], ql[r, q], kh[r, kk], kl[r, kk], True, True)
                    last.then_inc(s_done, 1)

                def transpose_probs(n):
                    pe.wait_ge(p_ready, 2 * n + 2)
                    pe.wait_ge(pt_lo, chunks_before(n))
                    for j in range(chunks(n % TT)):
                        bank, _, w = chunk(n, j)
                        for t in range(w):
                            for h in range(2):
                                k = P * (2 * j + t)
                                last = pe.transpose(ps[:, bank, P * (2 * t + h):P * (2 * t + h) + P],
                                                    pr[n % 2][:, h, k:k + P], ident)
                        last.then_inc(t_done, 1)

                def weigh_values(n):
                    b, c = divmod(n, TT)
                    kt, nt = tiles_of(c)
                    if n:
                        pe.wait_ge(o_done, 2 * n)
                    v = slice(P * (b % 2), P * (b % 2) + P)
                    for t in range(nt):
                        pe.wait_ge(pt_lo, chunks_before(n) + t // 2 + 1)
                        last = mm3(ps[:, 7, 0:2 * P], vh[:, kt + t, v], vl[:, kt + t, v],
                                   pth[:, t], ptl[:, t], t == 0, t == nt - 1)
                    last.then_inc(pv_done, 1)

                for s in range(2):
                    project_v(s)
                    s0, s1 = 2 * TT * s, 2 * TT * (s + 1)
                    for n in range(s0, s1 + 2):
                        new_pair = n < s1 and n % TT == 0
                        if n < s1 and not new_pair:
                            for h in range(2):
                                scores(n, h)
                        if n == s0 + 2:
                            pe.wait_ge(v_lo, TT * (s + 1))
                        if n - 2 >= s0:
                            weigh_values(n - 2)
                        if new_pair:
                            project_qk(n // TT)
                        if s0 <= n - 1 < s1:
                            transpose_probs(n - 1)
                        if new_pair:
                            pe.wait_ge(qk_lo, 4 * (n // TT + 1))
                            for h in range(2):
                                scores(n, h)

                def channel_mean(bank, src, ready):
                    for j in range(CB):
                        ready(j)
                        for h in range(2):
                            last = pe.matmul(ps[:, bank + h, :], ones_c, src(j)[:, HALF * h:HALF * h + HALF],
                                             start=j == 0, stop=j == CB - 1)
                    return last

                ones_c = rstdc[:, 0:P]
                pe.wait_ge(init_d, 1)
                pe.wait_ge(conv_d, 3 * CW)
                pe.wait_ge(conv_p, CW)
                pe.wait_ge(pt_lo, chunks_before(TT * PAIRS))
                channel_mean(4, lambda j: cv[:, j, :], lambda j: None).then_inc(mean_done, 1)
                n = FIRST_OUT
                weights_left(n, 0).then_inc(blk_used, 1)
                pe.wait_ge(o_done, 2 * TT * PAIRS)
                for j in range(CB):
                    pe.wait_ge(sq_done, j + 1)
                    for h in range(2):
                        last = pe.matmul(ps[:, 6 + h, :], ones_c, sqr[:, j % 2, HALF * h:HALF * h + HALF],
                                         start=j == 0, stop=j == CB - 1)
                    last.then_inc(sq_used, 1)

                for j in range(KC):
                    n = FIRST_OUT + 3 * j
                    if j:
                        pe.wait_ge(sig_gc, 2 * j)
                        weights_left(n, 0).then_inc(blk_used, 1)
                        pe.wait_ge(sig_ga, 2 * j)
                    weights_left(n + 1, 2).then_inc(blk_used, 1)
                    s = (n + 2) % RING
                    pe.wait_ge(w_lo, n + 3)
                    if j == 0:
                        pe.wait_ge(rstd_ok, 1)
                        pe.wait_ge(cent, CB)
                        pe.wait_ge(uo_lo, CB)
                        pe.wait_ge(a_lo, PAIRS)
                    else:
                        pe.wait_ge(mix2, 2 * j)
                    for bank, hi, lo, k0 in ((4, uoh, uol, 0), (6, ah, al, CB)):
                        for k in range(CB):
                            for h in range(2):
                                c = slice(HALF * h, HALF * h + HALF)
                                last = mm3(ps[:, bank + h, :], wh[:, s, k0 + k], wl[:, s, k0 + k],
                                           hi[:, k, c], lo[:, k, c], k == 0, k == CB - 1)
                    last.then_inc(blk_used, 1)

                pe.wait_ge(mixed, 2 * KC)
                for g in range(2):
                    pe.wait_ge(w_lo, FIRST_WO + 4 * g + 4)
                    b_h, b_l = ((wh, wl), (wh2, wl2))[g]
                    for t in range(TT + 3 * g):
                        i = TT * g + t
                        if t < TT:
                            if i >= 4:
                                pe.wait_ge(wo_add, i - 3)
                            c = slice(P * t, P * t + P)
                            for k in range(KC):
                                if i == 0:
                                    pe.wait_ge(m_lo, k + 1)
                                last = mm3(ps[:, i % 4, :], mh[:, k, c], ml[:, k, c],
                                           b_h[:, :, k, :], b_l[:, :, k, :], k == 0, k == KC - 1)
                            last.then_inc(wo_done, 1)
                        if g and 2 <= t < TT + 2:
                            moe_parts["transpose_x1"](pe, t - 2)
                        if g and t >= 3:
                            moe_parts["logits"](pe, t - 3)
                moe_parts["tensor"](pe)

            @block.scalar
            def _(act):
                for k in range(KC):
                    act.wait_ge(x_in[k], 16)
                    act.activation(xh[:, k, :], xraw[:, k, :], ACT.Copy).then_inc(x_hi, 1)
                act.wait_ge(par_in, 96)
                for j in range(CB):
                    act.wait_ge(blk_used, blk(2 * j + 1))
                    if j >= 2:
                        act.wait_ge(u_ready, j - 1)
                    g = 4 * (j % 2) + 2
                    act.activation(sig[:, j % 2, :], psf[:, HALF * g:HALF * g + SEQ], ACT.Sigmoid,
                                   bias=b_in_t[:, CB + j:CB + j + 1]).then_inc(sig_ready, 1)

                def exponentials(n):
                    nt = tiles_of(n % TT)[1]
                    for h in range(2):
                        act.wait_ge(s_nmx, 2 * n + h + 1)
                        act.activation(pr[n % 2][:, h, 0:nt * P], pr[n % 2][:, h, 0:nt * P], ACT.Exp, scale=SCALE,
                                       bias=nmx[:, h:h + 1], accum_out=rs[:, h:h + 1]).then_inc(exp_done, 1)

                def values_out(n):
                    b, c = divmod(n, TT)
                    act.wait_ge(pv_done, n + 1)
                    if n == TT * (PAIRS - 1):
                        act.wait_ge(conv_p, CW)
                    for h in range(2):
                        r = slice(HD * h, HD * h + HD)
                        act.activation(attn[r, b, P * c:P * c + P], ps[r, 7, P * h:P * h + P],
                                       ACT.Identity, bias=b_in_t[r, 16 + b:17 + b]).then_inc(o_done, 1)

                def qk_high(b):
                    n = N_GLU + N_SEG * (b // 2) + 2 + 2 * (b % 2)
                    for i, dst in enumerate((qh, kh)):
                        col = 8 + 4 * i + b
                        for h in range(2):
                            if h:
                                act.wait_ge(blk_used, blk(n + i))
                            else:
                                act.wait_ge(qk_half, 2 * b + i + 1)
                            act.activation(dst[:, HALF * h:HALF * h + HALF], ps[:, 2 * i + h, :], ACT.Identity,
                                           bias=b_in_t[:, col:col + 1]).then_inc(qk_hi, 1)

                def transposed_hi(n):
                    for j in range(chunks(n % TT)):
                        bank, cols, w = chunk(n, j)
                        act.wait_ge(t_done, chunks_before(n) + j + 1)
                        if n and j == 0:
                            act.wait_ge(pv_done, n)
                        act.activation(pth[:, 2 * j:2 * j + w].rearrange("p t h q -> p (t h q)"), ps[:, bank, 0:cols],
                                       ACT.Copy).then_inc(pt_hi, 1)

                for s in range(2):
                    for t in range(TT):
                        i = TT * s + t
                        act.wait_ge(v_done, i + 1)
                        if s:
                            act.wait_ge(pv_done, 2 * TT)
                        act.activation(vh[:, t, :], ps[:, 4 + t % 4, 0:2 * P], ACT.Copy).then_inc(v_hi, 1)
                    s0, s1 = 2 * TT * s, 2 * TT * (s + 1)
                    for n in range(s0, s1 + 2):
                        new_pair = n < s1 and n % TT == 0
                        if n < s1 and not new_pair:
                            exponentials(n)
                        if n - 2 >= s0:
                            values_out(n - 2)
                        if new_pair:
                            qk_high(n // TT)
                        if s0 <= n - 1 < s1:
                            transposed_hi(n - 1)
                        if new_pair:
                            exponentials(n)
                act.wait_ge(o_done, 2 * TT * PAIRS)
                act.wait_ge(s_max, 2 * TT * PAIRS)
                for b in range(PAIRS):
                    act.activation(ah[:, b, :], attn[:, b, :], ACT.Copy).then_inc(a_hi, 1)
                for j in range(CB):
                    act.wait_ge(cent, j + 1)
                    if j >= 2:
                        act.wait_ge(sq_used, j - 1)
                    act.activation(sqr[:, j % 2, :], cv[:, j, :], ACT.Square).then_inc(sq_done, 1)
                act.wait_ge(sq_used, CB)
                act.activation(act_u[:, 0, :], psf[:, 6 * HALF:8 * HALF], ACT.Sqrt, bias=eps[:]).then_inc(std_done, 1)
                for j in range(CB):
                    act.wait_ge(nrm, j + 1)
                    if j >= 1:
                        act.wait_ge(uo_lo, j)
                    act.activation(act_u[:, 0, :], cv[:, j, :], ACT.Silu, scale=cpar[:, 1, j:j + 1],
                                   bias=cpar[:, 2, j:j + 1]).then_inc(silu_done, 1)
                    act.wait_ge(silu_done, j + 1)
                    act.activation(uoh[:, j, :], act_u[:, 0, :], ACT.Copy).then_inc(uo_hi, 1)
                for j in range(KC):
                    for h in range(2):
                        i = 2 * j + h
                        act.wait_ge(blk_used, blk(FIRST_OUT + 3 * j))
                        if i:
                            act.wait_ge(mix1, i)
                        act.activation(sgc[:], ps[:, h, :], ACT.Sigmoid, bias=b_in_t[:, 20 + j:21 + j]).then_inc(sig_gc, 1)
                        act.wait_ge(blk_used, blk(FIRST_OUT + 3 * j + 1))
                        if i:
                            act.wait_ge(mixed, i)
                        act.activation(sga[:], ps[:, 2 + h, :], ACT.Sigmoid, bias=b_in_t[:, 28 + j:29 + j]).then_inc(sig_ga, 1)
                act.wait_ge(mixed, 2 * KC)
                act.wait_ge(blk_used, blk(FIRST_WO - 1))
                for j in range(KC):
                    src = mixa if j < 4 else mixb
                    act.activation(mh[:, j, :], src[:, j % 4, :], ACT.Copy).then_inc(m_hi, 1)
                for t in range(TT):
                    act.wait_ge(xres_in[t], 16)
                    act.activation(x1[:, t, :], x1[:, t, :], ACT.Copy, scale=ALPHA).then_inc(xres_s, 1)
                for t in range(TT + 2):
                    if t < TT:
                        act.wait_ge(st_ok, t + 1)
                        act.activation(rstd[:, t:t + 1], mv[:, t, 1:2], ACT.Sqrt, bias=eps[:]).then_inc(sd_ok, 1)
                        act.wait_ge(nmr_ok, t + 1)
                        act.activation(x1[:, t, :], x1[:, t, :], ACT.Identity, scale=rstd[:, t:t + 1],
                                       bias=nmr[:, t:t + 1]).then_inc(ln_a, 1)
                    if t >= 2:
                        moe_parts["copy_x1t"](act, t - 2)
                moe_parts["scalar"](act)

            @block.vector
            def _(dve):
                for k in range(KC):
                    dve.wait_ge(x_hi, k + 1)
                    dve.tensor_tensor(xl[:, k, :], xraw[:, k, :], xh[:, k, :], ALU.subtract).then_inc(x_lo, 1)
                dve.wait_ge(init_p, 2)
                dve.wait_ge(par_in, 96)

                def glu(j):
                    dve.wait_ge(sig_ready, j + 1)
                    a = 4 * (j % 2)
                    dve.scalar_tensor_tensor(out=u[:, j, PAD:], in0=psf[:, HALF * a:HALF * a + SEQ],
                                             scalar=b_in_t[:, j:j + 1], in1=sig[:, j % 2, :],
                                             op0=ALU.add, op1=ALU.mult).then_inc(u_ready, 1)

                def conv_taps(j, k0, k1):
                    dve.wait_ge(u_ready, j + 1)
                    for k in range(k0, k1):
                        tap, w = u[:, j, k:k + SEQ], dw_t[:, j, k:k + 1]
                        if k == 0:
                            dve.tensor_scalar(cv[:, j, :], tap, w, cpar[:, 0, j:j + 1], ALU.mult, ALU.add).then_inc(conv_d, 1)
                        else:
                            dve.wait_ge(conv_d, CW * j + k)
                            dve.scalar_tensor_tensor(out=cv[:, j, :], in0=tap, scalar=w, in1=cv[:, j, :],
                                                     op0=ALU.mult, op1=ALU.add).then_inc(conv_d, 1)

                glu(0)
                conv_taps(0, 0, 14)
                glu(1)
                conv_taps(0, 14, CW)
                glu(2)
                conv_taps(1, 0, 14)
                glu(3)
                conv_taps(1, 14, CW)

                def maxima(n):
                    nt = tiles_of(n % TT)[1]
                    for h in range(2):
                        m = 2 * n + h
                        dve.wait_ge(s_done, m + 1)
                        if n > 1 and h == 0:
                            dve.wait_ge(t_done, chunks_before(n - 1))
                        dve.tensor_tensor_reduce(out=pr[n % 2][:, h, 0:nt * P], in0=psf[:, 2 * HALF * h:2 * HALF * h + nt * P],
                                                 in1=bias[:, h, BANDW - nt * P:BANDW], scale=1.0, scalar=-3e38,
                                                 op0=ALU.add, op1=ALU.max, accum_out=mx[:, h:h + 1]).then_inc(s_max, 1)
                        dve.wait_ge(s_max, m + 1)
                        dve.tensor_scalar(nmx[:, h:h + 1], mx[:, h:h + 1], -SCALE, None, ALU.mult).then_inc(s_nmx, 1)

                def probabilities(n):
                    nt = tiles_of(n % TT)[1]
                    for h in range(2):
                        m = 2 * n + h
                        dve.wait_ge(exp_done, m + 1)
                        dve.reciprocal(rinv[:, h:h + 1], rs[:, h:h + 1]).then_inc(p_inv, 1)
                        dve.wait_ge(p_inv, m + 1)
                        dve.tensor_scalar(pr[n % 2][:, h, 0:nt * P], pr[n % 2][:, h, 0:nt * P], rinv[:, h:h + 1], None,
                                          ALU.mult).then_inc(p_ready, 1)

                def transposed_lo(n):
                    for j in range(chunks(n % TT)):
                        bank, cols, w = chunk(n, j)
                        dve.wait_ge(pt_hi, chunks_before(n) + j + 1)
                        dve.tensor_tensor(ptl[:, 2 * j:2 * j + w].rearrange("p t h q -> p (t h q)"), ps[:, bank, 0:cols],
                                          pth[:, 2 * j:2 * j + w].rearrange("p t h q -> p (t h q)"),
                                          ALU.subtract).then_inc(pt_lo, 1)

                def qk_low(b):
                    conv_taps(2, 8 * b, min(8 * b + 8, CW))
                    dve.wait_ge(bias_in, 16 * (b + 1))
                    dve.tensor_scalar(bias[:], bias[:], 1.0 / SCALE, None, ALU.mult).then_inc(bias_ok, 1)
                    dve.wait_ge(bias_ok, 3 * b + 1)
                    dve.memset(bias[0:HD, :, BANDW - HD:BANDW], MASKED).then_inc(bias_ok, 1)
                    dve.memset(bias[HD:P, :, 0:HD], MASKED).then_inc(bias_ok, 1)
                    for i, (hi, lo) in enumerate(((qh, ql), (kh, kl))):
                        col = 8 + 4 * i + b
                        for h in range(2):
                            c = slice(HALF * h, HALF * h + HALF)
                            dve.wait_ge(qk_hi, 4 * b + 2 * i + h + 1)
                            dve.scalar_tensor_tensor(out=lo[:, c], in0=ps[:, 2 * i + h, :],
                                                     scalar=b_in_t[:, col:col + 1], in1=hi[:, c],
                                                     op0=ALU.add, op1=ALU.subtract).then_inc(qk_lo, 1)
                    dve.wait_ge(bias_ok, 3 * b + 3)

                for s in range(2):
                    for t in range(TT):
                        i = TT * s + t
                        dve.wait_ge(v_hi, i + 1)
                        dve.tensor_tensor(vl[:, t, :], ps[:, 4 + t % 4, 0:2 * P], vh[:, t, :], ALU.subtract).then_inc(v_lo, 1)
                    s0, s1 = 2 * TT * s, 2 * TT * (s + 1)
                    for n in range(s0, s1 + 2):
                        new_pair = n < s1 and n % TT == 0
                        if new_pair:
                            qk_low(n // TT)
                        elif n < s1:
                            maxima(n)
                            probabilities(n)
                        if s0 <= n - 1 < s1:
                            transposed_lo(n - 1)
                        if new_pair:
                            maxima(n)
                            probabilities(n)
                dve.wait_ge(t_done, chunks_before(TT * PAIRS))
                dve.memset(rstdc[:, 0:P], 1.0 / DC).then_inc(init_d, 1)
                for b in range(PAIRS):
                    dve.wait_ge(a_hi, b + 1)
                    if b == 0:
                        dve.wait_ge(pv_done, TT * PAIRS)
                    dve.tensor_tensor(al[:, b, :], attn[:, b, :], ah[:, b, :], ALU.subtract).then_inc(a_lo, 1)
                dve.wait_ge(mean_done, 1)
                for j in range(CB):
                    dve.tensor_tensor(cv[:, j, :], cv[:, j, :], psf[:, 4 * HALF:6 * HALF], ALU.subtract).then_inc(cent, 1)
                dve.wait_ge(std_done, 1)
                dve.reciprocal(rstdc[:], act_u[:, 0, :]).then_inc(rstd_ok, 1)
                dve.wait_ge(rstd_ok, 1)
                dve.wait_ge(cent, CB)
                for j in range(CB):
                    dve.tensor_tensor(cv[:, j, :], cv[:, j, :], rstdc[:], ALU.mult).then_inc(nrm, 1)
                for j in range(CB):
                    dve.wait_ge(uo_hi, j + 1)
                    dve.tensor_tensor(uol[:, j, :], act_u[:, 0, :], uoh[:, j, :], ALU.subtract).then_inc(uo_lo, 1)
                dve.wait_ge(a_lo, PAIRS)
                for j in range(KC):
                    dst = mixa if j < 4 else mixb
                    for h in range(2):
                        i = 2 * j + h
                        c = slice(HALF * h, HALF * h + HALF)
                        dve.wait_ge(sig_ga, i + 1)
                        dve.wait_ge(blk_used, blk(FIRST_OUT + 3 * j + 2))
                        dve.tensor_tensor(dst[:, j % 4, c], sgc[:], ps[:, 4 + h, :], ALU.mult).then_inc(mix1, 1)
                        dve.tensor_tensor(sga[:], sga[:], ps[:, 6 + h, :], ALU.mult).then_inc(mix2, 1)
                        dve.wait_ge(mix1, i + 1)
                        dve.wait_ge(mix2, i + 1)
                        dve.tensor_tensor(dst[:, j % 4, c], dst[:, j % 4, c], sga[:], ALU.add).then_inc(mixed, 1)
                for j in range(KC):
                    src = mixa if j < 4 else mixb
                    dve.wait_ge(m_hi, j + 1)
                    dve.tensor_tensor(ml[:, j, :], src[:, j % 4, :], mh[:, j, :], ALU.subtract).then_inc(m_lo, 1)

                def finish_row(t):
                    for h in range(2):
                        dve.bn_stats(st6[:, h, :], x1[:, t, HALF * h:HALF * h + HALF]).then_inc(var_ok, 1)
                    dve.wait_ge(var_ok, 2 * t + 2)
                    dve.bn_aggr(mv[:, t, :], st6[:]).then_inc(st_ok, 1)
                    dve.wait_ge(sd_ok, t + 1)
                    dve.reciprocal(rstd[:, t:t + 1], rstd[:, t:t + 1]).then_inc(rst_ok, 1)
                    dve.wait_ge(rst_ok, t + 1)
                    dve.scalar_tensor_tensor(out=nmr[:, t:t + 1], in0=mv[:, t, 0:1], scalar=-1.0, in1=rstd[:, t:t + 1],
                                             op0=ALU.mult, op1=ALU.mult).then_inc(nmr_ok, 1)

                def affine_row(t):
                    dve.wait_ge(ln_a, t + 1)
                    dve.tensor_tensor(x1[:, t, :], x1[:, t, :], g1_b[:], ALU.mult).then_inc(ln_g, 1)
                    dve.wait_ge(ln_g, t + 1)
                    dve.tensor_tensor(x1[:, t, :], x1[:, t, :], b1_b[:], ALU.add).then_inc(x1_ok, 1)

                for g in range(2):
                    for t in range(TT):
                        i = TT * g + t
                        c = slice(HALF * g, HALF * g + HALF)
                        dve.wait_ge(wo_done, i + 1)
                        if g == 0:
                            dve.wait_ge(xres_ok, t + 1)
                        dve.tensor_tensor(x1[:, t, c], x1[:, t, c], ps[:, i % 4, :], ALU.add).then_inc(wo_add, 1)
                        if g:
                            dve.wait_ge(wo_add, i + 1)
                            if t:
                                affine_row(t - 1)
                            finish_row(t)
                affine_row(TT - 1)
                moe_parts["vector"](dve)

    return nc


T_E, T_PAR, T_NEXT, T_SPLIT_DN, T_SPLIT_GU = range(5)
POOL_GU, POOL_DN = (2, 5, 7), (1, 3)


def moe(nc, sem, m):
    (x1, x1t, hot_a, hot_b, wr_t, ones, rt, big, gu_h, gu_l, gu_raw, dn_h, dn_l, dn_raw, xg, xgh, xgl, hb, hbh, hbl, ys,
     xf, y1, y2, g2_b, b2_b, cst, eps, st6, mv, rstd, nmr, wgt, slot_i, ids_i, id_now, tab, cum_i, ends_i, rows_i, br_b,
     ps, psf, ident) = (m[k] for k in (
         "x1 x1t hot_a hot_b wr_t ones rt big gu_h gu_l gu_raw dn_h dn_l dn_raw xg xgh xgl hb hbh hbl ys "
         "xf y1 y2 g2_b b2_b cst eps st6 mv rstd nmr wgt slot_i ids_i id_now tab cum_i ends_i rows_i br_b "
         "ps psf ident").split())
    wexp, ln2_g, ln2_b, out, x1_dram, y_dram = (m[k] for k in "wexp ln2_g ln2_b out x1_dram y_dram".split())
    wr_in, w_lo, wo_done, wo_add, x1_ok, x1_out, m_lo, ln_g = (
        m[k] for k in "wr_in w_lo wo_done wo_add x1_ok x1_out m_lo ln_g".split())
    gu_in = [sem(f"gu_in{j}") for j in range(4)]; dn_in = sem("dn_in")
    gu_hi = sem("gu_hi"); gu_lo_d = sem("gu_lo_d"); gu_lo_p = sem("gu_lo_p")
    dn_hi = sem("dn_hi"); dn_lo_d = sem("dn_lo_d"); dn_lo_p = sem("dn_lo_p")
    xt_r = sem("xt_r"); xt_rc = sem("xt_rc"); lg_done = sem("lg_done")
    rchain = sem("rchain"); r_exp = sem("r_exp"); r_exp_in = sem("r_exp_in")
    m_ready = sem("m_ready"); pos_done = sem("pos_done"); hot = sem("hot"); ids_done = sem("ids_done")
    tables = sem("tables"); ids_ok = sem("ids_ok")
    idc = sem("idc"); id_set = sem("id_set"); gath = sem("gath")
    tx_done = sem("tx_done"); tx_hi = sem("tx_hi"); tx_lo = sem("tx_lo"); gu_rows = sem("gu_rows")
    silu_ok = sem("silu_ok"); h_ok = sem("h_ok")
    th_done = sem("th_done"); th_hi = sem("th_hi"); th_lo = sem("th_lo"); dn_done = sem("dn_done")
    y_ok = sem("y_ok"); y_out = sem("y_out")
    ln2_in = sem("ln2_in"); xf_in = [sem(f"xf_in{i}") for i in range(TT)]; y_in = [sem(f"y_in{i}") for i in range(4)]
    f_a = sem("f_a"); f_b = sem("f_b"); f_st = sem("f_st"); f_mv = sem("f_mv"); f_sd = sem("f_sd")
    f_rs = sem("f_rs"); f_nm = sem("f_nm"); f_ln = sem("f_ln"); f_g = sem("f_g"); f_ok = sem("f_ok"); f_out = sem("f_out")

    def const(c, n):
        return cst[:, c - C_TRI:c - C_TRI + n]
    tri, iota, tok, thr = const(C_TRI, P), const(C_IOTA, P), const(C_TOK, TT), const(C_THR, 7)
    upto = const(C_UPTO, NE * NE).rearrange("p (a b) -> p a b", b=NE)
    before = const(C_BEFORE, TT * TT).rearrange("p (a b) -> p a b", b=TT)
    earlier = const(C_EARLIER, 16).rearrange("p (a b) -> p a b", b=4)
    by_te = lambda a: a.rearrange("p (t e) -> p t e", e=NE)
    by_g = lambda a: a.rearrange("p (g e) -> p g e", e=EPG)
    prob, t1, both, rk, pick0, pick1, pos, tot = (rt[:, i, :] for i in range(8))
    picks = (pick0, pick1)
    s8 = rt[:, 8, :].rearrange("p (i n) -> p i n", n=16)
    s32 = rt[:, 9, :].rearrange("p (i n) -> p i n", n=32)

    def load(eng, row, i):
        return eng.value_load(tab[0:1, row, bass.ds(i, 1)], min_val=0, max_val=NE - 1 if row == T_E else 1)

    def ends(eng):
        total = eng.value_load(cum_i[0:1, NE - 1:NE], min_val=NE, max_val=MAX_TILES)
        end2 = eng.value_load(ends_i[0:1, 0:1], min_val=NE - 2, max_val=MAX_TILES - 2)
        end1 = eng.value_load(ends_i[0:1, 1:2], min_val=NE - 1, max_val=MAX_TILES - 1)
        return total, end2, end1

    def when(eng, row, i, static, then):
        if static is not None:
            if static:
                then()
            return
        flag = load(eng, row, i)
        with eng.If(flag > 0):
            then()
        eng.nop()

    def split_gu(i):
        return True if isinstance(i, int) and i == 0 else None

    def split_dn(i):
        return {0: False, 1: True}.get(i) if isinstance(i, int) else None

    def load_gu(sp, e, par, rows_before=None):
        for j in range(4):
            if e:
                sp.wait_ge(gu_in[j], 16 * e)
            if rows_before is not None:
                sp.wait_ge(gu_rows, rows_before + (j + 1))
            sp.dma_start(gu_raw[:, par, 2 * j:2 * j + 2, :], wexp[e][:, 2 * j:2 * j + 2, :]).then_inc(gu_in[j], 16)

    def load_dn(sp, e):
        sp.dma_start(dn_raw[:], wexp[e][:, KC:WROWS, :]).then_inc(dn_in, 16)

    def sync_part(sp):
        sp.wait_ge(lg_done, TT)
        sp.wait_ge(x1_out, 16 * TT)
        load_dn(sp, 0)
        sp.wait_ge(ids_done, 2)
        sp.wait_ge(tables, 1)
        load_gu(sp, 1, 1)
        for e in range(1, NE):
            if e + 1 < NE:
                load_gu(sp, e + 1, (e + 1) % 2,
                        sp.value_load(rows_i[0:1, e - 1:e], min_val=0, max_val=4 * MAX_TILES - 4))
            sp.wait_ge(dn_lo_d, 2 * e)
            sp.wait_ge(dn_lo_p, 2 * e)
            load_dn(sp, e)
        total = sp.value_load(cum_i[0:1, NE - 1:NE], min_val=NE, max_val=MAX_TILES)
        sp.wait_ge(gu_rows, 4 * total)
        sp.dma_start(g2_b[:], ln2_g.partition_broadcast(P)).then_inc(ln2_in, 16)
        sp.dma_start(b2_b[:], ln2_b.partition_broadcast(P)).then_inc(ln2_in, 16)
        for t in range(TT):
            sp.dma_start(xf[:, t, :], x1_dram[P * t:P * t + P, :]).then_inc(xf_in[t], 16)
        for t in range(TT):
            sp.wait_ge(f_ok, t + 1)
            sp.dma_start(out[P * t:P * t + P, :], xf[:, t, :]).then_inc(f_out, 16)
        sp.wait_ge(f_out, 16 * TT)

    def dn_low(eng, e, rows, done):
        for k in rows:
            eng.wait_ge(dn_hi, e * 4 + (k + 1))
            eng.tensor_tensor(dn_l[:, k, :], dn_raw[:, k, :], dn_h[:, k, :], ALU.subtract).then_inc(done, 1)

    def gu_low(eng, e, par, rows, done):
        for k in rows:
            eng.wait_ge(gu_hi, e * 8 + (k + 1))
            eng.tensor_tensor(gu_l[:, par, k, :], gu_raw[:, par, k, :], gu_h[:, par, k, :], ALU.subtract).then_inc(done, 1)

    def pool_part(pool):
        gu_low(pool, 0, 0, POOL_GU, gu_lo_p)
        pool.wait_ge(ids_ok, 1)
        pool.wait_ge(x1_out, 16 * TT)
        pool.wait_ge(xt_r, TT)
        total, end2, end1 = ends(pool)

        def gather(i):
            pool.tensor_copy(id_now[:], ids_i[:, bass.ds(i, 1)]).then_inc(idc, 1)
            pool.wait_ge(idc, i + 1)
            pool.sem_inc(id_set, 1)
            pool.indirect_dma_start(out=xg[:], out_offset=None, in_=x1_dram,
                                    in_offset=bass.IndirectOffsetOnAxis(ap=id_now[:, 0:1], axis=0)).then_inc(gath, 16)

        def store(i):
            pool.wait_ge(y_ok, i + 1)
            pool.dma_start(y_dram[bass.ds(i * P, P), :], ys[:]).then_inc(y_out, 16)

        def down_rows(i, first=False):
            e = 0 if first else load(pool, T_E, i - 1)
            dn_low(pool, e, POOL_DN, dn_lo_p)

        def gate_rows(i, rows, first=False):
            e, par = (0, 1) if first else (load(pool, T_E, i), load(pool, T_NEXT, i))
            gu_low(pool, e + 1, par if first else bass.ds(par, 1), rows, gu_lo_p)

        def step(i, has_store=True):
            pool.wait_ge(tx_done, i + 1)
            gather(i + 1)
            first = isinstance(i, int) and i == 0
            when(pool, T_SPLIT_DN, i, split_dn(i), lambda: down_rows(i, isinstance(i, int) and i == 1))
            if has_store:
                store(i - 2)
            when(pool, T_SPLIT_GU, i, split_gu(i), lambda: gate_rows(i, POOL_GU, first))

        gather(0)
        step(0, False)
        step(1, False)
        step(2)
        with pool.Fori(3, MAX_TILES) as i:
            with pool.If(i < total):
                step(i)
            pool.nop()
        when(pool, T_SPLIT_DN, total, None, lambda: down_rows(total))
        store(end2)
        store(end1)
        pool.wait_ge(y_out, end1 * 16 + 16)
        pool.sem_inc(id_set, 1)
        pool.wait_ge(gath, total * 16 + 16)
        pool.sem_inc(id_set, 1)
        for t in range(TT + 1):
            if t < TT:
                if t >= 4:
                    pool.wait_ge(f_b, 2 * (t - 3))
                for c, y in enumerate((y1, y2)):
                    pool.indirect_dma_start(out=y[:, t % 4, :], out_offset=None, in_=y_dram,
                                            in_offset=bass.IndirectOffsetOnAxis(ap=slot_i[:, c, t:t + 1], axis=0)
                                            ).then_inc(y_in[t % 4], 16)
            if t:
                if t == 1:
                    pool.wait_ge(ln2_in, 32)
                pool.wait_ge(f_g, t)
                pool.tensor_tensor(xf[:, t - 1, :], xf[:, t - 1, :], b2_b[:], ALU.add).then_inc(f_ok, 1)

    def transpose_x1(pe, t):
        pe.wait_ge(x1_ok, t + 1)
        if t:
            pe.wait_ge(xt_rc, t)
        for k in range(KC):
            last = pe.transpose(psf[:, 4 * HALF + P * k:4 * HALF + P * k + P], x1[:, t, P * k:P * k + P], ident)
        last.then_inc(xt_r, 1)

    def logits(pe, t):
        pe.wait_ge(xt_rc, t + 1)
        if t == 0:
            pe.wait_ge(wr_in, 48)
        for k in range(KC):
            last = pe.matmul(ps[:, 6, NE * t:NE * t + NE], x1t[:, k, :], wr_t[:, k, :], start=k == 0, stop=k == KC - 1)
        last.then_inc(lg_done, 1)

    def mm3(pe, o, a_h, a_l, b_h, b_l, first, last):
        pe.matmul(o, a_h, b_h, start=first, stop=False)
        pe.matmul(o, a_h, b_l, start=False, stop=False)
        return pe.matmul(o, a_l, b_h, start=False, stop=last)

    def tensor_part(pe):
        pe.wait_ge(m_ready, 1)
        pe.matmul(ps[:, 3, 0:P], tri, both, start=True, stop=True)
        pe.matmul(ps[:, 4, 0:P], ones[:], both, start=True, stop=True).then_inc(pos_done, 1)
        for c in range(2):
            pe.wait_ge(hot, c + 1)
            for t in range(TT):
                last = pe.matmul(ps[:, 5, 0:TAB], hot_a[:, c, t, :], hot_b[:, c, t, :], start=c == 0 and t == 0,
                                 stop=c == 1 and t == TT - 1)
            last.then_inc(ids_done, 1)
        pe.wait_ge(tables, 1)
        total, end2, end1 = ends(pe)

        def transpose_x(i):
            pe.wait_ge(gath, i * 16 + 16)
            if not (isinstance(i, int) and i == 0):
                pe.wait_ge(tx_lo, i)
            for k in range(KC):
                last = pe.transpose(psf[:, P * k:P * k + P], xg[:, P * k:P * k + P], ident)
            last.then_inc(tx_done, 1)

        def up(i):
            e, par = load(pe, T_E, i), load(pe, T_PAR, i)
            pe.wait_ge(tx_lo, i + 1)
            for k in range(KC):
                if k in POOL_GU:
                    pe.wait_ge(gu_lo_p, e * len(POOL_GU) + (POOL_GU.index(k) + 1))
                else:
                    pe.wait_ge(gu_lo_d, e * (KC - len(POOL_GU)) + (k - sum(r < k for r in POOL_GU) + 1))
                for h in range(2):
                    c = slice(HALF * h, HALF * h + HALF)
                    last = mm3(pe, ps[:, 2 + h, :], xgh[:, P * k:P * k + P], xgl[:, P * k:P * k + P],
                               gu_h[:, bass.ds(par, 1), k, c], gu_l[:, bass.ds(par, 1), k, c], k == 0, k == KC - 1)
                if k % 2:
                    last.then_inc(gu_rows, 1)

        def transpose_h(i):
            pe.wait_ge(h_ok, i + 1)
            if not (isinstance(i, int) and i == 0):
                pe.wait_ge(th_lo, i)
            for k in range(FC):
                last = pe.transpose(ps[:, 4, P * k:P * k + P], hb[:, P * k:P * k + P], ident)
            last.then_inc(th_done, 1)

        def down(i):
            e = load(pe, T_E, i)
            pe.wait_ge(th_lo, i + 1)
            pe.wait_ge(dn_lo_d, e * 2 + 2)
            pe.wait_ge(dn_lo_p, e * 2 + 2)
            if not (isinstance(i, int) and i == 0):
                pe.wait_ge(y_ok, i)
            for k in range(FC):
                for h in range(2):
                    c = slice(HALF * h, HALF * h + HALF)
                    last = mm3(pe, ps[:, 6 + h, :], hbh[:, P * k:P * k + P], hbl[:, P * k:P * k + P],
                               dn_h[:, k, c], dn_l[:, k, c], k == 0, k == FC - 1)
            last.then_inc(dn_done, 1)

        transpose_x(0)
        up(0)
        transpose_x(1)
        transpose_h(0)
        up(1)
        transpose_x(2)
        down(0)
        transpose_h(1)
        up(2)
        with pe.Fori(3, MAX_TILES) as i:
            with pe.If(i < total):
                transpose_x(i)
                down(i - 2)
                transpose_h(i - 1)
                up(i)
            pe.nop()
        down(end2)
        transpose_h(end1)
        down(end1)

    def copy_x1t(act, t):
        act.wait_ge(xt_r, t + 1)
        if t:
            act.wait_ge(lg_done, t)
        act.activation(x1t[:, :, :].rearrange("p k c -> p (k c)"), psf[:, 4 * HALF:6 * HALF], ACT.Copy).then_inc(xt_rc, 1)

    def scalar_part(act):
        act.wait_ge(r_exp_in, 1)
        act.activation(prob, prob, ACT.Exp).then_inc(r_exp, 1)

        def gu_high(e, par, rows):
            for k in rows:
                act.wait_ge(gu_in[k // 2], e * 16 + 16)
                act.activation(gu_h[:, par, k, :], gu_raw[:, par, k, :], ACT.Copy).then_inc(gu_hi, 1)

        act.wait_ge(wo_done, 2 * TT)
        gu_high(0, 0, range(KC))
        act.wait_ge(tables, 1)
        total, end2, end1 = ends(act)

        def x_t(i):
            act.wait_ge(tx_done, i + 1)
            if not (isinstance(i, int) and i == 0):
                act.wait_ge(gu_rows, 4 * i)
            act.activation(xgh[:], psf[:, 0:SEQ], ACT.Copy).then_inc(tx_hi, 1)

        def down_rows(i, first=False, before=None):
            e = 0 if first else load(act, T_E, i - 1)
            act.wait_ge(dn_in, e * 16 + 16)
            if not first:
                act.wait_ge(dn_done, i - 1 if before is None else before)
            for k in range(FC):
                act.activation(dn_h[:, k, :], dn_raw[:, k, :], ACT.Copy).then_inc(dn_hi, 1)

        def h_t(i):
            act.wait_ge(th_done, i + 1)
            if not (isinstance(i, int) and i == 0):
                act.wait_ge(dn_done, i)
            act.activation(hbh[:], ps[:, 4, :], ACT.Copy).then_inc(th_hi, 1)

        def gate_rows(i, rows, first=False):
            e, par = (0, 1) if first else (load(act, T_E, i), load(act, T_NEXT, i))
            gu_high(e + 1, par if first else bass.ds(par, 1), rows)

        def silu(i):
            act.wait_ge(gu_rows, 4 * i + 4)
            if not (isinstance(i, int) and i == 0):
                act.wait_ge(th_done, i)
            act.activation(hb[:], ps[:, 2, :], ACT.Silu).then_inc(silu_ok, 1)

        def step(i):
            first = isinstance(i, int) and i == 0
            x_t(i)
            when(act, T_SPLIT_DN, i, split_dn(i), lambda: down_rows(i, isinstance(i, int) and i == 1))
            if not first:
                h_t(i - 1)
            when(act, T_SPLIT_GU, i, split_gu(i), lambda: gate_rows(i, range(KC), first))
            silu(i)

        for i in range(3):
            step(i)
        with act.Fori(3, MAX_TILES) as i:
            with act.If(i < total):
                step(i)
            act.nop()
        when(act, T_SPLIT_DN, total, None, lambda: down_rows(total, before=end1))
        h_t(end1)
        for t in range(TT + 1):
            if t < TT:
                act.wait_ge(xf_in[t], 16)
                act.activation(xf[:, t, :], xf[:, t, :], ACT.Copy, scale=ALPHA).then_inc(f_a, 1)
            if t:
                act.wait_ge(f_mv, t)
                act.activation(rstd[:, t - 1:t], mv[:, t - 1, 1:2], ACT.Sqrt, bias=eps[:]).then_inc(f_sd, 1)
                act.wait_ge(f_nm, t)
                act.activation(xf[:, t - 1, :], xf[:, t - 1, :], ACT.Identity, scale=rstd[:, t - 1:t],
                               bias=nmr[:, t - 1:t]).then_inc(f_ln, 1)

    def vector_part(dve):
        count = [0]
        V = nc.vector

        def link(ins):
            count[0] += 1
            ins.then_inc(rchain, 1)
            dve.wait_ge(rchain, count[0])

        def over(a, n, m):
            return a.unsqueeze(2).broadcast_to([P, n, m])

        def rank(dst, src, n, a4, b4):
            v = by_g(src)
            me, other = v.unsqueeze(3).broadcast_to([P, n, EPG, EPG]), v.unsqueeze(2).broadcast_to([P, n, EPG, EPG])
            a = a4.rearrange("p (g a b) -> p g a b", a=EPG, b=EPG)
            b = b4.rearrange("p (g a b) -> p g a b", a=EPG, b=EPG)
            link(V.tensor_tensor(a, other, me, ALU.is_gt))
            link(V.tensor_tensor(b, other, me, ALU.is_equal))
            link(V.tensor_tensor(b, b, earlier.unsqueeze(1).broadcast_to([P, n, EPG, EPG]), ALU.mult))
            link(V.tensor_tensor(a, a, b, ALU.add))
            link(V.reduce_sum(by_g(dst), a, AX.X))

        dve.wait_ge(m_lo, KC)
        link(V.memset(ones[:], 1.0))
        dve.wait_ge(lg_done, TT)
        p = prob
        link(V.tensor_tensor(by_te(p), by_te(ps[:, 6, 0:P]), br_b[:, :].unsqueeze(1).broadcast_to([P, TT, NE]), ALU.add))
        top = s8[:, 0, 0:TT]
        link(V.reduce_max(top, by_te(p), AX.X))
        V.tensor_tensor(by_te(p), by_te(p), over(top, TT, NE), ALU.subtract).then_inc(r_exp_in, 1)
        dve.wait_ge(r_exp, 1)
        link(V.reduce_sum(top, by_te(p), AX.X))
        link(V.reciprocal(top, top))
        link(V.tensor_tensor(by_te(p), by_te(p), over(top, TT, NE), ALU.mult))
        rank(rk, p, 32, big[:, 0:512], big[:, 512:1024])
        link(V.scalar_tensor_tensor(out=t1, in0=rk, scalar=1.5, in1=p, op0=ALU.is_lt, op1=ALU.mult))
        gs, gr = s32[:, 0, :], s32[:, 1, :]
        link(V.reduce_sum(gs, by_g(t1), AX.X))
        rank(gr, gs, 8, big[:, 0:128], big[:, 128:256])
        link(V.tensor_scalar(gr, gr, 0.5, None, ALU.is_lt))
        for c, pick in enumerate(picks):
            link(V.scalar_tensor_tensor(out=by_g(pick), in0=by_g(rk), scalar=float(c), in1=over(gr, 32, EPG),
                                        op0=ALU.is_equal, op1=ALU.mult))
        V.tensor_tensor(both, pick0, pick1, ALU.add).then_inc(m_ready, 1)
        for c, pick in enumerate(picks):
            link(V.tensor_tensor(t1, p, pick, ALU.mult))
            link(V.reduce_sum(wgt[:, c, :], by_te(t1), AX.X))
        link(V.tensor_tensor(top, wgt[:, 0, :], wgt[:, 1, :], ALU.add))
        link(V.reciprocal(top, top))
        link(V.tensor_tensor(wgt[:, :, :], wgt[:, :, :], top.unsqueeze(1).broadcast_to([P, 2, TT]), ALU.mult))
        dve.wait_ge(pos_done, 1)
        link(V.tensor_copy(tot, ps[:, 4, 0:P]))
        tot_et = tot.rearrange("p (t e) -> p e t", e=NE)
        n_e, nt, cum, base = (s8[:, i, :] for i in range(1, 5))
        link(V.reduce_sum(n_e, tot_et, AX.X))
        cmp7 = big[:, 0:NE * 7].rearrange("p (e k) -> p e k", k=7)
        link(V.tensor_tensor(cmp7, over(n_e, NE, 7), thr.unsqueeze(1).broadcast_to([P, NE, 7]), ALU.is_gt))
        link(V.reduce_sum(nt, cmp7, AX.X))
        link(V.tensor_scalar(nt, nt, 1.0, None, ALU.add))
        ee = big[:, 0:NE * NE].rearrange("p (a b) -> p a b", b=NE)
        link(V.tensor_tensor(ee, upto, nt.unsqueeze(1).broadcast_to([P, NE, NE]), ALU.mult))
        link(V.reduce_sum(cum, ee, AX.X))
        link(V.tensor_tensor(base, cum, nt, ALU.subtract))
        before_e = before.unsqueeze(2).broadcast_to([P, TT, NE, TT])
        tet = big[:, :].rearrange("p (t e u) -> p t e u", e=NE, u=TT)
        link(V.tensor_tensor(tet, tot_et.unsqueeze(1).broadcast_to([P, TT, NE, TT]), before_e, ALU.mult))
        link(V.reduce_sum(by_te(pos), tet, AX.X))
        link(V.tensor_tensor(pos, pos, ps[:, 3, 0:P], ALU.add))
        for c, pick in enumerate(picks):
            hi, lo, q = s8[:, 5, 0:TT], s8[:, 6, 0:TT], s8[:, 7, 0:TT]
            link(V.tensor_tensor(t1, pick, pos, ALU.mult))
            link(V.reduce_sum(lo, by_te(t1), AX.X))
            link(V.tensor_tensor(by_te(t1), by_te(pick), base.unsqueeze(1).broadcast_to([P, TT, NE]), ALU.mult))
            link(V.reduce_sum(hi, by_te(t1), AX.X))
            c8 = big[:, 0:TT * 7].rearrange("p (t k) -> p t k", k=7)
            link(V.tensor_tensor(c8, over(lo, TT, 7), thr.unsqueeze(1).broadcast_to([P, TT, 7]), ALU.is_ge))
            link(V.reduce_sum(q, c8, AX.X))
            link(V.tensor_tensor(hi, hi, q, ALU.add))
            link(V.scalar_tensor_tensor(out=lo, in0=q, scalar=-float(P), in1=lo, op0=ALU.mult, op1=ALU.add))
            link(V.scalar_tensor_tensor(out=slot_i[:, c, :], in0=hi, scalar=float(P), in1=lo, op0=ALU.mult, op1=ALU.add))
            if c == 0:
                dve.wait_ge(w_lo, N_BLOCKS)
            link(V.tensor_tensor(hot_b[:, c], iota[:, 0:TAB].unsqueeze(1).broadcast_to([P, TT, TAB]), over(hi, TT, TAB),
                                 ALU.is_equal))
            link(V.tensor_tensor(hot_b[:, c], hot_b[:, c], over(tok, TT, TAB), ALU.mult))
            V.tensor_tensor(hot_a[:, c], iota.unsqueeze(1).broadcast_to([P, TT, P]), over(lo, TT, P),
                            ALU.is_equal).then_inc(hot, 1)
            dve.wait_ge(hot, c + 1)
        et, fst, fl = s32[:, 0, :], s32[:, 1, :], s32[:, 2, :]
        ie = big[:, 0:TAB * NE].rearrange("p (i e) -> p i e", e=NE)
        link(V.tensor_tensor(ie, over(iota[:, 0:TAB], TAB, NE), cum.unsqueeze(1).broadcast_to([P, TAB, NE]), ALU.is_ge))
        link(V.reduce_sum(et, ie, AX.X))
        link(V.tensor_scalar(et, et, float(NE - 1), None, ALU.min))
        link(V.tensor_copy(tab[:, T_E, :], et))
        link(V.tensor_scalar(tab[:, T_PAR, :], tab[:, T_E, :], 1, None, ALU.bitwise_and))
        link(V.tensor_scalar(tab[:, T_NEXT, :], tab[:, T_PAR, :], -1.0, 1.0, ALU.mult, ALU.add))
        link(V.memset(fst[:, 0:1], 1.0))
        link(V.tensor_tensor(fst[:, 1:TAB], et[:, 1:TAB], et[:, 0:TAB - 1], ALU.is_gt))
        link(V.memset(tab[:, T_SPLIT_DN, 0:1], 0))
        link(V.tensor_copy(tab[:, T_SPLIT_DN, 1:TAB], fst[:, 0:TAB - 1]))
        link(V.scalar_tensor_tensor(out=tab[:, T_SPLIT_GU, :], in0=et, scalar=NE - 1.5, in1=fst, op0=ALU.is_lt, op1=ALU.mult))
        link(V.tensor_scalar(rows_i[:], cum, -1.0, 4.0, ALU.add, ALU.mult))
        link(V.tensor_scalar(ends_i[:, 0:1], cum[:, NE - 1:NE], -2.0, None, ALU.add))
        link(V.tensor_scalar(ends_i[:, 1:2], cum[:, NE - 1:NE], -1.0, None, ALU.add))
        V.tensor_copy(cum_i[:], cum).then_inc(tables, 1)
        dve.wait_ge(ids_done, 2)
        V.tensor_copy(ids_i[:], ps[:, 5, 0:TAB]).then_inc(ids_ok, 1)
        mine_gu = [k for k in range(KC) if k not in POOL_GU]
        mine_dn = [k for k in range(FC) if k not in POOL_DN]
        gu_low(dve, 0, 0, mine_gu, gu_lo_d)
        dve.wait_ge(tables, 1)
        total, end2, end1 = ends(dve)

        def x_t(i):
            dve.wait_ge(tx_hi, i + 1)
            dve.tensor_tensor(xgl[:], psf[:, 0:SEQ], xgh[:], ALU.subtract).then_inc(tx_lo, 1)

        def down_rows(i, first=False):
            e = 0 if first else load(dve, T_E, i - 1)
            dn_low(dve, e, mine_dn, dn_lo_d)

        def h_t(i):
            dve.wait_ge(th_hi, i + 1)
            dve.tensor_tensor(hbl[:], ps[:, 4, :], hbh[:], ALU.subtract).then_inc(th_lo, 1)

        def gate_rows(i, rows, first=False):
            e, par = (0, 1) if first else (load(dve, T_E, i), load(dve, T_NEXT, i))
            gu_low(dve, e + 1, par if first else bass.ds(par, 1), rows, gu_lo_d)

        def gate(i):
            dve.wait_ge(silu_ok, i + 1)
            dve.tensor_tensor(hb[:], hb[:], ps[:, 3, :], ALU.mult).then_inc(h_ok, 1)

        def y(i):
            dve.wait_ge(dn_done, i + 1)
            if not (isinstance(i, int) and i == 0):
                dve.wait_ge(y_out, i * 16)
            dve.tensor_copy(ys[:], psf[:, 6 * HALF:8 * HALF]).then_inc(y_ok, 1)

        def step(i):
            static = isinstance(i, int)
            x_t(i)
            when(dve, T_SPLIT_DN, i, split_dn(i), lambda: down_rows(i, static and i == 1))
            if not (static and i < 2):
                y(i - 2)
            if not (static and i == 0):
                h_t(i - 1)
            when(dve, T_SPLIT_GU, i, split_gu(i), lambda: gate_rows(i, mine_gu, static and i == 0))
            gate(i)

        for i in range(3):
            step(i)
        with dve.Fori(3, MAX_TILES) as i:
            with dve.If(i < total):
                step(i)
            dve.nop()
        when(dve, T_SPLIT_DN, total, None, lambda: down_rows(total))
        y(end2)
        h_t(end1)
        y(end1)

        def combine(t):
            dve.wait_ge(f_a, t + 1)
            dve.wait_ge(y_in[t % 4], 32 * (t // 4 + 1))
            for c, yy in enumerate((y1, y2)):
                dve.scalar_tensor_tensor(out=xf[:, t, :], in0=yy[:, t % 4, :], scalar=wgt[:, c, t:t + 1],
                                         in1=xf[:, t, :], op0=ALU.mult, op1=ALU.add).then_inc(f_b, 1)
                dve.wait_ge(f_b, 2 * t + c + 1)
            for h in range(2):
                dve.bn_stats(st6[:, h, :], xf[:, t, HALF * h:HALF * h + HALF]).then_inc(f_st, 1)
            dve.wait_ge(f_st, 2 * t + 2)
            dve.bn_aggr(mv[:, t, :], st6[:]).then_inc(f_mv, 1)

        def normalise(t):
            dve.wait_ge(f_sd, t + 1)
            dve.reciprocal(rstd[:, t:t + 1], rstd[:, t:t + 1]).then_inc(f_rs, 1)
            dve.wait_ge(f_rs, t + 1)
            dve.scalar_tensor_tensor(out=nmr[:, t:t + 1], in0=mv[:, t, 0:1], scalar=-1.0, in1=rstd[:, t:t + 1],
                                     op0=ALU.mult, op1=ALU.mult).then_inc(f_nm, 1)

        def scale_row(t):
            dve.wait_ge(f_ln, t + 1)
            dve.tensor_tensor(xf[:, t, :], xf[:, t, :], g2_b[:], ALU.mult).then_inc(f_g, 1)

        dve.wait_ge(ln2_in, 32)
        for t in range(TT + 2):
            if t >= 1 and t <= TT:
                normalise(t - 1)
            if t < TT:
                combine(t)
            if t >= 1 and t <= TT:
                scale_row(t - 1)

    return {"load_expert_0": lambda sp: load_gu(sp, 0, 0), "sync": sync_part, "gpsimd": pool_part, "tensor": tensor_part,
            "transpose_x1": transpose_x1, "logits": logits, "scalar": scalar_part, "copy_x1t": copy_x1t,
            "vector": vector_part}


def laid_out(x, w_in, b_in, w_dw, b_dw, ln_conv_g, ln_conv_b, w_conv_out, rel_bias, w_attn_out, w_o, b_o,
             ln1_g, ln1_b, w_router, b_router, w_gate_up, w_down, ln2_g, ln2_b):
    con = np.ascontiguousarray
    x = np.asarray(x)[0]
    w_all = np.concatenate([np.asarray(w_in)[0], np.concatenate([np.asarray(w_conv_out)[0], np.asarray(w_attn_out)[0]], 0),
                            np.asarray(w_o)[0]], 1)
    blocks = w_all.reshape(KC, P, -1, P).transpose(2, 1, 0, 3)[block_columns()]
    rel = np.clip(np.arange(P)[:, None] - np.arange(BANDW)[None, :] + 512, -256, 256) + 256
    band = np.asarray(rel_bias)[0][:, rel]
    wexp = np.concatenate([np.asarray(w_gate_up)[0].reshape(NE, KC, P, 2 * FF), np.asarray(w_down)[0].reshape(NE, FC, P, D)], 1)
    col = lambda a, n: con(np.asarray(a)[0].reshape(n, P).T)
    return {
        "xT": con(x.T.reshape(KC, P, SEQ)), "x": con(x), "wblk": con(blocks), "b_in": col(b_in, 36),
        "dw": con(np.asarray(w_dw)[0].T.reshape(CB, P, CW).transpose(1, 0, 2)),
        "dwb": col(b_dw, CB), "lncg": col(ln_conv_g, CB), "lncb": col(ln_conv_b, CB),
        "relb": con(band.reshape(PAIRS, 2, P, BANDW).transpose(0, 2, 1, 3)),
        "b_o": con(np.asarray(b_o)[0]), "ln1_g": con(np.asarray(ln1_g)[0]), "ln1_b": con(np.asarray(ln1_b)[0]),
        "w_r": con(np.asarray(w_router).reshape(KC, P, NE).transpose(1, 0, 2)), "b_r": con(np.asarray(b_router)),
        "wexp": con(wexp.transpose(0, 2, 1, 3)),
        "ln2_g": con(np.asarray(ln2_g)[0]), "ln2_b": con(np.asarray(ln2_b)[0]), "consts": constants(),
    }


def kernel(**inputs):
    import concourse.bacc as bacc
    from concourse.bass_utils import run_bass_kernel_spmd

    nc = bacc.Bacc("TRN2", target_bir_lowering=False, num_devices=1)
    arrays = {f"in_{k}": v for k, v in laid_out(**inputs).items()}
    args = [nc.dram_tensor(n, a.shape, F32, kind="ExternalInput").ap() for n, a in arrays.items()]
    out = nc.dram_tensor("out_rows", (SEQ, D), F32, kind="ExternalOutput").ap()
    encoder_layer(nc, *args, out)
    r = run_bass_kernel_spmd(nc, [arrays], core_ids=[0])
    return r.results[0]["out_rows"].reshape(1, SEQ, D)
```

```python
import numpy as np
import concourse.bass as bass
from concourse import mybir
from contextlib import ExitStack

F32 = mybir.dt.float32
F32R = mybir.dt.float32r
I32 = mybir.dt.int32
U32 = mybir.dt.uint32
ALU = mybir.AluOpType
ACT = mybir.ActivationFunctionType
AX = mybir.AxisListType

P = 128
D = 1024
SEQ = 1024
KC = D // P
TT = SEQ // P
HALF = 512
DC = 512
CB = DC // P
CW = 31
PAD = CW - 1
HEADS, HD = 8, 64
PAIRS = HEADS // 2
BANDT = 5
BANDW = BANDT * P
SCALE = HD ** -0.5
NE, NGRP, EPG = 16, 4, 4
FF = 512
FC = FF // P
MAX_TILES = NE + (2 * SEQ - 1) // P
TAB = 32
WROWS = KC + FC
ALPHA = 2.0 ** 0.25
EPS = 1e-5
MASKED = -1e30
RING, RAWS = 4, 2

N_GLU = 2 * CB
N_SEG = 2 + 2 * 2
N_ATT = 2 * N_SEG
FIRST_OUT = N_GLU + N_ATT
FIRST_WO = FIRST_OUT + 3 * KC
N_BLOCKS = FIRST_WO + KC


def block_columns():
    a, g, q, k, v, gc, ga = (np.cumsum([0, 4, 4, 4, 4, 4, 8])).tolist()
    o, wo = 36, 44
    cols = []
    for j in range(CB):
        cols += [a + j, g + j]
    for s in range(2):
        cols += [v + 2 * s, v + 2 * s + 1, q + 2 * s, k + 2 * s, q + 2 * s + 1, k + 2 * s + 1]
    for j in range(KC):
        cols += [gc + j, ga + j, o + j]
    cols += [wo + j for j in range(KC)]
    return cols


C_ID, C_TRI, C_IOTA, C_TOK, C_THR, C_UPTO, C_BEFORE, C_EARLIER = 0, 128, 256, 384, 392, 400, 656, 720
C_WIDTH = 736
C_REST = C_WIDTH - C_TRI


def constants():
    c = np.zeros((P, C_WIDTH), np.float32)
    c[:, C_ID:C_ID + P] = np.eye(P)
    c[:, C_TRI:C_TRI + P] = np.triu(np.ones((P, P)), 1)
    c[:, C_IOTA:C_IOTA + P] = np.arange(P)[None, :]
    c[:, C_TOK:C_TOK + TT] = np.arange(P)[:, None] + P * np.arange(TT)[None, :]
    c[:, C_THR:C_THR + 7] = P * np.arange(1, 8)[None, :]
    c[:, C_UPTO:C_UPTO + NE * NE] = np.tril(np.ones((NE, NE))).ravel()
    c[:, C_BEFORE:C_BEFORE + TT * TT] = np.tril(np.ones((TT, TT)), -1).ravel()
    c[:, C_EARLIER:C_EARLIER + 16] = np.tril(np.ones((4, 4)), -1).ravel()
    return c


def encoder_layer(nc, xT, x, wblk, b_in, dw, dwb, lncg, lncb, relb, b_o, ln1_g, ln1_b,
                  w_r, b_r, wexp, ln2_g, ln2_b, consts, out):
    x1_dram = nc.dram_tensor("x1_rows", (SEQ, D), F32, kind="Internal").ap()
    y_dram = nc.dram_tensor("y_slots", (MAX_TILES * P, D), F32, kind="Internal").ap()
    ctx = ExitStack()
    with ctx:
        ARENA = 207 * 1024 + 512
        arena = ctx.enter_context(nc.sbuf_tensor("arena", [P, ARENA], mybir.dt.uint8))
        base = nc.sbuf_base - ARENA
        KB = 1024

        def at(name, shape, dt, kb):
            size = int(np.prod(shape[1:])) * 4
            assert kb * KB + size <= ARENA, name
            return nc.alloc_sbuf_tensor_at(name, shape, dt, offset=base + int(kb * KB))

        xh = at("xh", [P, KC, SEQ], F32R, 0)
        xl = at("xl", [P, KC, SEQ], F32R, 32)
        wh = at("wh", [P, RING, KC, P], F32R, 64)
        wl = at("wl", [P, RING, KC, P], F32R, 80)
        raw = at("raw", [P, RAWS, KC, P], F32, 96)
        attn = at("attn", [P, PAIRS, SEQ], F32, 104)
        u = at("u", [P, CB, PAD + SEQ], F32, 120)
        cv = at("cv", [P, CB, SEQ], F32, 136.5)
        qh = at("qh", [P, SEQ], F32R, 152.5)
        ql = at("ql", [P, SEQ], F32R, 156.5)
        kh = at("kh", [P, SEQ], F32R, 160.5)
        kl = at("kl", [P, SEQ], F32R, 164.5)
        vh = at("vh", [P, TT, 2 * P], F32R, 168.5)
        vl = at("vl", [P, TT, 2 * P], F32R, 176.5)
        bias = at("bias", [P, 2, BANDW], F32, 184.5)
        pr = (at("pr0", [P, 2, BANDW], F32, 189.5), at("pr1", [P, 2, BANDW], F32, 120))
        pth = at("pth", [P, BANDT, 2, P], F32R, 194.5)
        ptl = at("ptl", [P, BANDT, 2, P], F32R, 199.5)
        tapped = at("tapped", [P, SEQ], F32, 116)
        xraw = at("xraw", [P, KC, SEQ], F32, 152.5)
        sig = at("sig", [P, 2, SEQ], F32, 189.5)
        ah = at("ah", [P, PAIRS, SEQ], F32R, 152.5)
        al = at("al", [P, PAIRS, SEQ], F32R, 168.5)
        uoh = at("uoh", [P, CB, SEQ], F32R, 120)
        uol = at("uol", [P, CB, SEQ], F32R, 136.5)
        mixa = at("mixa", [P, 4, SEQ], F32, 104)
        mixb = at("mixb", [P, 4, SEQ], F32, 184.5)
        sqr = at("sqr", [P, 2, SEQ], F32, 184.5)
        rstdc = at("rstdc", [P, SEQ], F32, 192.5)
        act_u = (at("act_u0", [P, SEQ], F32, 196.5), at("act_u1", [P, SEQ], F32, 184.5))
        sgc = at("sgc", [P, HALF], F32, 200.5)
        sga = at("sga", [P, HALF], F32, 202.5)
        mh = at("mh", [P, KC, SEQ], F32R, 0)
        ml = at("ml", [P, KC, SEQ], F32R, 32)
        x1 = at("x1", [P, TT, D], F32, 170)
        bo_b = at("bo_b", [P, D], F32, 152.5)
        g1_b = at("g1_b", [P, D], F32, 156.5)
        b1_b = at("b1_b", [P, D], F32, 160.5)
        wh2 = at("wh2", [P, 4, KC, P], F32R, 120)
        wl2 = at("wl2", [P, 4, KC, P], F32R, 136)
        x1t = at("x1t", [P, KC, P], F32, 164.5)
        cst = at("cst", [P, C_REST], F32, 152.5)
        wr_t = at("wr_t", [P, KC, NE], F32, 155)
        ones = at("ones", [P, P], F32, 155.5)
        hot_a = at("hot_a", [P, 2, TT, P], F32, 128)
        hot_b = at("hot_b", [P, 2, TT, TAB], F32, 136)
        rt = at("rt", [P, 10, P], F32, 138)
        big = at("big", [P, TT * NE * TT], F32, 143)
        gu_h = at("gu_h", [P, 2, KC, 1024], F32R, 0)
        gu_l = at("gu_l", [P, 2, KC, 1024], F32R, 64)
        gu_raw = at("gu_raw", [P, 2, KC, 1024], F32, 64)
        dn_h = at("dn_h", [P, FC, 1024], F32R, 128)
        dn_l = at("dn_l", [P, FC, 1024], F32R, 144)
        dn_raw = at("dn_raw", [P, FC, 1024], F32, 160)
        xg = at("xg", [P, D], F32, 176)
        xgh = at("xgh", [P, D], F32R, 180)
        xgl = at("xgl", [P, D], F32R, 184)
        hb = at("hb", [P, FF], F32, 188)
        hbh = at("hbh", [P, FF], F32R, 190)
        hbl = at("hbl", [P, FF], F32R, 192)
        ys = at("ys", [P, D], F32, 194)
        xf = at("xf", [P, TT, D], F32, 0)
        y1 = at("y1", [P, TT, D], F32, 32)
        y2 = at("y2", [P, TT, D], F32, 64)
        g2_b = at("g2_b", [P, D], F32, 96)
        b2_b = at("b2_b", [P, D], F32, 100)
        diag = at("diag", [P, 2, TT, P], F32, 104)
        small = 204.5

        def tiny(name, shape, dt=F32):
            nonlocal small
            t = at(name, shape, dt, small)
            small += -(-int(np.prod(shape[1:])) * 4 // 32) * 32 / KB
            return t
        b_in_t = tiny("b_in_t", [P, 36])
        cpar = tiny("cpar", [P, 3, CB])
        dw_t = tiny("dw_t", [P, CB, CW])
        eps = tiny("eps", [P, 1])
        mx = tiny("mx", [P, 2])
        nmx = tiny("nmx", [P, 2])
        rs = tiny("rs", [P, 2])
        rinv = tiny("rinv", [P, 2])
        st6 = tiny("st6", [P, 2, 6])
        mv = tiny("mv", [P, TT, 2])
        rstd = tiny("rstd", [P, TT])
        nmr = tiny("nmr", [P, TT])
        wgt = tiny("wgt", [P, 2, TT])
        slot_i = tiny("slot_i", [P, 2, TT], I32)
        ids_i = tiny("ids_i", [P, TAB], I32)
        id_now = tiny("id_now", [P, 1], I32)
        tab = tiny("tab", [P, 5, TAB], I32)
        cum_i = tiny("cum_i", [P, NE], I32)
        ends_i = tiny("ends_i", [P, 2], I32)
        rows_i = tiny("rows_i", [P, NE], I32)
        br_b = tiny("br_b", [P, NE])
        ident_t = tiny("ident_t", [P, P])
        ident = ident_t[:]

        ps = ctx.enter_context(nc.psum_tensor("ps", [P, 8, HALF], F32))
        psf = ps[:, :, :].rearrange("p b n -> p (b n)")

        def sem(name):
            return ctx.enter_context(nc.semaphore(name))

        x_in = [sem(f"x_in{k}") for k in range(KC)]
        par_in = sem("par_in")
        raw_in = [sem(f"raw_in{r}") for r in range(RAWS)]
        bias_in = sem("bias_in")
        x_hi = sem("x_hi"); x_lo = sem("x_lo")
        w_hi = sem("w_hi"); w_lo = sem("w_lo")
        blk_used = sem("blk_used")
        sig_ready = sem("sig_ready"); u_ready = sem("u_ready")
        conv_d = sem("conv_d"); conv_p = sem("conv_p"); init_d = sem("init_d"); init_p = sem("init_p")
        v_done = sem("v_done"); v_hi = sem("v_hi"); v_lo = sem("v_lo")
        qk_half = sem("qk_half"); qk_hi = sem("qk_hi"); qk_lo = sem("qk_lo")
        bias_ok = sem("bias_ok")
        s_done = sem("s_done"); s_max = sem("s_max"); s_nmx = sem("s_nmx"); exp_done = sem("exp_done")
        p_inv = sem("p_inv"); p_ready0 = sem("p_ready0"); p_ready1 = sem("p_ready1")
        t_done = sem("t_done"); pt_hi = sem("pt_hi"); pt_lo = sem("pt_lo")
        pv_done = sem("pv_done"); o_done = sem("o_done")
        a_hi = sem("a_hi"); a_lo = sem("a_lo")
        mean_done = sem("mean_done"); cent = sem("cent"); sq_done = sem("sq_done"); sq_used = sem("sq_used")
        var_done = sem("var_done"); std_done = sem("std_done"); rstd_ok = sem("rstd_ok")
        nrm = sem("nrm"); silu_done = sem("silu_done"); uo_hi = sem("uo_hi"); uo_lo = sem("uo_lo")
        o_half = sem("o_half"); sig_gc = sem("sig_gc"); sig_ga = sem("sig_ga")
        mix1 = sem("mix1"); mix2 = sem("mix2"); mixed = sem("mixed")
        m_hi = sem("m_hi"); m_lo = sem("m_lo")
        xres_in = [sem(f"xres_in{i}") for i in range(TT)]
        lnp_in = sem("lnp_in"); xres_ok = sem("xres_ok"); tap_p = sem("tap_p"); zero_ok = sem("zero_ok"); zero_out = sem("zero_out")
        wo_done = sem("wo_done"); wo_add = sem("wo_add")
        st_ok = sem("st_ok"); var_ok = sem("var_ok"); sd_ok = sem("sd_ok"); rst_ok = sem("rst_ok")
        ln_g = sem("ln_g"); x1_ok = sem("x1_ok")
        x1_out = sem("x1_out"); wr_in = sem("wr_in")

        def blk(n):
            return n + 1 - sum(2 for s in range(2) if n > N_GLU + N_SEG * s)

        def wait_used(eng, n):
            s, r = divmod(n - N_GLU, N_SEG)
            if 0 <= s < 2 and r < 2:
                eng.wait_ge(v_done, TT * (s + 1))
            elif n >= FIRST_WO:
                eng.wait_ge(wo_done, TT)
            else:
                eng.wait_ge(blk_used, blk(n))

        def tiles_of(c):
            return max(0, c - BANDT + 1), min(c, BANDT - 1) + 1

        def chunks(c):
            return (tiles_of(c)[1] + 1) // 2

        def chunks_before(n):
            return sum(chunks(i % TT) for i in range(n))

        def chunk(n, j):
            w = min(2, tiles_of(n % TT)[1] - 2 * j)
            return 4 + j, 2 * P * w, w

        moe_parts = moe(nc, sem, locals())

        with nc.Block() as block:
            @block.sync
            def _(sp):
                def load_block(n):
                    if n >= RAWS:
                        sp.wait_ge(w_lo, n - RAWS + 1)
                    sp.dma_start(raw[:, n % RAWS], wblk[n]).then_inc(raw_in[n % RAWS], 16)

                def load_bias(b):
                    if b:
                        sp.wait_ge(s_max, 2 * TT * b)
                    sp.dma_start(bias[:], relb[b]).then_inc(bias_in, 16)

                load_block(0)
                for k in range(KC):
                    sp.dma_start(xraw[:, k, :], xT[k]).then_inc(x_in[k], 16)
                    if k == 3:
                        load_block(1)
                sp.dma_start(b_in_t[:], b_in).then_inc(par_in, 16)
                sp.dma_start(ident, consts[:, C_ID:C_ID + P]).then_inc(par_in, 16)
                for i, src in enumerate((dwb, lncg, lncb)):
                    sp.dma_start(cpar[:, i, :], src).then_inc(par_in, 16)
                sp.dma_start(dw_t[:], dw).then_inc(par_in, 16)
                load_bias(0)
                after = {N_GLU + 6: 1, N_GLU + N_SEG + 4: 2, FIRST_OUT: 3}
                for n in range(RAWS, FIRST_WO + 4 + RAWS):
                    load_block(n)
                    if n in after:
                        load_bias(after[n])
                    for i in range(NE + 2 * (n - RAWS), min(NE + 2 * (n - RAWS) + 2, MAX_TILES)):
                        if i == NE:
                            sp.wait_ge(zero_ok, 1)
                        sp.dma_start(y_dram[P * i:P * i + P, :], tapped[:]).then_inc(zero_out, 16)
                sp.wait_ge(blk_used, blk(FIRST_WO - 1))
                for dst, src in ((bo_b, b_o), (g1_b, ln1_g), (b1_b, ln1_b)):
                    sp.dma_start(dst[:], src.partition_broadcast(P)).then_inc(lnp_in, 16)
                for t in range(TT):
                    if t == 3:
                        sp.wait_ge(m_lo, KC)
                    sp.dma_start(x1[:, t, :], x[P * t:P * t + P, :]).then_inc(xres_in[t], 16)
                for n in range(FIRST_WO + 4 + RAWS, N_BLOCKS):
                    load_block(n)
                sp.wait_ge(xres_ok, TT)
                sp.dma_start(cst[:], consts[:, C_TRI:C_WIDTH]).then_inc(wr_in, 16)
                sp.dma_start(wr_t[:], w_r).then_inc(wr_in, 16)
                sp.dma_start(br_b[:], b_r.partition_broadcast(P)).then_inc(wr_in, 16)
                sp.wait_ge(wo_done, TT)
                moe_parts["load_expert_0"](sp)
                for t in range(TT):
                    sp.wait_ge(x1_ok, t + 1)
                    sp.dma_start(x1_dram[P * t:P * t + P, :], x1[:, t, :]).then_inc(x1_out, 16)
                moe_parts["sync"](sp)

            @block.gpsimd
            def _(pool):
                pool.memset(tapped[:], 0.0).then_inc(zero_ok, 1)
                pool.memset(eps[:], EPS).then_inc(init_p, 1)
                pool.memset(u[:, :, 0:PAD], 0.0).then_inc(init_p, 1)

                def split_block(n):
                    own = n - FIRST_WO - RING
                    hi, lo = (wh2[:, own], wl2[:, own]) if own >= 0 else (wh[:, n % RING], wl[:, n % RING])
                    pool.wait_ge(raw_in[n % RAWS], 16 * (n // RAWS + 1))
                    if own >= 0:
                        wait_used(pool, FIRST_WO - 1)
                    elif n >= RING:
                        wait_used(pool, n - RING)
                    pool.tensor_scalar(hi, raw[:, n % RAWS], 1.0, 1.0, ALU.mult, ALU.mult).then_inc(w_hi, 1)
                    pool.wait_ge(w_hi, n + 1)
                    pool.tensor_tensor(lo, raw[:, n % RAWS], hi, ALU.subtract).then_inc(w_lo, 1)

                def conv_taps(j, k0, k1):
                    pool.wait_ge(u_ready, j + 1)
                    for k in range(k0, k1):
                        tap, w = u[:, j, k:k + SEQ], dw_t[:, j, k:k + 1]
                        if k == 0:
                            pool.tensor_scalar(cv[:, j, :], tap, w, cpar[:, 0, j:j + 1], ALU.mult, ALU.add).then_inc(conv_p, 1)
                        else:
                            if k > 1:
                                pool.wait_ge(conv_p, k)
                            pool.tensor_scalar(tapped[:], tap, w, 1.0, ALU.mult, ALU.mult).then_inc(tap_p, 1)
                            pool.wait_ge(tap_p, k)
                            pool.wait_ge(conv_p, k)
                            pool.tensor_tensor(cv[:, j, :], cv[:, j, :], tapped[:], ALU.add).then_inc(conv_p, 1)

                for n in range(N_GLU + 4):
                    split_block(n)
                pool.wait_ge(par_in, 96)
                pool.wait_ge(zero_out, 16 * (MAX_TILES - NE))
                for i in range(3):
                    conv_taps(CB - 1, 10 * i, min(10 * i + 10 + i // 2, CW))
                    split_block(N_GLU + 4 + 2 * i)
                    split_block(N_GLU + 5 + 2 * i)
                for n in range(N_GLU + 10, FIRST_WO + 4):
                    split_block(n)
                for n in range(FIRST_WO + 4, N_BLOCKS):
                    split_block(n)
                moe_parts["gpsimd"](pool)

            @block.tensor
            def _(pe):
                def mm3(o, a_h, a_l, b_h, b_l, first, last):
                    pe.matmul(o, a_h, b_h, start=first, stop=False)
                    pe.matmul(o, a_h, b_l, start=False, stop=False)
                    return pe.matmul(o, a_l, b_h, start=False, stop=last)

                def weights_left(n, bank):
                    pe.wait_ge(w_lo, n + 1)
                    s = n % RING
                    for k in range(KC):
                        if n == 0:
                            pe.wait_ge(x_lo, k + 1)
                        for h in range(2):
                            c = slice(HALF * h, HALF * h + HALF)
                            last = mm3(ps[:, bank + h, :], wh[:, s, k], wl[:, s, k], xh[:, k, c], xl[:, k, c],
                                       k == 0, k == KC - 1)
                    return last

                for j in range(CB):
                    if j >= 2:
                        pe.wait_ge(u_ready, j - 1)
                    bank = 4 * (j % 2)
                    weights_left(2 * j, bank).then_inc(blk_used, 1)
                    weights_left(2 * j + 1, bank + 2).then_inc(blk_used, 1)

                def project_v(s):
                    n = N_GLU + N_SEG * s
                    pe.wait_ge(w_lo, n + 2)
                    r = n % RING
                    for t in range(TT):
                        i = TT * s + t
                        if i >= 4:
                            pe.wait_ge(v_lo, i - 3)
                        else:
                            pe.wait_ge(u_ready, CB)
                        if s and t == 0:
                            pe.wait_ge(o_done, 4 * TT)
                        c = slice(P * t, P * t + P)
                        for k in range(KC):
                            last = mm3(ps[:, 4 + t % 4, 0:2 * P], xh[:, k, c], xl[:, k, c],
                                       wh[:, r:r + 2, k, :], wl[:, r:r + 2, k, :], k == 0, k == KC - 1)
                        last.then_inc(v_done, 1)

                def project_qk(b):
                    n = N_GLU + N_SEG * (b // 2) + 2 + 2 * (b % 2)
                    if b:
                        pe.wait_ge(s_max, 2 * TT * b)
                    for i in range(2):
                        pe.wait_ge(w_lo, n + i + 1)
                        r = (n + i) % RING
                        for h in range(2):
                            c = slice(HALF * h, HALF * h + HALF)
                            for k in range(KC):
                                last = mm3(ps[:, 2 * i + h, :], wh[:, r, k], wl[:, r, k], xh[:, k, c], xl[:, k, c],
                                           k == 0, k == KC - 1)
                            last.then_inc(blk_used if h else qk_half, 1)

                def scores(n, h):
                    b, c = divmod(n, TT)
                    kt, nt = tiles_of(c)
                    if n:
                        pe.wait_ge(s_max, 2 * n - 1 + h)
                    r = slice(HD * h, HD * h + HD)
                    q = slice(P * c, P * c + P)
                    for k0 in range(0, nt * P, HALF):
                        w = min(HALF, nt * P - k0)
                        kk = slice(P * kt + k0, P * kt + k0 + w)
                        last = mm3(ps[:, 2 * h + k0 // HALF, 0:w], qh[r, q], ql[r, q], kh[r, kk], kl[r, kk], True, True)
                    last.then_inc(s_done, 1)

                def transpose_probs(n):
                    pe.wait_ge(p_ready0, n + 1)
                    pe.wait_ge(p_ready1, n + 1)
                    pe.wait_ge(pt_lo, chunks_before(n))
                    for j in range(chunks(n % TT)):
                        bank, _, w = chunk(n, j)
                        for t in range(w):
                            for h in range(2):
                                k = P * (2 * j + t)
                                last = pe.transpose(ps[:, bank, P * (2 * t + h):P * (2 * t + h) + P],
                                                    pr[n % 2][:, h, k:k + P], ident)
                        last.then_inc(t_done, 1)

                def weigh_values(n):
                    b, c = divmod(n, TT)
                    kt, nt = tiles_of(c)
                    if n:
                        pe.wait_ge(o_done, 2 * n)
                    v = slice(P * (b % 2), P * (b % 2) + P)
                    for t in range(nt):
                        pe.wait_ge(pt_lo, chunks_before(n) + t // 2 + 1)
                        last = mm3(ps[:, 7, 0:2 * P], vh[:, kt + t, v], vl[:, kt + t, v],
                                   pth[:, t], ptl[:, t], t == 0, t == nt - 1)
                    last.then_inc(pv_done, 1)

                def channel_mean(bank, src, j):
                    for h in range(2):
                        last = pe.matmul(ps[:, bank + h, :], ones_c, src[:, HALF * h:HALF * h + HALF],
                                         start=j == 0, stop=j == CB - 1)
                    return last

                ones_c = rstdc[:, 0:P]
                for s in range(2):
                    project_v(s)
                    s0, s1 = 2 * TT * s, 2 * TT * (s + 1)
                    for n in range(s0, s1 + 2):
                        new_pair = n < s1 and n % TT == 0
                        if n < s1 and not new_pair:
                            for h in range(2):
                                scores(n, h)
                        if n == s0 + 2:
                            pe.wait_ge(v_lo, TT * (s + 1))
                        if n - 2 >= s0:
                            weigh_values(n - 2)
                        if new_pair:
                            project_qk(n // TT)
                        if s0 <= n - 1 < s1:
                            transpose_probs(n - 1)
                        if n == TT * PAIRS:
                            pe.wait_ge(s_max, 2 * TT * PAIRS)
                            pe.wait_ge(init_d, 1)
                            pe.wait_ge(conv_d, 3 * CW)
                            pe.wait_ge(conv_p, CW)
                            for j in range(CB):
                                last = channel_mean(2, cv[:, j, :], j)
                            last.then_inc(mean_done, 1)
                        if new_pair:
                            pe.wait_ge(qk_lo, 4 * (n // TT + 1))
                            for h in range(2):
                                scores(n, h)

                weights_left(FIRST_OUT, 0).then_inc(blk_used, 1)
                pe.wait_ge(o_done, 2 * TT * PAIRS)
                for j in range(CB):
                    pe.wait_ge(sq_done, j + 1)
                    channel_mean(6, sqr[:, j % 2, :], j).then_inc(sq_used, 1)

                for j in range(KC):
                    n = FIRST_OUT + 3 * j
                    if j:
                        pe.wait_ge(sig_gc, 2 * j)
                        weights_left(n, 0).then_inc(blk_used, 1)
                        pe.wait_ge(sig_ga, 2 * j)
                    else:
                        pe.wait_ge(cent, CB)
                    weights_left(n + 1, 2).then_inc(blk_used, 1)
                    s = (n + 2) % RING
                    pe.wait_ge(w_lo, n + 3)
                    if j == 0:
                        pe.wait_ge(std_done, 1)
                        pe.wait_ge(a_lo, PAIRS)
                        pe.wait_ge(pt_lo, chunks_before(TT * PAIRS))
                    for h in range(2):
                        if j:
                            pe.wait_ge(mix2, 2 * j - 1 + h)
                        for bank, hi, lo, k0 in ((6, ah, al, CB), (4, uoh, uol, 0)):
                            c = slice(HALF * h, HALF * h + HALF)
                            for k in range(CB):
                                if j + h == 0 and bank == 4:
                                    pe.wait_ge(uo_lo, k + 1)
                                last = mm3(ps[:, bank + h, :], wh[:, s, k0 + k], wl[:, s, k0 + k],
                                           hi[:, k, c], lo[:, k, c], k == 0, k == CB - 1)
                        last.then_inc(blk_used if h else o_half, 1)

                pe.wait_ge(mixed, 2 * KC)
                for g in range(2):
                    pe.wait_ge(w_lo, FIRST_WO + 4 * g + 4)
                    b_h, b_l = ((wh, wl), (wh2, wl2))[g]
                    for t in range(TT + 2 * g):
                        i = TT * g + t
                        if t < TT:
                            if i >= 4:
                                pe.wait_ge(wo_add, i - 3)
                            c = slice(P * t, P * t + P)
                            for k in range(KC):
                                if i == 0:
                                    pe.wait_ge(m_lo, k + 1)
                                last = mm3(ps[:, i % 4, :], mh[:, k, c], ml[:, k, c],
                                           b_h[:, :, k, :], b_l[:, :, k, :], k == 0, k == KC - 1)
                            last.then_inc(wo_done, 1)
                        if g and t >= 2:
                            moe_parts["logits"](pe, t - 2)
                        if g and 1 <= t < TT + 1:
                            moe_parts["transpose_x1"](pe, t - 1)
                moe_parts["tensor"](pe)

            @block.scalar
            def _(act):
                for k in range(KC):
                    act.wait_ge(x_in[k], 16)
                    act.activation(xh[:, k, :], xraw[:, k, :], ACT.Copy).then_inc(x_hi, 1)
                act.wait_ge(par_in, 96)
                for j in range(CB):
                    act.wait_ge(blk_used, blk(2 * j + 1))
                    if j >= 2:
                        act.wait_ge(u_ready, j - 1)
                    g = 4 * (j % 2) + 2
                    act.activation(sig[:, j % 2, :], psf[:, HALF * g:HALF * g + SEQ], ACT.Sigmoid,
                                   bias=b_in_t[:, CB + j:CB + j + 1]).then_inc(sig_ready, 1)

                def exponentials(n):
                    nt = tiles_of(n % TT)[1]
                    for h in range(2):
                        act.wait_ge(s_nmx, 2 * n + h + 1)
                        act.activation(pr[n % 2][:, h, 0:nt * P], pr[n % 2][:, h, 0:nt * P], ACT.Exp, scale=SCALE,
                                       bias=nmx[:, h:h + 1], accum_out=rs[:, h:h + 1]).then_inc(exp_done, 1)

                def probabilities(n):
                    nt = tiles_of(n % TT)[1]
                    act.wait_ge(p_inv, 2 * n + 2)
                    act.activation(pr[n % 2][:, 1, 0:nt * P], pr[n % 2][:, 1, 0:nt * P], ACT.Copy,
                                   scale=rinv[:, 1:2]).then_inc(p_ready1, 1)

                def values_out(n):
                    b, c = divmod(n, TT)
                    act.wait_ge(pv_done, n + 1)
                    if n == TT * (PAIRS - 1):
                        act.wait_ge(conv_p, CW)
                    for h in range(2):
                        r = slice(HD * h, HD * h + HD)
                        act.activation(attn[r, b, P * c:P * c + P], ps[r, 7, P * h:P * h + P],
                                       ACT.Identity, bias=b_in_t[r, 16 + b:17 + b]).then_inc(o_done, 1)

                def qk_high(b):
                    n = N_GLU + N_SEG * (b // 2) + 2 + 2 * (b % 2)
                    for i, dst in enumerate((qh, kh)):
                        col = 8 + 4 * i + b
                        for h in range(2):
                            if h:
                                act.wait_ge(blk_used, blk(n + i))
                            else:
                                act.wait_ge(qk_half, 2 * b + i + 1)
                            act.activation(dst[:, HALF * h:HALF * h + HALF], ps[:, 2 * i + h, :], ACT.Identity,
                                           bias=b_in_t[:, col:col + 1]).then_inc(qk_hi, 1)

                def transposed_hi(n):
                    for j in range(chunks(n % TT)):
                        bank, cols, w = chunk(n, j)
                        act.wait_ge(t_done, chunks_before(n) + j + 1)
                        if n and j == 0:
                            act.wait_ge(pv_done, n)
                        act.activation(pth[:, 2 * j:2 * j + w].rearrange("p t h q -> p (t h q)"), ps[:, bank, 0:cols],
                                       ACT.Copy).then_inc(pt_hi, 1)

                for s in range(2):
                    for t in range(TT):
                        i = TT * s + t
                        act.wait_ge(v_done, i + 1)
                        if s:
                            act.wait_ge(pv_done, 2 * TT)
                        act.activation(vh[:, t, :], ps[:, 4 + t % 4, 0:2 * P], ACT.Copy).then_inc(v_hi, 1)
                    s0, s1 = 2 * TT * s, 2 * TT * (s + 1)
                    for n in range(s0, s1 + 2):
                        new_pair = n < s1 and n % TT == 0
                        if n < s1 and not new_pair:
                            exponentials(n)
                        if new_pair:
                            if n - 2 >= s0:
                                values_out(n - 2)
                            qk_high(n // TT)
                        if s0 <= n - 1 < s1:
                            transposed_hi(n - 1)
                        if new_pair:
                            exponentials(n)
                        if n < s1:
                            probabilities(n)
                        if n - 2 >= s0 and not new_pair:
                            values_out(n - 2)
                act.wait_ge(t_done, chunks_before(TT * PAIRS))
                for j in range(CB):
                    act.wait_ge(cent, j + 1)
                    if j >= 2:
                        act.wait_ge(sq_used, j - 1)
                    act.activation(sqr[:, j % 2, :], cv[:, j, :], ACT.Square).then_inc(sq_done, 1)
                act.wait_ge(o_done, 2 * TT * PAIRS)
                act.wait_ge(s_max, 2 * TT * PAIRS)
                for b in range(PAIRS):
                    act.activation(ah[:, b, :], attn[:, b, :], ACT.Copy).then_inc(a_hi, 1)
                act.wait_ge(sq_used, CB)
                act.activation(act_u[0][:], psf[:, 6 * HALF:8 * HALF], ACT.Sqrt, bias=eps[:]).then_inc(std_done, 1)
                act.wait_ge(rstd_ok, 1)
                for j in range(CB + 1):
                    if j < CB:
                        act.wait_ge(nrm, j + 1)
                        if j >= 2:
                            act.wait_ge(uo_lo, j - 1)
                        act.activation(act_u[j % 2][:], cv[:, j, :], ACT.Silu, scale=cpar[:, 1, j:j + 1],
                                       bias=cpar[:, 2, j:j + 1]).then_inc(silu_done, 1)
                    if j:
                        act.wait_ge(silu_done, j)
                        act.activation(uoh[:, j - 1, :], act_u[(j - 1) % 2][:], ACT.Copy).then_inc(uo_hi, 1)
                for j in range(KC):
                    for h in range(2):
                        i = 2 * j + h
                        act.wait_ge(blk_used, blk(FIRST_OUT + 3 * j))
                        if i:
                            act.wait_ge(mix1, i)
                        act.activation(sgc[:], ps[:, h, :], ACT.Sigmoid, bias=b_in_t[:, 20 + j:21 + j]).then_inc(sig_gc, 1)
                        act.wait_ge(blk_used, blk(FIRST_OUT + 3 * j + 1))
                        if i:
                            act.wait_ge(mixed, i)
                        act.activation(sga[:], ps[:, 2 + h, :], ACT.Sigmoid, bias=b_in_t[:, 28 + j:29 + j]).then_inc(sig_ga, 1)
                act.wait_ge(mixed, 2 * KC)
                act.wait_ge(blk_used, blk(FIRST_WO - 1))
                for j in range(KC):
                    src = mixa if j < 4 else mixb
                    act.activation(mh[:, j, :], src[:, j % 4, :], ACT.Copy).then_inc(m_hi, 1)
                for t in range(TT + 1):
                    if t < TT:
                        act.wait_ge(st_ok, t + 1)
                        act.activation(rstd[:, t:t + 1], mv[:, t, 1:2], ACT.Sqrt, bias=eps[:]).then_inc(sd_ok, 1)
                    if t >= 1:
                        moe_parts["copy_x1t"](act, t - 1)
                moe_parts["scalar"](act)

            @block.vector
            def _(dve):
                for k in range(KC):
                    dve.wait_ge(x_hi, k + 1)
                    dve.tensor_tensor(xl[:, k, :], xraw[:, k, :], xh[:, k, :], ALU.subtract).then_inc(x_lo, 1)
                dve.wait_ge(init_p, 2)
                dve.wait_ge(par_in, 96)

                def glu(j):
                    dve.wait_ge(sig_ready, j + 1)
                    a = 4 * (j % 2)
                    dve.scalar_tensor_tensor(out=u[:, j, PAD:], in0=psf[:, HALF * a:HALF * a + SEQ],
                                             scalar=b_in_t[:, j:j + 1], in1=sig[:, j % 2, :],
                                             op0=ALU.add, op1=ALU.mult).then_inc(u_ready, 1)

                def conv_taps(j, k0, k1):
                    dve.wait_ge(u_ready, j + 1)
                    for k in range(k0, k1):
                        tap, w = u[:, j, k:k + SEQ], dw_t[:, j, k:k + 1]
                        if k == 0:
                            dve.tensor_scalar(cv[:, j, :], tap, w, cpar[:, 0, j:j + 1], ALU.mult, ALU.add).then_inc(conv_d, 1)
                        else:
                            dve.wait_ge(conv_d, CW * j + k)
                            dve.scalar_tensor_tensor(out=cv[:, j, :], in0=tap, scalar=w, in1=cv[:, j, :],
                                                     op0=ALU.mult, op1=ALU.add).then_inc(conv_d, 1)

                glu(0)
                conv_taps(0, 0, 14)
                glu(1)
                conv_taps(0, 14, CW)
                glu(2)
                conv_taps(1, 0, 8)
                glu(3)

                def maxima(n):
                    nt = tiles_of(n % TT)[1]
                    for h in range(2):
                        m = 2 * n + h
                        dve.wait_ge(s_done, m + 1)
                        if n > 1 and h == 0:
                            dve.wait_ge(t_done, chunks_before(n - 1))
                        dve.tensor_tensor_reduce(out=pr[n % 2][:, h, 0:nt * P], in0=psf[:, 2 * HALF * h:2 * HALF * h + nt * P],
                                                 in1=bias[:, h, BANDW - nt * P:BANDW], scale=1.0, scalar=-3e38,
                                                 op0=ALU.add, op1=ALU.max, accum_out=mx[:, h:h + 1]).then_inc(s_max, 1)
                        dve.wait_ge(s_max, m + 1)
                        dve.tensor_scalar(nmx[:, h:h + 1], mx[:, h:h + 1], -SCALE, None, ALU.mult).then_inc(s_nmx, 1)

                def probabilities(n):
                    nt = tiles_of(n % TT)[1]
                    for h in range(2):
                        m = 2 * n + h
                        dve.wait_ge(exp_done, m + 1)
                        dve.reciprocal(rinv[:, h:h + 1], rs[:, h:h + 1]).then_inc(p_inv, 1)
                        if h == 0:
                            dve.wait_ge(p_inv, m + 1)
                            dve.tensor_scalar(pr[n % 2][:, h, 0:nt * P], pr[n % 2][:, h, 0:nt * P], rinv[:, h:h + 1], None,
                                              ALU.mult).then_inc(p_ready0, 1)

                def transposed_lo(n):
                    for j in range(chunks(n % TT)):
                        bank, cols, w = chunk(n, j)
                        dve.wait_ge(pt_hi, chunks_before(n) + j + 1)
                        dve.tensor_tensor(ptl[:, 2 * j:2 * j + w].rearrange("p t h q -> p (t h q)"), ps[:, bank, 0:cols],
                                          pth[:, 2 * j:2 * j + w].rearrange("p t h q -> p (t h q)"),
                                          ALU.subtract).then_inc(pt_lo, 1)

                def qk_low(b):
                    if b == 0:
                        conv_taps(1, 24, CW)
                    conv_taps(2, 9 * b - 5 if b else 0, 9 * b + 4)
                    dve.wait_ge(bias_in, 16 * (b + 1))
                    dve.tensor_scalar(bias[:], bias[:], 1.0 / SCALE, None, ALU.mult).then_inc(bias_ok, 1)
                    dve.wait_ge(bias_ok, 3 * b + 1)
                    dve.memset(bias[0:HD, :, BANDW - HD:BANDW], MASKED).then_inc(bias_ok, 1)
                    dve.memset(bias[HD:P, :, 0:HD], MASKED).then_inc(bias_ok, 1)
                    for i, (hi, lo) in enumerate(((qh, ql), (kh, kl))):
                        col = 8 + 4 * i + b
                        for h in range(2):
                            c = slice(HALF * h, HALF * h + HALF)
                            dve.wait_ge(qk_hi, 4 * b + 2 * i + h + 1)
                            dve.scalar_tensor_tensor(out=lo[:, c], in0=ps[:, 2 * i + h, :],
                                                     scalar=b_in_t[:, col:col + 1], in1=hi[:, c],
                                                     op0=ALU.add, op1=ALU.subtract).then_inc(qk_lo, 1)
                    dve.wait_ge(bias_ok, 3 * b + 3)

                for s in range(2):
                    for t in range(TT):
                        i = TT * s + t
                        dve.wait_ge(v_hi, i + 1)
                        dve.tensor_tensor(vl[:, t, :], ps[:, 4 + t % 4, 0:2 * P], vh[:, t, :], ALU.subtract).then_inc(v_lo, 1)
                        if s == 0:
                            conv_taps(1, 8 + 2 * t, 10 + 2 * t)
                    s0, s1 = 2 * TT * s, 2 * TT * (s + 1)
                    for n in range(s0, s1 + 2):
                        new_pair = n < s1 and n % TT == 0
                        if new_pair:
                            qk_low(n // TT)
                        elif n < s1:
                            maxima(n)
                            probabilities(n)
                        if n == TT * PAIRS:
                            dve.wait_ge(t_done, chunks_before(TT * PAIRS - 1))
                            dve.memset(rstdc[:, 0:P], 1.0 / DC).then_inc(init_d, 1)
                        if s0 <= n - 1 < s1:
                            transposed_lo(n - 1)
                        if new_pair:
                            maxima(n)
                            probabilities(n)
                for j in range(CB):
                    if j == 0:
                        dve.wait_ge(mean_done, 1)
                    dve.tensor_tensor(cv[:, j, :], cv[:, j, :], psf[:, 2 * HALF:4 * HALF], ALU.subtract).then_inc(cent, 1)
                for b in range(PAIRS):
                    dve.wait_ge(a_hi, b + 1)
                    if b == 0:
                        dve.wait_ge(pv_done, TT * PAIRS)
                    dve.tensor_tensor(al[:, b, :], attn[:, b, :], ah[:, b, :], ALU.subtract).then_inc(a_lo, 1)
                dve.wait_ge(std_done, 1)
                dve.reciprocal(rstdc[:], act_u[0][:]).then_inc(rstd_ok, 1)
                dve.wait_ge(rstd_ok, 1)
                dve.wait_ge(cent, CB)
                for j in range(CB):
                    dve.tensor_tensor(cv[:, j, :], cv[:, j, :], rstdc[:], ALU.mult).then_inc(nrm, 1)
                for j in range(CB):
                    dve.wait_ge(uo_hi, j + 1)
                    dve.tensor_tensor(uol[:, j, :], act_u[j % 2][:], uoh[:, j, :], ALU.subtract).then_inc(uo_lo, 1)
                dve.wait_ge(a_lo, PAIRS)
                for j in range(KC):
                    dst = mixa if j < 4 else mixb
                    for h in range(2):
                        i = 2 * j + h
                        c = slice(HALF * h, HALF * h + HALF)
                        dve.wait_ge(sig_ga, i + 1)
                        if h:
                            dve.wait_ge(blk_used, blk(FIRST_OUT + 3 * j + 2))
                        else:
                            dve.wait_ge(o_half, j + 1)
                        dve.tensor_tensor(dst[:, j % 4, c], sgc[:], ps[:, 4 + h, :], ALU.mult).then_inc(mix1, 1)
                        dve.tensor_tensor(sga[:], sga[:], ps[:, 6 + h, :], ALU.mult).then_inc(mix2, 1)
                        dve.wait_ge(mix1, i + 1)
                        dve.wait_ge(mix2, i + 1)
                        dve.tensor_tensor(dst[:, j % 4, c], dst[:, j % 4, c], sga[:], ALU.add).then_inc(mixed, 1)
                for j in range(KC):
                    src = mixa if j < 4 else mixb
                    dve.wait_ge(m_hi, j + 1)
                    dve.tensor_tensor(ml[:, j, :], src[:, j % 4, :], mh[:, j, :], ALU.subtract).then_inc(m_lo, 1)

                def finish_row(t):
                    for h in range(2):
                        dve.bn_stats(st6[:, h, :], x1[:, t, HALF * h:HALF * h + HALF]).then_inc(var_ok, 1)
                    dve.wait_ge(var_ok, 2 * t + 2)
                    dve.bn_aggr(mv[:, t, :], st6[:]).then_inc(st_ok, 1)
                    dve.wait_ge(st_ok, t + 1)
                    dve.scalar_tensor_tensor(out=x1[:, t, :], in0=x1[:, t, :], scalar=mv[:, t, 0:1], in1=g1_b[:],
                                             op0=ALU.subtract, op1=ALU.mult).then_inc(ln_g, 1)
                    dve.wait_ge(sd_ok, t + 1)
                    dve.reciprocal(rstd[:, t:t + 1], rstd[:, t:t + 1]).then_inc(rst_ok, 1)
                    dve.wait_ge(rst_ok, t + 1)
                    dve.wait_ge(ln_g, t + 1)
                    dve.scalar_tensor_tensor(out=x1[:, t, :], in0=x1[:, t, :], scalar=rstd[:, t:t + 1], in1=b1_b[:],
                                             op0=ALU.mult, op1=ALU.add).then_inc(x1_ok, 1)

                def residual(t):
                    dve.wait_ge(xres_in[t], 16)
                    dve.scalar_tensor_tensor(out=x1[:, t, :], in0=x1[:, t, :], scalar=ALPHA, in1=bo_b[:],
                                             op0=ALU.mult, op1=ALU.add).then_inc(xres_ok, 1)

                dve.wait_ge(lnp_in, 48)
                residual(0)
                for g in range(2):
                    for t in range(TT):
                        i = TT * g + t
                        c = slice(HALF * g, HALF * g + HALF)
                        if g == 0 and t + 1 < TT:
                            residual(t + 1)
                        dve.wait_ge(wo_done, i + 1)
                        if g == 0:
                            dve.wait_ge(xres_ok, t + 1)
                        dve.tensor_tensor(x1[:, t, c], x1[:, t, c], ps[:, i % 4, :], ALU.add).then_inc(wo_add, 1)
                        if g:
                            dve.wait_ge(wo_add, i + 1)
                            finish_row(t)
                moe_parts["vector"](dve)

    return nc


T_E, T_PAR, T_NEXT, T_SPLIT_DN, T_SPLIT_GU = range(5)
POOL_G = (1, 3, 5)
POOL_GU, POOL_DN = (2, 5, 7), (1, 3)


def moe(nc, sem, m):
    (x1, x1t, hot_a, hot_b, wr_t, ones, rt, big, gu_h, gu_l, gu_raw, dn_h, dn_l, dn_raw, xg, xgh, xgl, hb, hbh, hbl, ys,
     xf, y1, y2, diag, g2_b, b2_b, cst, eps, st6, mv, rstd, nmr, wgt, slot_i, ids_i, id_now, tab, cum_i, ends_i, rows_i, br_b,
     ps, psf, ident) = (m[k] for k in (
         "x1 x1t hot_a hot_b wr_t ones rt big gu_h gu_l gu_raw dn_h dn_l dn_raw xg xgh xgl hb hbh hbl ys "
         "xf y1 y2 diag g2_b b2_b cst eps st6 mv rstd nmr wgt slot_i ids_i id_now tab cum_i ends_i rows_i br_b "
         "ps psf ident").split())
    wexp, ln2_g, ln2_b, out, x1_dram, y_dram = (m[k] for k in "wexp ln2_g ln2_b out x1_dram y_dram".split())
    wr_in, wo_done, x1_ok, x1_out, xres_ok = (m[k] for k in "wr_in wo_done x1_ok x1_out xres_ok".split())
    gu_in = [sem(f"gu_in{j}") for j in range(4)]; dn_in = sem("dn_in")
    gu_hi = sem("gu_hi"); gu_lo_d = sem("gu_lo_d"); gu_lo_p = sem("gu_lo_p")
    dn_hi = sem("dn_hi"); dn_lo_d = sem("dn_lo_d"); dn_lo_p = sem("dn_lo_p")
    xt_r = sem("xt_r"); xt_rc = sem("xt_rc"); lg_done = sem("lg_done")
    rchain = sem("rchain"); r_exp = sem("r_exp"); r_exp_in = sem("r_exp_in")
    m_ready = sem("m_ready"); pos_done = sem("pos_done"); hot = sem("hot"); ids_done = sem("ids_done")
    tables = sem("tables"); ids_ok = sem("ids_ok")
    idc = sem("idc"); id_set = sem("id_set"); gath = sem("gath")
    tx_done = sem("tx_done"); tx_hi = sem("tx_hi"); tx_lo = sem("tx_lo"); gu_rows = sem("gu_rows")
    silu_ok = sem("silu_ok"); h_ok = sem("h_ok")
    th_done = sem("th_done"); th_hi = sem("th_hi"); th_lo = sem("th_lo"); dn_done = sem("dn_done")
    y_ok = sem("y_ok"); y_out = sem("y_out")
    ln2_in = sem("ln2_in"); xf_in = [sem(f"xf_in{i}") for i in range(TT)]; y_in = [sem(f"y_in{i}") for i in range(TT)]
    f_diag = sem("f_diag"); f_sum = sem("f_sum"); f_gp = sem("f_gp"); f_b = sem("f_b"); f_st = sem("f_st"); f_mv = sem("f_mv"); f_sd = sem("f_sd")
    f_rs = sem("f_rs"); f_nm = sem("f_nm"); f_ln = sem("f_ln"); f_g = sem("f_g"); f_ok = sem("f_ok"); f_out = sem("f_out")

    def const(c, n):
        return cst[:, c - C_TRI:c - C_TRI + n]
    tri, iota, tok, thr = const(C_TRI, P), const(C_IOTA, P), const(C_TOK, TT), const(C_THR, 7)
    upto = const(C_UPTO, NE * NE).rearrange("p (a b) -> p a b", b=NE)
    before = const(C_BEFORE, TT * TT).rearrange("p (a b) -> p a b", b=TT)
    earlier = const(C_EARLIER, 16).rearrange("p (a b) -> p a b", b=4)
    by_te = lambda a: a.rearrange("p (t e) -> p t e", e=NE)
    by_g = lambda a: a.rearrange("p (g e) -> p g e", e=EPG)
    prob, t1, both, rk, pick0, pick1, pos, tot = (rt[:, i, :] for i in range(8))
    picks = (pick0, pick1)
    s8 = rt[:, 8, :].rearrange("p (i n) -> p i n", n=16)
    s32 = rt[:, 9, :].rearrange("p (i n) -> p i n", n=32)

    def load(eng, row, i):
        return eng.value_load(tab[0:1, row, bass.ds(i, 1)], min_val=0, max_val=NE - 1 if row == T_E else 1)

    def ends(eng):
        total = eng.value_load(cum_i[0:1, NE - 1:NE], min_val=NE, max_val=MAX_TILES)
        end2 = eng.value_load(ends_i[0:1, 0:1], min_val=NE - 2, max_val=MAX_TILES - 2)
        end1 = eng.value_load(ends_i[0:1, 1:2], min_val=NE - 1, max_val=MAX_TILES - 1)
        return total, end2, end1

    def when(eng, row, i, static, then):
        if static is not None:
            if static:
                then()
            return
        flag = load(eng, row, i)
        with eng.If(flag > 0):
            then()
        eng.nop()

    def split_gu(i):
        return True if isinstance(i, int) and i == 0 else None

    def split_dn(i):
        return {0: False, 1: True}.get(i) if isinstance(i, int) else None

    def load_gu(sp, e, par, rows_before=None):
        for j in range(4):
            if e:
                sp.wait_ge(gu_in[j], 16 * e)
            if rows_before is not None:
                sp.wait_ge(gu_rows, rows_before + (j + 1))
            sp.dma_start(gu_raw[:, par, 2 * j:2 * j + 2, :], wexp[e][:, 2 * j:2 * j + 2, :]).then_inc(gu_in[j], 16)

    def load_dn(sp, e):
        sp.dma_start(dn_raw[:], wexp[e][:, KC:WROWS, :]).then_inc(dn_in, 16)

    def sync_part(sp):
        sp.wait_ge(wo_done, 2 * TT)
        load_gu(sp, 1, 1)
        sp.wait_ge(lg_done, TT)
        sp.wait_ge(x1_out, 16 * TT)
        load_dn(sp, 0)
        sp.wait_ge(ids_done, 2)
        sp.wait_ge(tables, 1)
        for e in range(1, NE):
            if e + 1 < NE:
                load_gu(sp, e + 1, (e + 1) % 2,
                        sp.value_load(rows_i[0:1, e - 1:e], min_val=0, max_val=4 * MAX_TILES - 4))
            sp.wait_ge(dn_lo_d, 2 * e)
            sp.wait_ge(dn_lo_p, 2 * e)
            load_dn(sp, e)
        total = sp.value_load(cum_i[0:1, NE - 1:NE], min_val=NE, max_val=MAX_TILES)
        sp.wait_ge(gu_rows, 4 * total)
        sp.dma_start(g2_b[:], ln2_g.partition_broadcast(P)).then_inc(ln2_in, 16)
        sp.dma_start(b2_b[:], ln2_b.partition_broadcast(P)).then_inc(ln2_in, 16)
        for t in range(TT):
            sp.dma_start(xf[:, t, :], x1_dram[P * t:P * t + P, :]).then_inc(xf_in[t], 16)
        for t in range(TT):
            sp.wait_ge(f_ok, t + 1)
            sp.dma_start(out[P * t:P * t + P, :], xf[:, t, :]).then_inc(f_out, 16)
        sp.wait_ge(f_out, 16 * TT)

    def dn_low(eng, e, rows, done):
        for k in rows:
            eng.wait_ge(dn_hi, e * 4 + (k + 1))
            eng.tensor_tensor(dn_l[:, k, :], dn_raw[:, k, :], dn_h[:, k, :], ALU.subtract).then_inc(done, 1)

    def gu_low(eng, e, par, rows, done):
        for k in rows:
            eng.wait_ge(gu_hi, e * 8 + (k + 1))
            eng.tensor_tensor(gu_l[:, par, k, :], gu_raw[:, par, k, :], gu_h[:, par, k, :], ALU.subtract).then_inc(done, 1)

    def pool_part(pool):
        for k in range(KC):
            gu_low(pool, 0, 0, (k,), gu_lo_p if k in POOL_GU else gu_lo_d)
        pool.wait_ge(ids_ok, 1)
        pool.wait_ge(x1_out, 16 * TT)
        pool.wait_ge(xt_r, TT)

        def gather(i):
            pool.tensor_copy(id_now[:], ids_i[:, i:i + 1] if isinstance(i, int) else ids_i[:, bass.ds(i, 1)]).then_inc(idc, 1)
            pool.wait_ge(idc, i + 1)
            pool.sem_inc(id_set, 1)
            pool.indirect_dma_start(out=xg[:], out_offset=None, in_=x1_dram,
                                    in_offset=bass.IndirectOffsetOnAxis(ap=id_now[:, 0:1], axis=0)).then_inc(gath, 16)

        def store(i):
            pool.wait_ge(y_ok, i + 1)
            pool.dma_start(y_dram[bass.ds(i * P, P), :], ys[:]).then_inc(y_out, 16)

        def down_rows(i, first=False):
            e = 0 if first else load(pool, T_E, i - 1)
            dn_low(pool, e, POOL_DN, dn_lo_p)

        def gate_rows(i, rows, first=False):
            e, par = (0, 1) if first else (load(pool, T_E, i), load(pool, T_NEXT, i))
            gu_low(pool, e + 1, par if first else bass.ds(par, 1), rows, gu_lo_p)

        def step(i, has_store=True):
            pool.wait_ge(tx_done, i + 1)
            gather(i + 1)
            first = isinstance(i, int) and i == 0
            when(pool, T_SPLIT_DN, i, split_dn(i), lambda: down_rows(i, isinstance(i, int) and i == 1))
            if has_store:
                store(i - 2)
            when(pool, T_SPLIT_GU, i, split_gu(i), lambda: gate_rows(i, POOL_GU, first))

        gather(0)
        total, end2, end1 = ends(pool)
        step(0, False)
        step(1, False)
        step(2)
        with pool.Fori(3, MAX_TILES) as i:
            with pool.If(i < total):
                step(i)
            pool.nop()
        when(pool, T_SPLIT_DN, total, None, lambda: down_rows(total))
        store(end2)
        store(end1)
        pool.wait_ge(y_out, end1 * 16 + 16)
        pool.sem_inc(id_set, 1)
        pool.wait_ge(gath, total * 16 + 16)
        pool.sem_inc(id_set, 1)
        for t in range(TT):
            for c, y in enumerate((y1, y2)):
                pool.indirect_dma_start(out=y[:, t, :], out_offset=None, in_=y_dram,
                                        in_offset=bass.IndirectOffsetOnAxis(ap=slot_i[:, c, t:t + 1], axis=0)
                                        ).then_inc(y_in[t], 16)
        pool.wait_ge(ln2_in, 32)
        for t in range(TT - 1):
            if t in POOL_G:
                pool.wait_ge(f_ln, t + 1)
                pool.tensor_tensor(xf[:, t, :], xf[:, t, :], g2_b[:], ALU.mult).then_inc(f_gp, 1)
                pool.wait_ge(f_gp, POOL_G.index(t) + 1)
            else:
                pool.wait_ge(f_g, t + 1 - sum(r < t for r in POOL_G))
            pool.tensor_tensor(xf[:, t, :], xf[:, t, :], b2_b[:], ALU.add).then_inc(f_ok, 1)

    def transpose_x1(pe, t):
        pe.wait_ge(x1_ok, t + 1)
        if t:
            pe.wait_ge(xt_rc, t)
        for k in range(KC):
            last = pe.transpose(psf[:, 4 * HALF + P * k:4 * HALF + P * k + P], x1[:, t, P * k:P * k + P], ident)
        last.then_inc(xt_r, 1)

    def logits(pe, t):
        pe.wait_ge(xt_rc, t + 1)
        if t == 0:
            pe.wait_ge(wr_in, 48)
        for k in range(KC):
            last = pe.matmul(ps[:, 6, NE * t:NE * t + NE], x1t[:, k, :], wr_t[:, k, :], start=k == 0, stop=k == KC - 1)
        last.then_inc(lg_done, 1)

    def mm3(pe, o, a_h, a_l, b_h, b_l, first, last):
        pe.matmul(o, a_h, b_h, start=first, stop=False)
        pe.matmul(o, a_h, b_l, start=False, stop=False)
        return pe.matmul(o, a_l, b_h, start=False, stop=last)

    def tensor_part(pe):
        pe.wait_ge(m_ready, 1)
        pe.matmul(ps[:, 3, 0:P], tri, both, start=True, stop=True)
        pe.matmul(ps[:, 4, 0:P], ones[:], both, start=True, stop=True).then_inc(pos_done, 1)
        for c in range(2):
            pe.wait_ge(hot, c + 1)
            for t in range(TT):
                last = pe.matmul(ps[:, 5, 0:TAB], hot_a[:, c, t, :], hot_b[:, c, t, :], start=c == 0 and t == 0,
                                 stop=c == 1 and t == TT - 1)
            last.then_inc(ids_done, 1)
        pe.wait_ge(tables, 1)
        total, end2, end1 = ends(pe)

        def transpose_x(i):
            pe.wait_ge(gath, i * 16 + 16)
            if not (isinstance(i, int) and i == 0):
                pe.wait_ge(tx_lo, i)
            for k in range(KC):
                last = pe.transpose(psf[:, P * k:P * k + P], xg[:, P * k:P * k + P], ident)
            last.then_inc(tx_done, 1)

        def up(i):
            e, par = load(pe, T_E, i), load(pe, T_PAR, i)
            pe.wait_ge(tx_lo, i + 1)
            for k in range(KC):
                if k in POOL_GU:
                    pe.wait_ge(gu_lo_p, e * len(POOL_GU) + (POOL_GU.index(k) + 1))
                else:
                    pe.wait_ge(gu_lo_d, e * (KC - len(POOL_GU)) + (k - sum(r < k for r in POOL_GU) + 1))
                for h in range(2):
                    c = slice(HALF * h, HALF * h + HALF)
                    last = mm3(pe, ps[:, 2 + h, :], xgh[:, P * k:P * k + P], xgl[:, P * k:P * k + P],
                               gu_h[:, bass.ds(par, 1), k, c], gu_l[:, bass.ds(par, 1), k, c], k == 0, k == KC - 1)
                if k % 2:
                    last.then_inc(gu_rows, 1)

        def transpose_h(i):
            pe.wait_ge(h_ok, i + 1)
            if not (isinstance(i, int) and i == 0):
                pe.wait_ge(th_lo, i)
            for k in range(FC):
                last = pe.transpose(ps[:, 4, P * k:P * k + P], hb[:, P * k:P * k + P], ident)
            last.then_inc(th_done, 1)

        def down(i):
            e = load(pe, T_E, i)
            pe.wait_ge(th_lo, i + 1)
            pe.wait_ge(dn_lo_d, e * 2 + 2)
            pe.wait_ge(dn_lo_p, e * 2 + 2)
            if not (isinstance(i, int) and i == 0):
                pe.wait_ge(y_ok, i)
            for k in range(FC):
                for h in range(2):
                    c = slice(HALF * h, HALF * h + HALF)
                    last = mm3(pe, ps[:, 6 + h, :], hbh[:, P * k:P * k + P], hbl[:, P * k:P * k + P],
                               dn_h[:, k, c], dn_l[:, k, c], k == 0, k == FC - 1)
            last.then_inc(dn_done, 1)

        transpose_x(0)
        up(0)
        transpose_x(1)
        transpose_h(0)
        up(1)
        transpose_x(2)
        down(0)
        transpose_h(1)
        up(2)
        with pe.Fori(3, MAX_TILES) as i:
            with pe.If(i < total):
                transpose_x(i)
                down(i - 2)
                transpose_h(i - 1)
                up(i)
            pe.nop()
        down(end2)
        transpose_h(end1)
        down(end1)
        pe.wait_ge(y_ok, end1 + 1)
        for t in range(TT):
            pe.wait_ge(f_diag, 2 * t + 2)
            pe.wait_ge(y_in[t], 32)
            if t >= 4:
                pe.wait_ge(f_b, t - 3)
            for h in range(2):
                for c, y in enumerate((y1, y2)):
                    last = pe.matmul(ps[:, 2 * (t % 4) + h, :], diag[:, c, t, :], y[:, t, HALF * h:HALF * h + HALF],
                                     start=c == 0, stop=c == 1)
            last.then_inc(f_sum, 1)

    def copy_x1t(act, t):
        act.wait_ge(xt_r, t + 1)
        if t:
            act.wait_ge(lg_done, t)
        act.activation(x1t[:, :, :].rearrange("p k c -> p (k c)"), psf[:, 4 * HALF:6 * HALF], ACT.Copy).then_inc(xt_rc, 1)

    def scalar_part(act):
        act.wait_ge(r_exp_in, 1)
        act.activation(prob, prob, ACT.Exp).then_inc(r_exp, 1)

        def gu_high(e, par, rows):
            for k in rows:
                act.wait_ge(gu_in[k // 2], e * 16 + 16)
                act.activation(gu_h[:, par, k, :], gu_raw[:, par, k, :], ACT.Copy).then_inc(gu_hi, 1)

        act.wait_ge(wo_done, 2 * TT)
        gu_high(0, 0, range(KC))
        gu_high(1, 1, range(KC))
        act.wait_ge(tables, 1)
        total, end2, end1 = ends(act)

        def x_t(i):
            act.wait_ge(tx_done, i + 1)
            if not (isinstance(i, int) and i == 0):
                act.wait_ge(gu_rows, 4 * i)
            act.activation(xgh[:], psf[:, 0:SEQ], ACT.Copy).then_inc(tx_hi, 1)

        def down_rows(i, first=False, before=None):
            e = 0 if first else load(act, T_E, i - 1)
            act.wait_ge(dn_in, e * 16 + 16)
            if not first:
                act.wait_ge(dn_done, i - 1 if before is None else before)
            for k in range(FC):
                act.activation(dn_h[:, k, :], dn_raw[:, k, :], ACT.Copy).then_inc(dn_hi, 1)

        def h_t(i):
            act.wait_ge(th_done, i + 1)
            if not (isinstance(i, int) and i == 0):
                act.wait_ge(dn_done, i)
            act.activation(hbh[:], ps[:, 4, :], ACT.Copy).then_inc(th_hi, 1)

        def gate_rows(i, rows):
            e, par = load(act, T_E, i), load(act, T_NEXT, i)
            gu_high(e + 1, bass.ds(par, 1), rows)

        def silu(i):
            act.wait_ge(gu_rows, 4 * i + 4)
            if not (isinstance(i, int) and i == 0):
                act.wait_ge(th_done, i)
            act.activation(hb[:], ps[:, 2, :], ACT.Silu).then_inc(silu_ok, 1)

        def step(i):
            first = isinstance(i, int) and i == 0
            x_t(i)
            when(act, T_SPLIT_DN, i, split_dn(i), lambda: down_rows(i, isinstance(i, int) and i == 1))
            if not first:
                h_t(i - 1)
            if not first:
                when(act, T_SPLIT_GU, i, split_gu(i), lambda: gate_rows(i, range(KC)))
            silu(i)

        for i in range(3):
            step(i)
        with act.Fori(3, MAX_TILES) as i:
            with act.If(i < total):
                step(i)
            act.nop()
        when(act, T_SPLIT_DN, total, None, lambda: down_rows(total, before=end1))
        h_t(end1)
        act.wait_ge(gu_rows, 4 * total)
        for t in range(TT):
            for c in range(2):
                act.activation(diag[:, c, t, :], ident, ACT.Copy, scale=wgt[:, c, t:t + 1]).then_inc(f_diag, 1)
        for t in range(TT):
            act.wait_ge(f_mv, t + 1)
            act.activation(rstd[:, t:t + 1], mv[:, t, 1:2], ACT.Sqrt, bias=eps[:]).then_inc(f_sd, 1)
            act.wait_ge(f_nm, t + 1)
            act.activation(xf[:, t, :], xf[:, t, :], ACT.Identity, scale=rstd[:, t:t + 1],
                           bias=nmr[:, t:t + 1]).then_inc(f_ln, 1)

    def vector_part(dve):
        count = [0]
        V = nc.vector

        def link(ins):
            count[0] += 1
            ins.then_inc(rchain, 1)
            dve.wait_ge(rchain, count[0])

        def over(a, n, m):
            return a.unsqueeze(2).broadcast_to([P, n, m])

        def rank(dst, src, n, a4, b4):
            v = by_g(src)
            me, other = v.unsqueeze(3).broadcast_to([P, n, EPG, EPG]), v.unsqueeze(2).broadcast_to([P, n, EPG, EPG])
            a = a4.rearrange("p (g a b) -> p g a b", a=EPG, b=EPG)
            b = b4.rearrange("p (g a b) -> p g a b", a=EPG, b=EPG)
            link(V.tensor_tensor(a, other, me, ALU.is_gt))
            link(V.tensor_tensor(b, other, me, ALU.is_equal))
            link(V.tensor_tensor(b, b, earlier.unsqueeze(1).broadcast_to([P, n, EPG, EPG]), ALU.mult))
            link(V.tensor_tensor(a, a, b, ALU.add))
            link(V.reduce_sum(by_g(dst), a, AX.X))

        dve.wait_ge(xres_ok, TT)
        link(V.memset(ones[:], 1.0))
        dve.wait_ge(lg_done, TT)
        p = prob
        link(V.tensor_tensor(by_te(p), by_te(ps[:, 6, 0:P]), br_b[:, :].unsqueeze(1).broadcast_to([P, TT, NE]), ALU.add))
        top = s8[:, 0, 0:TT]
        link(V.reduce_max(top, by_te(p), AX.X))
        V.tensor_tensor(by_te(p), by_te(p), over(top, TT, NE), ALU.subtract).then_inc(r_exp_in, 1)
        dve.wait_ge(r_exp, 1)
        link(V.reduce_sum(top, by_te(p), AX.X))
        link(V.reciprocal(top, top))
        link(V.tensor_tensor(by_te(p), by_te(p), over(top, TT, NE), ALU.mult))
        rank(rk, p, 32, big[:, 0:512], big[:, 512:1024])
        link(V.scalar_tensor_tensor(out=t1, in0=rk, scalar=1.5, in1=p, op0=ALU.is_lt, op1=ALU.mult))
        gs, gr = s32[:, 0, :], s32[:, 1, :]
        link(V.reduce_sum(gs, by_g(t1), AX.X))
        rank(gr, gs, 8, big[:, 0:128], big[:, 128:256])
        link(V.tensor_scalar(gr, gr, 0.5, None, ALU.is_lt))
        for c, pick in enumerate(picks):
            link(V.scalar_tensor_tensor(out=by_g(pick), in0=by_g(rk), scalar=float(c), in1=over(gr, 32, EPG),
                                        op0=ALU.is_equal, op1=ALU.mult))
        V.tensor_tensor(both, pick0, pick1, ALU.add).then_inc(m_ready, 1)
        dve.wait_ge(pos_done, 1)
        link(V.tensor_copy(tot, ps[:, 4, 0:P]))
        tot_et = tot.rearrange("p (t e) -> p e t", e=NE)
        n_e, nt, cum, base = (s8[:, i, :] for i in range(1, 5))
        link(V.reduce_sum(n_e, tot_et, AX.X))
        cmp7 = big[:, 0:NE * 7].rearrange("p (e k) -> p e k", k=7)
        link(V.tensor_tensor(cmp7, over(n_e, NE, 7), thr.unsqueeze(1).broadcast_to([P, NE, 7]), ALU.is_gt))
        link(V.reduce_sum(nt, cmp7, AX.X))
        link(V.tensor_scalar(nt, nt, 1.0, None, ALU.add))
        ee = big[:, 0:NE * NE].rearrange("p (a b) -> p a b", b=NE)
        link(V.tensor_tensor(ee, upto, nt.unsqueeze(1).broadcast_to([P, NE, NE]), ALU.mult))
        link(V.reduce_sum(cum, ee, AX.X))
        link(V.tensor_tensor(base, cum, nt, ALU.subtract))
        before_e = before.unsqueeze(2).broadcast_to([P, TT, NE, TT])
        tet = big[:, :].rearrange("p (t e u) -> p t e u", e=NE, u=TT)
        link(V.tensor_tensor(tet, tot_et.unsqueeze(1).broadcast_to([P, TT, NE, TT]), before_e, ALU.mult))
        link(V.reduce_sum(by_te(pos), tet, AX.X))
        link(V.tensor_tensor(pos, pos, ps[:, 3, 0:P], ALU.add))
        for c, pick in enumerate(picks):
            hi, lo, q = s8[:, 5, 0:TT], s8[:, 6, 0:TT], s8[:, 7, 0:TT]
            link(V.tensor_tensor(t1, pick, pos, ALU.mult))
            link(V.reduce_sum(lo, by_te(t1), AX.X))
            link(V.tensor_tensor(by_te(t1), by_te(pick), base.unsqueeze(1).broadcast_to([P, TT, NE]), ALU.mult))
            link(V.reduce_sum(hi, by_te(t1), AX.X))
            c8 = big[:, 0:TT * 7].rearrange("p (t k) -> p t k", k=7)
            link(V.tensor_tensor(c8, over(lo, TT, 7), thr.unsqueeze(1).broadcast_to([P, TT, 7]), ALU.is_ge))
            link(V.reduce_sum(q, c8, AX.X))
            link(V.tensor_tensor(hi, hi, q, ALU.add))
            link(V.scalar_tensor_tensor(out=lo, in0=q, scalar=-float(P), in1=lo, op0=ALU.mult, op1=ALU.add))
            link(V.scalar_tensor_tensor(out=slot_i[:, c, :], in0=hi, scalar=float(P), in1=lo, op0=ALU.mult, op1=ALU.add))
            link(V.tensor_tensor(hot_b[:, c], iota[:, 0:TAB].unsqueeze(1).broadcast_to([P, TT, TAB]), over(hi, TT, TAB),
                                 ALU.is_equal))
            link(V.tensor_tensor(hot_b[:, c], hot_b[:, c], over(tok, TT, TAB), ALU.mult))
            V.tensor_tensor(hot_a[:, c], iota.unsqueeze(1).broadcast_to([P, TT, P]), over(lo, TT, P),
                            ALU.is_equal).then_inc(hot, 1)
            dve.wait_ge(hot, c + 1)
        et, fst, fl = s32[:, 0, :], s32[:, 1, :], s32[:, 2, :]
        ie = big[:, 0:TAB * NE].rearrange("p (i e) -> p i e", e=NE)
        link(V.tensor_tensor(ie, over(iota[:, 0:TAB], TAB, NE), cum.unsqueeze(1).broadcast_to([P, TAB, NE]), ALU.is_ge))
        link(V.reduce_sum(et, ie, AX.X))
        link(V.tensor_scalar(et, et, float(NE - 1), None, ALU.min))
        link(V.tensor_copy(tab[:, T_E, :], et))
        link(V.tensor_scalar(tab[:, T_PAR, :], tab[:, T_E, :], 1, None, ALU.bitwise_and))
        link(V.tensor_scalar(tab[:, T_NEXT, :], tab[:, T_PAR, :], -1.0, 1.0, ALU.mult, ALU.add))
        link(V.memset(fst[:, 0:1], 1.0))
        link(V.tensor_tensor(fst[:, 1:TAB], et[:, 1:TAB], et[:, 0:TAB - 1], ALU.is_gt))
        link(V.memset(tab[:, T_SPLIT_DN, 0:1], 0))
        link(V.tensor_copy(tab[:, T_SPLIT_DN, 1:TAB], fst[:, 0:TAB - 1]))
        link(V.scalar_tensor_tensor(out=tab[:, T_SPLIT_GU, :], in0=et, scalar=NE - 1.5, in1=fst, op0=ALU.is_lt, op1=ALU.mult))
        link(V.tensor_scalar(rows_i[:], cum, -1.0, 4.0, ALU.add, ALU.mult))
        link(V.tensor_scalar(ends_i[:, 0:1], cum[:, NE - 1:NE], -2.0, None, ALU.add))
        link(V.tensor_scalar(ends_i[:, 1:2], cum[:, NE - 1:NE], -1.0, None, ALU.add))
        V.tensor_copy(cum_i[:], cum).then_inc(tables, 1)
        dve.wait_ge(ids_done, 2)
        V.tensor_copy(ids_i[:], ps[:, 5, 0:TAB]).then_inc(ids_ok, 1)
        for c, pick in enumerate(picks):
            link(V.tensor_tensor(t1, p, pick, ALU.mult))
            link(V.reduce_sum(wgt[:, c, :], by_te(t1), AX.X))
        link(V.tensor_tensor(top, wgt[:, 0, :], wgt[:, 1, :], ALU.add))
        link(V.reciprocal(top, top))
        link(V.tensor_tensor(wgt[:, :, :], wgt[:, :, :], top.unsqueeze(1).broadcast_to([P, 2, TT]), ALU.mult))
        mine_gu = [k for k in range(KC) if k not in POOL_GU]
        mine_dn = [k for k in range(FC) if k not in POOL_DN]
        dve.wait_ge(tables, 1)
        total, end2, end1 = ends(dve)

        def x_t(i):
            dve.wait_ge(tx_hi, i + 1)
            dve.tensor_tensor(xgl[:], psf[:, 0:SEQ], xgh[:], ALU.subtract).then_inc(tx_lo, 1)

        def down_rows(i, first=False):
            e = 0 if first else load(dve, T_E, i - 1)
            dn_low(dve, e, mine_dn, dn_lo_d)

        def h_t(i):
            dve.wait_ge(th_hi, i + 1)
            dve.tensor_tensor(hbl[:], ps[:, 4, :], hbh[:], ALU.subtract).then_inc(th_lo, 1)

        def gate_rows(i, rows, first=False):
            e, par = (0, 1) if first else (load(dve, T_E, i), load(dve, T_NEXT, i))
            gu_low(dve, e + 1, par if first else bass.ds(par, 1), rows, gu_lo_d)

        def gate(i):
            dve.wait_ge(silu_ok, i + 1)
            dve.tensor_tensor(hb[:], hb[:], ps[:, 3, :], ALU.mult).then_inc(h_ok, 1)

        def y(i):
            dve.wait_ge(dn_done, i + 1)
            if not (isinstance(i, int) and i == 0):
                dve.wait_ge(y_out, i * 16)
            dve.tensor_copy(ys[:], psf[:, 6 * HALF:8 * HALF]).then_inc(y_ok, 1)

        def step(i):
            static = isinstance(i, int)
            x_t(i)
            when(dve, T_SPLIT_DN, i, split_dn(i), lambda: down_rows(i, static and i == 1))
            if not (static and i < 2):
                y(i - 2)
            if not (static and i == 0):
                h_t(i - 1)
            when(dve, T_SPLIT_GU, i, split_gu(i), lambda: gate_rows(i, mine_gu, static and i == 0))
            gate(i)

        for i in range(3):
            step(i)
        with dve.Fori(3, MAX_TILES) as i:
            with dve.If(i < total):
                step(i)
            dve.nop()
        when(dve, T_SPLIT_DN, total, None, lambda: down_rows(total))
        y(end2)
        h_t(end1)
        y(end1)

        def combine(t):
            dve.wait_ge(xf_in[t], 16)
            dve.wait_ge(f_sum, t + 1)
            bank = 2 * (t % 4)
            dve.scalar_tensor_tensor(out=xf[:, t, :], in0=xf[:, t, :], scalar=ALPHA,
                                     in1=psf[:, HALF * bank:HALF * bank + D], op0=ALU.mult, op1=ALU.add).then_inc(f_b, 1)
            dve.wait_ge(f_b, t + 1)
            for h in range(2):
                dve.bn_stats(st6[:, h, :], xf[:, t, HALF * h:HALF * h + HALF]).then_inc(f_st, 1)
            dve.wait_ge(f_st, 2 * t + 2)
            dve.bn_aggr(mv[:, t, :], st6[:]).then_inc(f_mv, 1)

        def normalise(t):
            dve.wait_ge(f_sd, t + 1)
            dve.reciprocal(rstd[:, t:t + 1], rstd[:, t:t + 1]).then_inc(f_rs, 1)
            dve.wait_ge(f_rs, t + 1)
            dve.scalar_tensor_tensor(out=nmr[:, t:t + 1], in0=mv[:, t, 0:1], scalar=-1.0, in1=rstd[:, t:t + 1],
                                     op0=ALU.mult, op1=ALU.mult).then_inc(f_nm, 1)

        def scale_row(t):
            dve.wait_ge(f_ln, t + 1)
            dve.tensor_tensor(xf[:, t, :], xf[:, t, :], g2_b[:], ALU.mult).then_inc(f_g, 1)

        dve.wait_ge(ln2_in, 32)
        for t in range(TT + 2):
            if t < TT:
                combine(t)
            if 1 <= t <= TT:
                normalise(t - 1)
            if t >= 2 and t - 2 not in POOL_G:
                scale_row(t - 2)
        dve.wait_ge(f_g, TT - len(POOL_G))
        dve.wait_ge(f_ok, TT - 1)
        dve.tensor_tensor(xf[:, TT - 1, :], xf[:, TT - 1, :], b2_b[:], ALU.add).then_inc(f_ok, 1)

    return {"load_expert_0": lambda sp: load_gu(sp, 0, 0), "sync": sync_part, "gpsimd": pool_part, "tensor": tensor_part,
            "transpose_x1": transpose_x1, "logits": logits, "scalar": scalar_part, "copy_x1t": copy_x1t,
            "vector": vector_part}


def laid_out(x, w_in, b_in, w_dw, b_dw, ln_conv_g, ln_conv_b, w_conv_out, rel_bias, w_attn_out, w_o, b_o,
             ln1_g, ln1_b, w_router, b_router, w_gate_up, w_down, ln2_g, ln2_b):
    con = np.ascontiguousarray
    x = np.asarray(x)[0]
    w_all = np.concatenate([np.asarray(w_in)[0], np.concatenate([np.asarray(w_conv_out)[0], np.asarray(w_attn_out)[0]], 0),
                            np.asarray(w_o)[0]], 1)
    blocks = w_all.reshape(KC, P, -1, P).transpose(2, 1, 0, 3)[block_columns()]
    rel = np.clip(np.arange(P)[:, None] - np.arange(BANDW)[None, :] + 512, -256, 256) + 256
    band = np.asarray(rel_bias)[0][:, rel]
    wexp = np.concatenate([np.asarray(w_gate_up)[0].reshape(NE, KC, P, 2 * FF), np.asarray(w_down)[0].reshape(NE, FC, P, D)], 1)
    col = lambda a, n: con(np.asarray(a)[0].reshape(n, P).T)
    return {
        "xT": con(x.T.reshape(KC, P, SEQ)), "x": con(x), "wblk": con(blocks), "b_in": col(b_in, 36),
        "dw": con(np.asarray(w_dw)[0].T.reshape(CB, P, CW).transpose(1, 0, 2)),
        "dwb": col(b_dw, CB), "lncg": col(ln_conv_g, CB), "lncb": col(ln_conv_b, CB),
        "relb": con(band.reshape(PAIRS, 2, P, BANDW).transpose(0, 2, 1, 3)),
        "b_o": con(np.asarray(b_o)[0]), "ln1_g": con(np.asarray(ln1_g)[0]), "ln1_b": con(np.asarray(ln1_b)[0]),
        "w_r": con(np.asarray(w_router).reshape(KC, P, NE).transpose(1, 0, 2)), "b_r": con(np.asarray(b_router)),
        "wexp": con(wexp.transpose(0, 2, 1, 3)),
        "ln2_g": con(np.asarray(ln2_g)[0]), "ln2_b": con(np.asarray(ln2_b)[0]), "consts": constants(),
    }


def kernel(**inputs):
    import concourse.bacc as bacc
    from concourse.bass_utils import run_bass_kernel_spmd

    nc = bacc.Bacc("TRN2", target_bir_lowering=False, num_devices=1)
    arrays = {f"in_{k}": v for k, v in laid_out(**inputs).items()}
    args = [nc.dram_tensor(n, a.shape, F32, kind="ExternalInput").ap() for n, a in arrays.items()]
    out = nc.dram_tensor("out_rows", (SEQ, D), F32, kind="ExternalOutput").ap()
    encoder_layer(nc, *args, out)
    r = run_bass_kernel_spmd(nc, [arrays], core_ids=[0])
    return r.results[0]["out_rows"].reshape(1, SEQ, D)
```
